# Optimizing a Trainium2 kernel written in Bass

```python
import math
import jax
import jax.numpy as jnp
from jax import lax
import numpy as np

D_MODEL = 1024
BATCH = 1
SEQ = 1024
DEPTH = 1

CONV_WIDTH = 4
RMS_EPS = 1e-6
LRU_WIDTH = D_MODEL
LRU_HEADS = 16
LRU_HEAD_DIM = LRU_WIDTH // LRU_HEADS
LRU_C = 8.0
SSD_INNER = 2 * D_MODEL
SSD_HEAD_DIM = 64
SSD_HEADS = SSD_INNER // SSD_HEAD_DIM
SSD_GROUPS = 4
SSD_HEADS_PER_GROUP = SSD_HEADS // SSD_GROUPS
SSD_STATE = 128
SSD_CHUNK = 128
SSD_CONV_DIM = SSD_INNER + 2 * SSD_GROUPS * SSD_STATE
PEER_HEADS = 8
PEER_KEYS = 128
PEER_EXPERTS = PEER_KEYS * PEER_KEYS
PEER_TOPK = 16
PEER_QUERY_DIM = 256
PEER_HALF = PEER_QUERY_DIM // 2
PEER_TOKEN_BLOCK = 128
IN_DIM = LRU_WIDTH + SSD_INNER + SSD_CONV_DIM + SSD_HEADS + 2 * D_MODEL

kernel_name = 'hybrid_rglru_ssd_peer_block'

def rms_norm(x, w):
    xf = x.astype(jnp.float32)
    y = xf * lax.rsqrt(jnp.mean(xf * xf, axis=-1, keepdims=True) + RMS_EPS)
    return (y * w.astype(jnp.float32)).astype(x.dtype)

def causal_depthwise_conv(x, w, b):
    y = lax.conv_general_dilated(
        x, w[:, None, :], window_strides=(1,), padding=[(CONV_WIDTH - 1, 0)],
        dimension_numbers=('NWC', 'WIO', 'NWC'), feature_group_count=x.shape[-1])
    return y + b

def rg_lru(x, w_a, b_a, w_x, b_x, lam):
    bsz, seqlen, _ = x.shape
    xh = x.reshape(bsz, seqlen, LRU_HEADS, LRU_HEAD_DIM)
    r = jax.nn.sigmoid(jnp.einsum('blhi,hij->blhj', xh, w_a).reshape(bsz, seqlen, LRU_WIDTH) + b_a)
    i = jax.nn.sigmoid(jnp.einsum('blhi,hij->blhj', xh, w_x).reshape(bsz, seqlen, LRU_WIDTH) + b_x)
    log_a = -LRU_C * r.astype(jnp.float32) * jax.nn.softplus(-lam.astype(jnp.float32))
    a = jnp.exp(log_a)
    u = jnp.sqrt(-jnp.expm1(2.0 * log_a)) * (i * x).astype(jnp.float32)

    def step(h, au):
        a_t, u_t = au
        h = a_t * h + u_t
        return h, h

    h0 = jnp.zeros((bsz, LRU_WIDTH), jnp.float32)
    _, hs = lax.scan(step, h0, (jnp.swapaxes(a, 0, 1), jnp.swapaxes(u, 0, 1)))
    return jnp.swapaxes(hs, 0, 1).astype(x.dtype)

def ssd_mixer(xbc, z, dt_raw, conv_w, conv_b, dt_bias, a_log, d_skip, norm_w):
    dtype = xbc.dtype
    f32 = jnp.float32
    bsz, seqlen, _ = xbc.shape
    G, HG, P, N, Q = SSD_GROUPS, SSD_HEADS_PER_GROUP, SSD_HEAD_DIM, SSD_STATE, SSD_CHUNK
    nc = seqlen // Q
    xbc = jax.nn.silu(causal_depthwise_conv(xbc, conv_w, conv_b)).astype(f32)
    xs, bm, cm = jnp.split(xbc, [SSD_INNER, SSD_INNER + G * N], axis=-1)
    xs = xs.reshape(bsz, nc, Q, G, HG, P)
    bm = bm.reshape(bsz, nc, Q, G, N)
    cm = cm.reshape(bsz, nc, Q, G, N)
    dt = jax.nn.softplus(dt_raw.astype(f32) + dt_bias.astype(f32))
    a = -jnp.exp(a_log.astype(f32))
    da = (dt * a).reshape(bsz, nc, Q, G, HG).transpose(0, 3, 4, 1, 2)
    xdt = xs * dt.reshape(bsz, nc, Q, G, HG)[..., None]
    a_cs = jnp.cumsum(da, axis=-1)
    causal = jnp.tril(jnp.ones((Q, Q), dtype=bool))
    decay_ls = jnp.exp(jnp.where(causal, a_cs[..., :, None] - a_cs[..., None, :], -jnp.inf))
    cb = jnp.einsum('bclgn,bcsgn->bgcls', cm, bm)
    y_diag = jnp.einsum('bghcls,bcsghp->bclghp', cb[:, :, None] * decay_ls, xdt)
    decay_states = jnp.exp(a_cs[..., -1:] - a_cs).transpose(0, 3, 4, 1, 2)
    states = jnp.einsum('bclgn,bclghp->bcghpn', bm, xdt * decay_states[..., None])
    chunk_decay = jnp.exp(a_cs[..., -1])

    def step(s, inp):
        dec, st = inp
        return dec[..., None, None] * s + st, s

    s0 = jnp.zeros((bsz, G, HG, P, N), f32)
    _, prev = lax.scan(step, s0, (jnp.moveaxis(chunk_decay, -1, 0), jnp.moveaxis(states, 1, 0)))
    prev = jnp.moveaxis(prev, 0, 1)
    decay_out = jnp.exp(a_cs).transpose(0, 3, 4, 1, 2)
    y_off = jnp.einsum('bclgn,bcghpn->bclghp', cm, prev) * decay_out[..., None]
    y = y_diag + y_off + xs * d_skip.astype(f32).reshape(G, HG)[:, :, None]
    y = y.reshape(bsz, seqlen, SSD_INNER)
    yg = (y * jax.nn.silu(z.astype(f32))).reshape(bsz, seqlen, G, SSD_INNER // G)
    y = rms_norm(yg, norm_w.reshape(G, SSD_INNER // G)).reshape(bsz, seqlen, SSD_INNER)
    return y.astype(dtype)

def peer_ffn(h, w_q, sub_keys, expert_down, expert_up):
    tokens = h.reshape(-1, D_MODEL)
    nblk = tokens.shape[0] // PEER_TOKEN_BLOCK
    K = PEER_TOPK

    def block(xb):
        t = xb.shape[0]
        q = (xb @ w_q).reshape(t, PEER_HEADS, 2, PEER_HALF)
        s = jnp.einsum('thpd,hpkd->thpk', q, sub_keys).astype(jnp.float32)
        sv, si = lax.top_k(s, K)
        cand = sv[:, :, 0, :, None] + sv[:, :, 1, None, :]
        cv, ci = lax.top_k(cand.reshape(t, PEER_HEADS, K * K), K)
        i1 = jnp.take_along_axis(si[:, :, 0, :], ci // K, axis=-1)
        i2 = jnp.take_along_axis(si[:, :, 1, :], ci % K, axis=-1)
        idx = i1 * PEER_KEYS + i2
        g = jax.nn.softmax(cv, axis=-1)
        u = expert_down[idx]
        act = jax.nn.gelu(jnp.einsum('thkd,td->thk', u, xb).astype(jnp.float32), approximate=False)
        v = expert_up[idx]
        return jnp.einsum('thk,thkd->td', (g * act).astype(xb.dtype), v)

    out = lax.map(block, tokens.reshape(nblk, PEER_TOKEN_BLOCK, D_MODEL))
    return out.reshape(h.shape)

def setup_inputs(seed: int = 0):
    key = jax.random.key(seed)
    ks = jax.random.split(key, 32)
    f32 = jnp.float32
    L = DEPTH

    def nrm(k, shape, scale):
        return jax.random.normal(k, shape, f32) * scale

    def gain(k, shape):
        return 1.0 + 0.05 * jax.random.normal(k, shape, f32)

    x = nrm(ks[0], (BATCH, SEQ, D_MODEL), 1.0)
    c = nrm(ks[1], (BATCH, D_MODEL), 1.0)
    w_ada = nrm(ks[2], (L, D_MODEL, 6 * D_MODEL), 0.5 * D_MODEL ** -0.5)
    b_ada = nrm(ks[3], (L, 6 * D_MODEL), 0.01)
    norm_pre_mix = gain(ks[4], (L, D_MODEL))
    norm_post_mix = gain(ks[5], (L, D_MODEL))
    norm_pre_ffn = gain(ks[6], (L, D_MODEL))
    norm_post_ffn = gain(ks[7], (L, D_MODEL))
    w_in = nrm(ks[8], (L, D_MODEL, IN_DIM), D_MODEL ** -0.5)
    lru_conv_w = nrm(ks[9], (L, CONV_WIDTH, LRU_WIDTH), CONV_WIDTH ** -0.5)
    lru_conv_b = nrm(ks[10], (L, LRU_WIDTH), 0.01)
    lru_wa = nrm(ks[11], (L, LRU_HEADS, LRU_HEAD_DIM, LRU_HEAD_DIM), LRU_HEAD_DIM ** -0.5)
    lru_ba = nrm(ks[12], (L, LRU_WIDTH), 0.01)
    lru_wx = nrm(ks[13], (L, LRU_HEADS, LRU_HEAD_DIM, LRU_HEAD_DIM), LRU_HEAD_DIM ** -0.5)
    lru_bx = nrm(ks[14], (L, LRU_WIDTH), 0.01)
    a_pow = jax.random.uniform(ks[15], (L, LRU_WIDTH), f32, 0.9, 0.999)
    a_base = a_pow ** (1.0 / LRU_C)
    lru_lambda = jnp.log(a_base) - jnp.log1p(-a_base)
    ssd_conv_w = nrm(ks[16], (L, CONV_WIDTH, SSD_CONV_DIM), CONV_WIDTH ** -0.5)
    ssd_conv_b = nrm(ks[17], (L, SSD_CONV_DIM), 0.01)
    dt0 = jnp.exp(jax.random.uniform(ks[18], (L, SSD_HEADS), f32, math.log(1e-3), math.log(1e-1)))
    ssd_dt_bias = dt0 + jnp.log(-jnp.expm1(-dt0))
    ssd_a_log = jnp.log(jax.random.uniform(ks[19], (L, SSD_HEADS), f32, 1.0, 16.0))
    ssd_d = 1.0 + 0.1 * jax.random.normal(ks[20], (L, SSD_HEADS), f32)
    ssd_norm_w = gain(ks[21], (L, SSD_INNER))
    w_lru_out = nrm(ks[22], (L, LRU_WIDTH, D_MODEL), LRU_WIDTH ** -0.5)
    w_ssd_out = nrm(ks[23], (L, SSD_INNER, D_MODEL), SSD_INNER ** -0.5)
    w_o = nrm(ks[24], (L, D_MODEL, D_MODEL), D_MODEL ** -0.5)
    peer_wq = nrm(ks[25], (L, D_MODEL, PEER_HEADS * PEER_QUERY_DIM), D_MODEL ** -0.5)
    peer_sub_keys = nrm(ks[26], (L, PEER_HEADS, 2, PEER_KEYS, PEER_HALF), PEER_HALF ** -0.5)
    peer_down = nrm(ks[27], (L, PEER_EXPERTS, D_MODEL), D_MODEL ** -0.5)
    peer_up = nrm(ks[28], (L, PEER_EXPERTS, D_MODEL), (PEER_HEADS * PEER_TOPK) ** -0.5)
    return {
        'x': x, 'c': c, 'w_ada': w_ada, 'b_ada': b_ada,
        'norm_pre_mix': norm_pre_mix, 'norm_post_mix': norm_post_mix,
        'norm_pre_ffn': norm_pre_ffn, 'norm_post_ffn': norm_post_ffn,
        'w_in': w_in, 'lru_conv_w': lru_conv_w, 'lru_conv_b': lru_conv_b,
        'lru_wa': lru_wa, 'lru_ba': lru_ba, 'lru_wx': lru_wx, 'lru_bx': lru_bx,
        'lru_lambda': lru_lambda, 'ssd_conv_w': ssd_conv_w, 'ssd_conv_b': ssd_conv_b,
        'ssd_dt_bias': ssd_dt_bias, 'ssd_a_log': ssd_a_log, 'ssd_d': ssd_d,
        'ssd_norm_w': ssd_norm_w, 'w_lru_out': w_lru_out, 'w_ssd_out': w_ssd_out,
        'w_o': w_o, 'peer_wq': peer_wq, 'peer_sub_keys': peer_sub_keys,
        'peer_down': peer_down, 'peer_up': peer_up,
    }

def reference(x, c, w_ada, b_ada, norm_pre_mix, norm_post_mix, norm_pre_ffn, norm_post_ffn,
              w_in, lru_conv_w, lru_conv_b, lru_wa, lru_ba, lru_wx, lru_bx, lru_lambda,
              ssd_conv_w, ssd_conv_b, ssd_dt_bias, ssd_a_log, ssd_d, ssd_norm_w,
              w_lru_out, w_ssd_out, w_o, peer_wq, peer_sub_keys, peer_down, peer_up):
    o1 = LRU_WIDTH
    o2 = o1 + SSD_INNER
    o3 = o2 + SSD_CONV_DIM
    o4 = o3 + SSD_HEADS
    o5 = o4 + D_MODEL
    c_act = jax.nn.silu(c)
    for l in range(DEPTH):
        mod = c_act @ w_ada[l] + b_ada[l]
        shift1, scale1, gate1, shift2, scale2, gate2 = jnp.split(mod[:, None, :], 6, axis=-1)
        h = rms_norm(x, norm_pre_mix[l]) * (1.0 + scale1) + shift1
        proj = h @ w_in[l]
        lru_x, ssd_z, ssd_xbc, ssd_dt, gate_lru, gate_ssd = jnp.split(proj, [o1, o2, o3, o4, o5], axis=-1)
        y_lru = rg_lru(causal_depthwise_conv(lru_x, lru_conv_w[l], lru_conv_b[l]),
                       lru_wa[l], lru_ba[l], lru_wx[l], lru_bx[l], lru_lambda[l])
        y_ssd = ssd_mixer(ssd_xbc, ssd_z, ssd_dt, ssd_conv_w[l], ssd_conv_b[l],
                          ssd_dt_bias[l], ssd_a_log[l], ssd_d[l], ssd_norm_w[l])
        merged = (jax.nn.sigmoid(gate_lru) * (y_lru @ w_lru_out[l])
                  + jax.nn.sigmoid(gate_ssd) * (y_ssd @ w_ssd_out[l]))
        x = x + gate1 * rms_norm(merged @ w_o[l], norm_post_mix[l])
        h = rms_norm(x, norm_pre_ffn[l]) * (1.0 + scale2) + shift2
        y_ffn = peer_ffn(h, peer_wq[l], peer_sub_keys[l], peer_down[l], peer_up[l])
        x = x + gate2 * rms_norm(y_ffn, norm_post_ffn[l])
    return x


_drawn_inputs = setup_inputs


def setup_inputs(seed=0):
    import zlib

    import numpy as np

    out = dict(_drawn_inputs(seed))
    spreads = {}
    factors = {'norm_post_ffn': 4.136, 'lru_ba': 8.0, 'lru_bx': 5.758, 'ssd_conv_b': 4.153}
    for name, (base, spread) in spreads.items():
        noise = np.random.default_rng([zlib.crc32(name.encode()), seed]).standard_normal(out[name].shape)
        drawn = base * np.exp(spread * noise) if base else spread * noise
        out[name] = jnp.asarray(drawn.astype(out[name].dtype))
    for name, factor in factors.items():
        out[name] = (out[name] * factor).astype(out[name].dtype)
    return out
```

```python
from contextlib import ExitStack

import concourse.bass as bass
from concourse import mybir

F32 = mybir.dt.float32
F32R = mybir.dt.float32r
BF16 = mybir.dt.bfloat16
U32 = mybir.dt.uint32
ALU = mybir.AluOpType
ACT = mybir.ActivationFunctionType
AX = mybir.AxisListType

P = 128
T = 1024
TB = T // P
TH = 512
D = 1024
KD = D // P
CW = 4
EPS = 1e-6
LRU_C = 8.0
SI = 2048
SH = 32
SG = 4
SHG = SH // SG
SP_ = SI // SH
XBC = SI + 2 * SG * P
COL_LRU, COL_Z, COL_XBC = 0, D, D + SI
COL_DT = COL_XBC + XBC
COL_GATE = COL_DT + SH
NEG = -30000.0

VEC = {}
_row = 0
for _name, _n in (("b_ada", 48), ("norm_pre_mix", 8), ("norm_pre_ffn", 8), ("lru_conv_w", 32),
                  ("lru_conv_b", 8), ("lru_ba", 8), ("lru_bx", 8), ("lru_lambda", 8),
                  ("ssd_conv_w", 96), ("ssd_conv_b", 24), ("ssd_norm_w", 16), ("c", 8)):
    VEC[_name] = _row
    _row += _n
VEC_TILES = ((0, 128), (128, 120), (248, 24))
assert _row == 272 and VEC["ssd_norm_w"] == 248


class Machine:

    def __init__(self, nc, stack):
        self.nc, self.stack = nc, stack
        self.phase_sems = []

    def sb(self, stack, name, shape, dt=F32):
        return stack.enter_context(self.nc.sbuf_tensor(name, shape, dt))

    def ps(self, stack, name, shape, dt=F32):
        return stack.enter_context(self.nc.psum_tensor(name, shape, dt))

    def kept_sem(self, name):
        return self.stack.enter_context(self.nc.semaphore(name))

    def sem(self, name):
        self.phase_sems.append(self.nc.alloc_semaphore(name))
        return self.phase_sems[-1]

    def end_phase(self):
        self.nc.all_engine_barrier()
        self.nc.clear_and_free_semaphores(self.phase_sems)
        self.nc.all_engine_barrier()
        self.phase_sems = []


def vectors_and_norm(m, inp, keep):
    nc = m.nc
    with ExitStack() as st:
        rows = m.sb(st, "vec_rows", [P, 3, P])
        x_in = m.sb(st, "x_in", [P, TB, D])
        junk = m.sb(st, "square_out", [P, D])
        w_ada = m.sb(st, "w_ada_sb", [P, 2, KD, D])
        ssq = m.sb(st, "x_ssq", [P, TB])
        std = m.sb(st, "x_std", [P, TB])
        rstd = m.sb(st, "x_rstd", [P, TB])
        h_full = m.sb(st, "h_full", [P, 2, TH])
        mult1 = m.sb(st, "mult1", [P, KD])
        eps = m.sb(st, "eps0", [P, 1])
        c_cols = m.sb(st, "c_cols", [P, KD])
        c_wide = m.sb(st, "c_wide", [P, KD, P])
        norm_rows = m.sb(st, "norm_rows", [P, 2, D])
        ps_a = [m.ps(st, f"p0_a{i}", [P, 512]) for i in range(2)]
        ps_b = [m.ps(st, f"p0_b{i}", [P, 512]) for i in range(2)]
        ps_mod = [m.ps(st, f"p0_mod{i}", [P, 512]) for i in range(4)]
        ident, tri, mask, ones = keep["ident"], keep["tri"], keep["mask"], keep["ones"]
        cols, mod, gate_rows = keep["cols"], keep["mod"], keep["gate_rows"]
        hT = keep["hT"]

        consts_ready = keep["consts_ready"]
        consts_set = m.sem("consts_set")
        vec_loaded = m.sem("vec_loaded")
        row_vecs_loaded = m.sem("row_vecs_loaded")
        x_loaded = [m.sem(f"x_loaded{i}") for i in range(4)]
        ada_loaded = [m.sem(f"ada_loaded{i}") for i in range(2)]
        cols_turned = m.sem("cols_turned")
        cols_ready = m.sem("cols_ready")
        c_ready = m.sem("c_ready")
        ssq_ready = m.sem("ssq_ready")
        std_ready = m.sem("std_ready")
        rstd_ready = m.sem("rstd_ready")
        xn_ready = m.sem("xn_ready")
        mod_done = m.sem("mod_done")
        mod_ready = m.sem("mod_ready")
        mult_ready = m.sem("mult_ready")
        turned = m.sem("x_turned")
        full_ready = m.sem("h_full_ready")
        hi_ready = m.sem("h_hi_ready")
        lo_ready = m.sem("h_lo_ready")
        rows_done = m.sem("gate_rows_done")
        rows_ready = m.sem("gate_rows_ready")

        VECS = len(VEC)

        def vec_parts():
            for name, shape in (("b_ada", "one (a b) -> (one a) b"), ("norm_pre_mix", None),
                                ("norm_pre_ffn", None), ("lru_conv_w", "w"), ("lru_conv_b", None),
                                ("lru_ba", None), ("lru_bx", None), ("lru_lambda", None),
                                ("ssd_conv_w", "w"), ("ssd_conv_b", None), ("ssd_norm_w", None),
                                ("c", None)):
                pattern = "o w (a b) -> (o w a) b" if shape == "w" else "o (a b) -> (o a) b"
                src = inp[name].rearrange(pattern, b=P)
                yield src, VEC[name]

        SEGS = (0, 1, 3, 4, 2, 5)

        with nc.Block() as block:
            @block.sync
            def _(sp):
                n = 0
                for src, row in vec_parts():
                    tile = (row >= VEC_TILES[1][0]) + (row >= VEC_TILES[2][0])
                    at = row - VEC_TILES[tile][0]
                    sp.dma_start(rows[at:at + src.shape[0], tile, :], src).then_inc(vec_loaded, 16)
                    n += 1
                assert n == VECS
                for t in range(TB):
                    sp.dma_start(x_in[:, t, :], inp["x"][0, t * P:(t + 1) * P, :]).then_inc(x_loaded[t // 2], 16)
                for g, (seg, norm) in enumerate(((2, "norm_post_mix"), (5, "norm_post_ffn"))):
                    sp.dma_start(gate_rows[:, g, :], inp["b_ada"][0, seg * D:(seg + 1) * D].partition_broadcast(P)
                                 ).then_inc(row_vecs_loaded, 16)
                    sp.dma_start(norm_rows[:, g, :], inp[norm][0].partition_broadcast(P)).then_inc(row_vecs_loaded, 16)
                for i, s in enumerate(SEGS):
                    if i >= 2:
                        sp.wait_ge(mod_done, i - 1)
                    sp.dma_start(w_ada[:, i % 2], inp["w_ada"][0, :, s * D:(s + 1) * D].rearrange(
                        "(k p) n -> p k n", p=P)).then_inc(ada_loaded[i % 2], 16)

            @block.gpsimd
            def _(pool):
                pool.memset(ident[:], 0.0).then_inc(consts_set, 1)
                pool.memset(tri[:], 1.0).then_inc(consts_set, 1)
                pool.memset(mask[:], 0.0).then_inc(consts_set, 1)
                pool.memset(ones[:], 1.0).then_inc(consts_ready, 1)
                pool.memset(eps[:], EPS).then_inc(consts_ready, 1)
                pool.wait_ge(consts_set, 3)
                pool.affine_select(out=ident[:], in_=ident[:], compare_op=ALU.not_equal, fill=1.0, base=0,
                                   pattern=[[-1, P]], channel_multiplier=1).then_inc(consts_ready, 1)
                pool.affine_select(out=tri[:], in_=tri[:], compare_op=ALU.is_ge, fill=0.0, base=0,
                                   pattern=[[1, P]], channel_multiplier=-1).then_inc(consts_ready, 1)
                pool.affine_select(out=mask[:], in_=mask[:], compare_op=ALU.is_ge, fill=NEG, base=0,
                                   pattern=[[0, 4], [1, P]], channel_multiplier=-1).then_inc(consts_ready, 1)
                for n in range(2 * KD):
                    k, half = divmod(n, 2)
                    pool.wait_ge(full_ready, n + 1)
                    pool.tensor_copy(hT[0][:, k, half * TH:(half + 1) * TH], h_full[:, n % 2, :]).then_inc(hi_ready, 1)

            @block.scalar
            def _(act):
                act.wait_ge(consts_ready, 5)
                for t in range(TB):
                    act.wait_ge(x_loaded[t // 2], 32)
                    act.activation(junk[:], x_in[:, t, :], ACT.Square, accum_out=ssq[:, t:t + 1]).then_inc(ssq_ready, 1)
                    act.wait_ge(ssq_ready, t + 1)
                act.activation(std[:], ssq[:], ACT.Sqrt, bias=eps[:], scale=1.0 / D).then_inc(std_ready, 1)
                act.wait_ge(cols_ready, 3)
                act.activation(c_cols[:], cols[:, VEC["c"]:VEC["c"] + KD], ACT.Silu).then_inc(c_ready, 1)

            @block.vector
            def _(dve):
                for t, (row, n) in enumerate(VEC_TILES):
                    dve.wait_ge(cols_turned, t + 1)
                    dve.tensor_copy(cols[:, row:row + n], ps_a[t % 2][:, 0:n]).then_inc(cols_ready, 1)
                dve.wait_ge(c_ready, 1)
                dve.tensor_copy(c_wide[:], c_cols[:].unsqueeze(2).to_broadcast([P, KD, P])).then_inc(c_ready, 1)
                dve.wait_ge(std_ready, 1)
                dve.reciprocal(rstd[:], std[:]).then_inc(rstd_ready, 1)
                dve.wait_ge(rstd_ready, 1)
                for t in range(TB):
                    dve.tensor_scalar(x_in[:, t, :], x_in[:, t, :], rstd[:, t:t + 1], None, ALU.mult).then_inc(xn_ready, 1)
                for i, s in enumerate(SEGS[:4]):
                    dve.wait_ge(mod_done, i + 1)
                    dve.tensor_tensor(mod[:, i, :], ps_mod[i][:, 0:KD], cols[:, s * KD:(s + 1) * KD], ALU.add).then_inc(mod_ready, 1)
                    if i == 1:
                        dve.wait_ge(mod_ready, 2)
                        nw = VEC["norm_pre_mix"]
                        dve.scalar_tensor_tensor(mult1[:], mod[:, 1, :], 1.0, cols[:, nw:nw + KD],
                                                 ALU.add, ALU.mult).then_inc(mult_ready, 1)
                        dve.wait_ge(mult_ready, 1)
                        for n in range(2 * KD):
                            k, half = divmod(n, 2)
                            dve.wait_ge(turned, n + 1)
                            if n >= 2:
                                dve.wait_ge(hi_ready, n - 1)
                            dve.tensor_scalar(h_full[:, n % 2, :], ps_a[n % 2][:], mult1[:, k:k + 1],
                                              mod[:, 0, k:k + 1], ALU.mult, ALU.add).then_inc(full_ready, 1)
                            dve.wait_ge(hi_ready, n + 1)
                            sl = slice(half * TH, (half + 1) * TH)
                            dve.tensor_tensor(hT[1][:, k, sl], h_full[:, n % 2, :],
                                              hT[0][:, k, sl].bitcast(F32), ALU.subtract).then_inc(lo_ready, 1)
                dve.wait_ge(mod_ready, 4)
                nw = VEC["norm_pre_ffn"]
                dve.scalar_tensor_tensor(mod[:, 3, :], mod[:, 3, :], 1.0, cols[:, nw:nw + KD],
                                         ALU.add, ALU.mult).then_inc(mult_ready, 1)
                dve.wait_ge(row_vecs_loaded, 16 * 4)
                for n in range(4):
                    dve.wait_ge(rows_done, n + 1)
                    part = gate_rows[:, n // 2, (n % 2) * TH:(n % 2 + 1) * TH]
                    dve.tensor_tensor(part, ps_b[n % 2][:], part, ALU.add).then_inc(rows_ready, 1)
                dve.wait_ge(rows_ready, 4)
                dve.tensor_tensor(gate_rows[:], gate_rows[:], norm_rows[:], ALU.mult).then_inc(rows_ready, 1)

            @block.tensor
            def _(pe):
                pe.wait_ge(consts_ready, 5)
                pe.wait_ge(vec_loaded, 16 * VECS)
                for t, (row, n) in enumerate(VEC_TILES):
                    if t >= 2:
                        pe.wait_ge(cols_ready, t - 1)
                    pe.transpose(ps_a[t % 2][:, 0:n], rows[0:n, t, :], ident[0:n, 0:n]).then_inc(cols_turned, 1)
                pe.wait_ge(c_ready, 2)
                for i, s in enumerate(SEGS):
                    pe.wait_ge(ada_loaded[i % 2], 16 * (i // 2 + 1))
                    if i < 4:
                        for j in range(KD):
                            for k in range(KD):
                                mm = pe.matmul(ps_mod[i][:, j:j + 1], w_ada[:, i % 2, k, j * P:(j + 1) * P],
                                               c_cols[:, k:k + 1], start=(k == 0), stop=(k == KD - 1),
                                               skip_group_check=True)
                        mm.then_inc(mod_done, 1)
                    else:
                        for half in range(2):
                            n = 2 * (i - 4) + half
                            if n >= 2:
                                pe.wait_ge(rows_ready, n - 1)
                            for k in range(KD):
                                mm = pe.matmul(ps_b[n % 2][:], c_wide[:, k, :],
                                               w_ada[:, i % 2, k, half * TH:(half + 1) * TH],
                                               start=(k == 0), stop=(k == KD - 1))
                            mm.then_inc(rows_done, 1)
                    if i == 1:
                        pe.wait_ge(xn_ready, TB)
                        for n in range(2 * KD):
                            k, half = divmod(n, 2)
                            if n >= 2:
                                pe.wait_ge(full_ready, n - 1)
                            else:
                                pe.wait_ge(cols_ready, 3)
                            for j in range(4):
                                mm = pe.transpose(ps_a[n % 2][:, j * P:(j + 1) * P],
                                                  x_in[:, half * 4 + j, k * P:(k + 1) * P], ident[:])
                            mm.then_inc(turned, 1)


def pairs(eng, lo, hi, body):
    assert lo % 2 == 0 and hi % 2 == 0
    if lo == 0:
        body(0, 0)
        body(1, 1)
        lo = 2
    with eng.Fori(lo // 2, hi // 2) as p:
        body(p * 2, 0)
        body(p * 2 + 1, 1)


def wait_from(eng, sem, value):
    if not isinstance(value, int) or value > 0:
        eng.wait_ge(sem, value)


def alone(eng, passed):
    eng.sem_inc(passed, 1)


def of_buffer(i, u):
    return (i - u) * 8


def project_in(m, inp, keep, scratch):
    nc = m.nc
    N_LRU, N_XBC, N_Z, N_GATE = KD, XBC // P, SI // P, 2 * KD
    B_XBC = N_LRU
    B_Z = B_XBC + N_XBC
    B_GATE = B_Z + N_Z
    TILES = B_GATE + N_GATE
    pool_passed, act_passed = keep["pool_passed"], keep["act_passed"]
    hT, cols, sp_in, sp_out = keep["hT"], keep["cols"], keep["sp_in"], keep["sp_out"]
    with ExitStack() as st:
        w_raw = m.sb(st, "w_raw", [P, 2, KD, P])
        w_hi = m.sb(st, "w_hi", [P, 2, KD, P], F32R)
        w_lo = m.sb(st, "w_lo", [P, 2, KD, P], F32R)
        dt_raw = m.sb(st, "w_dt_raw", [P, KD, SH])
        dt_hi = m.sb(st, "w_dt_hi", [P, KD, SH], F32R)
        dt_lo = m.sb(st, "w_dt_lo", [P, KD, SH], F32R)
        dt_bias = m.sb(st, "dt_bias", [P, SH])
        pre = m.sb(st, "conv_in", [P, 2, CW - 1 + T])
        acc = m.sb(st, "conv_out", [P, 2, T])
        fin = m.sb(st, "act_out", [P, 2, T])
        xl = m.sb(st, "lru_x", [P, KD, T])
        w_gate = m.sb(st, "lru_w", [P, 2, KD, P])
        w_cur = m.sb(st, "lru_w_cur", [P, 2, P])
        r_, i_, a_ = (m.sb(st, n, [P, T]) for n in ("lru_r", "lru_i", "lru_a"))
        th, v_, sq, ix, hl = (m.sb(st, n, [P, T]) for n in ("lru_tanh", "lru_v", "lru_sqrt", "lru_ix", "lru_h"))
        NS = KD + TB * SH
        s_abs, s_e, s_u, s_c = (m.sb(st, n, [P, NS]) for n in ("sp_abs", "sp_exp", "sp_one_plus", "sp_corr"))
        ps = [m.ps(st, f"p1_{i}", [P, 2, TH]) for i in range(2)]
        ps_g = m.ps(st, "p1_gates", [P, 2, TH])
        ps_dt = m.ps(st, "p1_dt", [P, 512])

        w_loaded = [m.sem(f"w_in_loaded{i}") for i in range(2)]
        small_loaded = m.sem("small_loaded")
        zeroed = m.sem("lru_w_zeroed")
        hi_done, lo_done = m.sem("w_hi_done"), m.sem("w_lo_done")
        dt_split, dt_done = m.sem("dt_split"), m.sem("dt_done")
        sp_dve, sp_act = m.sem("softplus_dve"), m.sem("softplus_act")
        mm_done, evac_done = m.sem("proj_done"), m.sem("proj_evacuated")
        conv_step, silu_done = m.sem("conv_step"), m.sem("silu_done")
        act_done = m.sem("act_done")
        stored = [m.sem(f"act_stored{i}") for i in range(2)]
        w_cur_ready, lru_mm, sig_done = m.sem("lru_w_ready"), m.sem("lru_products"), m.sem("lru_sigmoids")
        exp_done, v_done, sqrt_done = m.sem("lru_exp_tanh"), m.sem("lru_v_done"), m.sem("lru_sqrt_done")
        ix_done, u_done, scan_done = m.sem("lru_ix_done"), m.sem("lru_u_done"), m.sem("lru_scan_done")
        h_stored = m.sem("lru_h_stored")

        def w_in(col, j):
            return inp["w_in"][0, :, bass.ds(j * P + col, P)].rearrange("(k p) n -> p k n", p=P)

        SEGMENTS = ((0, B_XBC, COL_LRU), (B_XBC, B_Z, COL_XBC - B_XBC * P),
                    (B_Z, B_GATE, COL_Z - B_Z * P), (B_GATE, TILES, COL_GATE - B_GATE * P))

        def quads(eng, tile, lru):
            for seg in (2, 3):
                lo, hi, _ = SEGMENTS[seg]
                with eng.Fori(lo // 4, hi // 4) as p:
                    j = p - B_Z // 4
                    for q in range(4):
                        tile(p * 4 + q, q % 2, seg)
                        lru(j, q)

        with nc.Block() as block:
            @block.sync
            def _(sp):
                sp.dma_start(dt_raw[:], inp["w_in"][0, :, COL_DT:COL_DT + SH].rearrange("(k p) n -> p k n", p=P)
                             ).then_inc(small_loaded, 16)
                sp.dma_start(dt_bias[:], inp["ssd_dt_bias"][0].partition_broadcast(P)).then_inc(small_loaded, 16)

                def load(col):
                    def body(i, u):
                        wait_from(sp, lo_done, i - 1)
                        sp.dma_start(w_raw[:, u], w_in(col, i)).then_inc(w_loaded[u], 16)
                    return body

                pairs(sp, 0, B_XBC, load(SEGMENTS[0][2]))
                sp.wait_ge(zeroed, 1)
                for g, name in enumerate(("lru_wa", "lru_wx")):
                    for odd in range(2):
                        at = slice(64 * odd, 64 * odd + 64)
                        sp.dma_start(w_gate[at, g, :, at],
                                     inp[name][0].rearrange("(j two) a b -> two a j b", two=2)[odd]
                                     ).then_inc(small_loaded, 16)
                for lo, hi, col in SEGMENTS[1:]:
                    pairs(sp, lo, hi, load(col))

            @block.gpsimd
            def _(pool):
                pool.memset(w_gate[:], 0.0).then_inc(zeroed, 1)
                pool.memset(pre[:, :, 0:CW - 1], 0.0).then_inc(zeroed, 1)
                pool.wait_ge(small_loaded, 32)
                pool.tensor_copy(dt_hi[:], dt_raw[:]).then_inc(dt_split, 1)
                pool.wait_ge(dt_split, 1)
                pool.tensor_tensor(dt_lo[:], dt_raw[:], dt_hi[:].bitcast(F32), ALU.subtract).then_inc(dt_split, 1)

                def cut(i, u, seg=0):
                    pool.wait_ge(w_loaded[u], of_buffer(i, u) + 16)
                    wait_from(pool, mm_done, i - 1)
                    alone(pool, pool_passed)
                    pool.tensor_copy(w_hi[:, u], w_raw[:, u]).then_inc(hi_done, 1)
                    pool.wait_ge(hi_done, i + 1)
                    pool.tensor_tensor(w_lo[:, u], w_raw[:, u], w_hi[:, u].bitcast(F32), ALU.subtract
                                       ).then_inc(lo_done, 1)

                def lru(j, q):
                    if q == 0:
                        wait_from(pool, lru_mm, j * 2)
                        alone(pool, pool_passed)
                        pool.tensor_copy(w_cur[:], w_gate[:, :, bass.ds(j, 1), :].rearrange("p g o n -> p (g o) n")
                                         ).then_inc(w_cur_ready, 1)
                    if q == 3:
                        pool.wait_ge(sig_done, j * 4 + 4)
                        wait_from(pool, u_done, j)
                        pool.tensor_tensor(ix[:], i_[:], xl[:, bass.ds(j, 1), :].rearrange("p o n -> p (o n)"),
                                           ALU.mult).then_inc(ix_done, 1)

                pairs(pool, 0, B_XBC, cut)
                pairs(pool, B_XBC, B_Z, cut)
                pool.wait_ge(small_loaded, 96)
                quads(pool, cut, lru)

            @block.tensor
            def _(pe):
                pe.wait_ge(dt_split, 2)
                for t in range(TB):
                    n = 0
                    for k in range(KD):
                        for h, w in ((0, dt_hi), (0, dt_lo), (1, dt_hi)):
                            mm = pe.matmul(ps_dt[:, t * SH:(t + 1) * SH], hT[h][:, k, t * P:(t + 1) * P], w[:, k, :],
                                           start=(n == 0), stop=(n == 3 * KD - 1), skip_group_check=True)
                            n += 1
                mm.then_inc(dt_done, 1)

                def tile(i, u, seg=0):
                    pe.wait_ge(lo_done, i + 1)
                    wait_from(pe, evac_done, i - 1)
                    for half in range(2):
                        n = 0
                        for k in range(KD):
                            for w, h in ((w_hi, 0), (w_hi, 1), (w_lo, 0)):
                                mm = pe.matmul(ps[u][:, half, :], w[:, u, k, :], hT[h][:, k, half * TH:(half + 1) * TH],
                                               start=(n == 0), stop=(n == 3 * KD - 1))
                                n += 1
                    mm.then_inc(mm_done, 1)

                def lru(j, q):
                    if q > 1:
                        return
                    if q == 0:
                        pe.wait_ge(w_cur_ready, j + 1)
                    wait_from(pe, sig_done, j * 4 + 2 * q)
                    for g in range(2):
                        mm = pe.matmul(ps_g[:, g, :], w_cur[:, g, :],
                                       xl[:, bass.ds(j, 1), q * TH:(q + 1) * TH].rearrange("p o n -> p (o n)"),
                                       start=True, stop=True)
                    mm.then_inc(lru_mm, 1)

                pairs(pe, 0, B_XBC, tile)
                pairs(pe, B_XBC, B_Z, tile)
                pe.wait_ge(conv_step, 4 * B_XBC)
                quads(pe, tile, lru)

            @block.scalar
            def _(act):
                act.wait_ge(sp_dve, 2)
                act.activation(s_abs[:], sp_in[:], ACT.Abs).then_inc(sp_act, 1)
                act.wait_ge(sp_act, 1)
                act.activation(s_e[:], s_abs[:], ACT.Exp, scale=-1.0).then_inc(sp_act, 1)
                act.wait_ge(sp_dve, 3)
                act.activation(sp_out[:], s_u[:], ACT.Ln).then_inc(sp_act, 1)

                def conv(i, u, seg):
                    act.wait_ge(mm_done, i + 1)
                    wait_from(act, conv_step, i * 4 - 4)
                    act.copy(pre[:, u, CW - 1:], ps[u][:].rearrange("p h n -> p (h n)")).then_inc(evac_done, 1)
                    if seg == 1:
                        act.wait_ge(conv_step, i * 4 + 4)
                        wait_from(act, stored[u], of_buffer(i - B_XBC, u) if isinstance(i, int) else of_buffer(i, u) - 8 * B_XBC)
                        act.activation(fin[:, u], acc[:, u], ACT.Silu).then_inc(silu_done, 1)
                        act.wait_ge(silu_done, i - B_XBC + 1)
                        act.dma_start(scratch["xbc"][bass.ds((i - B_XBC) * P, P), :], fin[:, u]).then_inc(stored[u], 16)

                def direct(i, u, seg):
                    act.wait_ge(mm_done, i + 1)
                    act.wait_ge(stored[u], of_buffer(i, u) - 8 * B_XBC)
                    act.activation(fin[:, u], ps[u][:].rearrange("p h n -> p (h n)"),
                                   ACT.Silu if seg == 2 else ACT.Sigmoid).then_inc(evac_done, 1)
                    act.wait_ge(evac_done, i + 1)
                    dest = scratch["z" if seg == 2 else "gates"]
                    act.dma_start(dest[bass.ds((i - SEGMENTS[seg][0]) * P, P), :], fin[:, u]).then_inc(stored[u], 16)

                def lru(j, q):
                    if q < 2:
                        act.wait_ge(lru_mm, j * 2 + q + 1)
                        if q == 0:
                            wait_from(act, ix_done, j)
                            wait_from(act, exp_done, j * 2)
                        alone(act, act_passed)
                        for g, (dst, b) in enumerate(((r_, "lru_ba"), (i_, "lru_bx"))):
                            act.activation(dst[:, q * TH:(q + 1) * TH], ps_g[:, g, :], ACT.Sigmoid,
                                           bias=cols[:, bass.ds(j + VEC[b], 1)]).then_inc(sig_done, 1)
                    if q == 1:
                        act.wait_ge(sig_done, j * 4 + 4)
                        wait_from(act, scan_done, j)
                        alone(act, act_passed)
                        act.activation(a_[:], r_[:], ACT.Exp, scale=sp_out[:, bass.ds(j, 1)]).then_inc(exp_done, 1)
                        act.activation(th[:], r_[:], ACT.Tanh, scale=sp_in[:, bass.ds(j, 1)]).then_inc(exp_done, 1)
                    if q == 2:
                        act.wait_ge(v_done, j * 2 + 2)
                        act.activation(sq[:], v_[:], ACT.Sqrt).then_inc(sqrt_done, 1)
                    if q == 3:
                        act.wait_ge(scan_done, j + 1)
                        act.dma_start(scratch["y_lru"][bass.ds(j * P, P), :], hl[:]).then_inc(h_stored, 16)

                pairs(act, 0, B_XBC, lambda i, u: conv(i, u, 0))
                pairs(act, B_XBC, B_Z, lambda i, u: conv(i, u, 1))
                act.wait_ge(sp_dve, 9)
                quads(act, direct, lru)
                act.wait_ge(h_stored, 16 * KD)
                for u in range(2):
                    act.wait_ge(stored[u], 8 * (TILES - B_XBC))

            @block.vector
            def _(dve):
                dve.tensor_scalar(sp_in[:, 0:KD], cols[:, VEC["lru_lambda"]:VEC["lru_lambda"] + KD], -1.0, None,
                                  ALU.mult).then_inc(sp_dve, 1)
                dve.wait_ge(dt_done, 1)
                dve.tensor_tensor(sp_in[:, KD:].rearrange("p (t h) -> p t h", h=SH),
                                  ps_dt[:, 0:TB * SH].rearrange("p (t h) -> p t h", h=SH),
                                  dt_bias[:].unsqueeze(1).to_broadcast([P, TB, SH]), ALU.add).then_inc(sp_dve, 1)
                dve.wait_ge(sp_act, 2)
                dve.tensor_scalar(s_u[:], s_e[:], 1.0, None, ALU.add).then_inc(sp_dve, 1)
                dve.wait_ge(sp_dve, 3)
                dve.scalar_tensor_tensor(s_c[:], s_u[:], -1.0, s_e[:], ALU.add, ALU.subtract).then_inc(sp_dve, 1)
                dve.reciprocal(s_abs[:], s_u[:]).then_inc(sp_dve, 1)
                dve.wait_ge(sp_dve, 5)
                dve.tensor_tensor(s_c[:], s_c[:], s_abs[:], ALU.mult).then_inc(sp_dve, 1)
                dve.wait_ge(sp_dve, 6)
                dve.wait_ge(sp_act, 3)
                dve.tensor_tensor(sp_out[:], sp_out[:], s_c[:], ALU.subtract).then_inc(sp_dve, 1)
                dve.wait_ge(sp_dve, 7)
                dve.scalar_tensor_tensor(sp_out[:], sp_in[:], 0.0, sp_out[:], ALU.max, ALU.add).then_inc(sp_dve, 1)
                dve.wait_ge(sp_dve, 8)
                dve.tensor_scalar(sp_in[:, 0:KD], sp_out[:, 0:KD], LRU_C, None, ALU.mult).then_inc(sp_dve, 1)
                dve.wait_ge(sp_dve, 9)
                dve.tensor_scalar(sp_out[:, 0:KD], sp_in[:, 0:KD], -1.0, None, ALU.mult).then_inc(sp_dve, 1)

                dve.wait_ge(zeroed, 2)

                def conv(i, u, seg):
                    w, b, first, n = (("lru_conv_w", "lru_conv_b", 0, KD) if seg == 0 else
                                      ("ssd_conv_w", "ssd_conv_b", B_XBC, XBC // P))
                    j = i - first
                    if seg == 0:
                        dst = xl[:, j, :] if isinstance(j, int) else xl[:, bass.ds(j, 1), :].rearrange("p o n -> p (o n)")
                    else:
                        dst = acc[:, u, :]
                        wait_from(dve, silu_done, j - 1)
                    dve.wait_ge(evac_done, i + 1)
                    col = lambda c: cols[:, bass.ds(j + c, 1)]
                    dve.tensor_scalar(dst, pre[:, u, CW - 1:], col(VEC[w] + (CW - 1) * n), col(VEC[b]),
                                      ALU.mult, ALU.add).then_inc(conv_step, 1)
                    for s in range(1, CW):
                        tap = CW - 1 - s
                        dve.wait_ge(conv_step, i * 4 + s)
                        dve.scalar_tensor_tensor(dst, pre[:, u, tap:tap + T], col(VEC[w] + tap * n), dst,
                                                 ALU.mult, ALU.add).then_inc(conv_step, 1)

                pairs(dve, 0, B_XBC, lambda i, u: conv(i, u, 0))
                conv(B_XBC, 0, 1)
                conv(B_XBC + 1, 1, 1)
                pairs(dve, B_XBC + 2, B_Z, lambda i, u: conv(i, u, 1))
                with dve.Fori(0, KD) as j:
                    dve.wait_ge(exp_done, j * 2 + 2)
                    dve.tensor_tensor(v_[:], a_[:], a_[:], ALU.mult).then_inc(v_done, 1)
                    dve.wait_ge(v_done, j * 2 + 1)
                    dve.scalar_tensor_tensor(v_[:], v_[:], 1.0, th[:], ALU.add, ALU.mult).then_inc(v_done, 1)
                    dve.wait_ge(sqrt_done, j + 1)
                    dve.wait_ge(ix_done, j + 1)
                    dve.tensor_tensor(v_[:], sq[:], ix[:], ALU.mult).then_inc(u_done, 1)
                    dve.wait_ge(u_done, j + 1)
                    dve.wait_ge(h_stored, j * 16)
                    dve.tensor_tensor_scan(hl[:], a_[:], v_[:], 0.0, ALU.mult, ALU.add).then_inc(scan_done, 1)


def ssd(m, inp, keep, scratch):
    nc = m.nc
    CH = T // P
    W = SHG * SP_
    WT = W // P
    cols = keep["cols"]
    ident, tri, mask, ones = keep["ident"], keep["tri"], keep["mask"], keep["ones"]
    dt_all = keep["sp_out"][:, KD:].rearrange("p (c h) -> p c h", h=SH)
    act_passed, pool_passed = keep["act_passed"], keep["pool_passed"]
    with ExitStack() as st:
        xbc = m.sb(st, "xbc_chunk", [P, 2, XBC // P, P])
        zc = m.sb(st, "z_chunk", [P, 2, SI // P, P])
        a_row = m.sb(st, "a_row", [P, SH])
        d_row = m.sb(st, "d_row", [P, SH])
        da = m.sb(st, "da", [P, CH, SH])
        da_cur = [m.sb(st, f"da_cur{i}", [P, 2, SH], F32R) for i in range(2)]
        tri_r = m.sb(st, "tri_r", [P, P], F32R)
        ident_b = m.sb(st, "ident_b", [P, P], BF16)
        neg_acs = m.sb(st, "neg_acs", [P, CH, SH])
        dec_out = m.sb(st, "decay_out", [P, CH, SH])
        dec_state = m.sb(st, "decay_state", [P, CH, SH])
        dec_chunk = m.sb(st, "decay_chunk", [P, CH, SH])
        state = m.sb(st, "state", [P, SG, W])
        state_dec = m.sb(st, "state_dec", [P, W])
        xt = m.sb(st, "x_tok", [P, 2, W])
        xdt = m.sb(st, "x_dt", [P, 2, W])
        xdd = m.sb(st, "x_dt_decay", [P, 2, W])
        x_d = m.sb(st, "x_skip", [P, 2, W])
        bt = m.sb(st, "b_tok", [P, 2, P])
        ell = m.sb(st, "decay_ls", [P, SHG, P])
        mm_ = m.sb(st, "cb_decay", [P, 2, SHG, P])
        yo = m.sb(st, "y_tok", [P, 2, W])
        sq = m.sb(st, "y_sq", [P, 2, W])
        y_all = m.sb(st, "y_all", [P, SI // P, T])
        ss_all = m.sb(st, "ss_all", [P, SG, T])
        eps = m.sb(st, "eps2", [P, 1])
        ps_x = m.ps(st, "p2_x", [P, 512])
        ps_cb = m.ps(st, "p2_cb", [P, 512])
        ps_l = m.ps(st, "p2_l", [P, 2, 512])
        ps_o = m.ps(st, "p2_o", [P, 512])
        ps_s = m.ps(st, "p2_s", [P, 512])
        ps_y = m.ps(st, "p2_y", [P, 512])
        ps_q = m.ps(st, "p2_q", [P, 512])

        loaded = [m.sem(f"chunk_loaded{i}") for i in range(2)]
        rows_loaded, pre_dve, pre_act = m.sem("ssd_rows_loaded"), m.sem("ssd_pre_dve"), m.sem("ssd_pre_act")
        pre_pe, pre_pool = m.sem("ssd_pre_pe"), m.sem("ssd_pre_pool")
        cur_ready = m.sem("da_cur_ready")
        turned, spread = m.sem("ssd_turned"), m.sem("acs_spread")
        off_done, state_mm, y_done, ss_done = m.sem("y_off_done"), m.sem("state_mm"), m.sem("y_done"), m.sem("ss_done")
        xt_done, ell_done, sq_done, ss_kept = m.sem("x_tok_done"), m.sem("decay_ls_done"), m.sem("sq_done"), m.sem("ss_kept")
        bt_done, yo_done, state_done = m.sem("b_tok_done"), m.sem("y_tok_done"), m.sem("state_done")
        m_done, yg_done = m.sem("cb_decay_done"), m.sem("y_gated")
        pool_step = m.sem("ssd_pool_step")
        end_act, end_dve, y_stored = m.sem("ssd_end_act"), m.sem("ssd_end_dve"), m.sem("y_stored")

        LAST = CH * SG - 1

        def heads(ap):
            return ap.rearrange("p (h q) -> p h q", q=SP_)

        def per_head(ap, c, g):
            part = ap[:, bass.ds(c, 1), g * SHG:(g + 1) * SHG].rearrange("p o h -> p (o h)")
            return part.unsqueeze(2).to_broadcast([P, SHG, SP_])

        def token_slice(ap, lo, n, c):
            return ap[:, lo:lo + n, bass.ds(c * P, P)]

        with nc.Block() as block:
            @block.sync
            def _(sp):
                sp.dma_start(a_row[:], inp["ssd_a_log"][0].partition_broadcast(P)).then_inc(rows_loaded, 16)
                sp.dma_start(d_row[:], inp["ssd_d"][0].partition_broadcast(P)).then_inc(rows_loaded, 16)

                def load(c, u):
                    wait_from(sp, yg_done, c * 4 - 4)
                    sp.dma_start(xbc[:, u], scratch["xbc"].rearrange("(k p) t -> p k t", p=P)[:, :, bass.ds(c * P, P)]
                                 ).then_inc(loaded[u], 16)
                    sp.dma_start(zc[:, u], scratch["z"].rearrange("(k p) t -> p k t", p=P)[:, :, bass.ds(c * P, P)]
                                 ).then_inc(loaded[u], 16)

                pairs(sp, 0, CH, load)
                for k in range(SI // P):
                    sp.wait_ge(end_dve, 2 + k)
                    sp.dma_start(scratch["y_ssd"][k * P:(k + 1) * P, :], y_all[:, k, :]).then_inc(y_stored, 16)
                sp.wait_ge(y_stored, 16 * (SI // P))

            @block.gpsimd
            def _(pool):
                pool.memset(state[:], 0.0).then_inc(pre_pool, 1)
                pool.memset(eps[:], EPS).then_inc(pre_pool, 1)
                pool.wait_ge(rows_loaded, 32)
                pool.wait_ge(pre_act, 4)
                pool.wait_ge(pre_pool, 2)

                def step(c, u, g):
                    n, v = c * 4 + g, g % 2
                    pool.wait_ge(xt_done, n + 1)
                    wait_from(pool, y_done, n - 1)
                    alone(pool, pool_passed)
                    pool.tensor_tensor(heads(xdt[:, v]), heads(xt[:, v]), per_head(dt_all, c, g), ALU.mult
                                       ).then_inc(pool_step, 1)
                    pool.wait_ge(pool_step, n * 4 + 1)
                    wait_from(pool, state_mm, n - 1)
                    alone(pool, pool_passed)
                    pool.tensor_tensor(heads(xdd[:, v]), heads(xdt[:, v]), per_head(dec_state, c, g), ALU.mult
                                       ).then_inc(pool_step, 1)
                    wait_from(pool, yo_done, n * 2 - 2)
                    pool.tensor_tensor(heads(x_d[:, v]), heads(xt[:, v]),
                                       d_row[:, g * SHG:(g + 1) * SHG].unsqueeze(2).to_broadcast([P, SHG, SP_]),
                                       ALU.mult).then_inc(pool_step, 1)
                    wait_from(pool, state_done, n)
                    alone(pool, pool_passed)
                    pool.tensor_tensor(heads(state_dec[:]), heads(state[:, g]), per_head(dec_chunk, c, g), ALU.mult
                                       ).then_inc(pool_step, 1)

                pairs(pool, 0, CH, lambda c, u: [step(c, u, g) for g in range(SG)])

            @block.tensor
            def _(pe):
                pe.wait_ge(pre_dve, 3)
                pe.matmul(ps_x[:, 0:CH * SH], tri[:], da[:].rearrange("p c h -> p (c h)"), start=True, stop=True
                          ).then_inc(pre_pe, 1)
                pe.matmul(ps_cb[:, 0:CH * SH], ones[:], da[:].rearrange("p c h -> p (c h)"), start=True, stop=True
                          ).then_inc(pre_pe, 1)
                pe.wait_ge(pre_act, 4)
                pe.wait_ge(pre_dve, 6)
                pe.wait_ge(pre_pool, 2)

                def turn(c, u, g):
                    n = c * 4 + g
                    if g == 0:
                        pe.wait_ge(loaded[u], of_buffer(c, u) * 2 + 32)
                        pe.wait_ge(cur_ready, c * 2 + 2)
                    wait_from(pe, xt_done, n)
                    for j in range(WT):
                        pe.transpose(ps_x[:, j * P:(j + 1) * P], xbc[:, u, g * WT + j, :], ident[:])
                    wait_from(pe, m_done, n)
                    b_tile, c_tile = xbc[:, u, SI // P + g, :], xbc[:, u, SI // P + SG + g, :]
                    pe.matmul(ps_cb[:, 0:P], b_tile, c_tile, start=True, stop=True, skip_group_check=True)
                    pe.transpose(ps_cb[:, P:2 * P], b_tile, ident[:]).then_inc(turned, 1)
                    wait_from(pe, ell_done, n * 8)
                    for q in range(2):
                        pe.matmul(ps_l[:, q, :], ident_b[:], mask[:].rearrange("p a b -> p (a b)"), start=True,
                                  stop=False, skip_group_check=True)
                        for h in range(SHG // 2):
                            head = g * SHG + q * (SHG // 2) + h
                            for part in range(2):
                                mm = pe.matmul(ps_l[:, q, h * P:(h + 1) * P],
                                               da_cur[u][:, part, head:head + 1].to_broadcast([P, P]), tri_r[:],
                                               start=False, stop=(part == 1), skip_group_check=True)
                    mm.then_inc(spread, 1)

                def multiply(c, u, g):
                    n, v = c * 4 + g, g % 2
                    wait_from(pe, state_done, n - 3)
                    wait_from(pe, yo_done, n * 2)
                    pe.matmul(ps_o[:], xbc[:, u, SI // P + SG + g, :], state[:, g], start=True, stop=True
                              ).then_inc(off_done, 1)
                    pe.wait_ge(bt_done, n + 1)
                    pe.wait_ge(pool_step, n * 4 + 2)
                    wait_from(pe, state_done, n)
                    pe.matmul(ps_s[:], bt[:, v], xdd[:, v], start=True, stop=True).then_inc(state_mm, 1)
                    pe.wait_ge(yo_done, n * 2 + 2)
                    wait_from(pe, yg_done, n)
                    for j in range(WT):
                        pe.matmul(ps_y[:, j * P:(j + 1) * P], yo[:, v, j * P:(j + 1) * P], ident[:],
                                  start=(j == 0), stop=False, skip_group_check=True)
                    pe.wait_ge(m_done, n + 1)
                    for h in range(SHG):
                        at = slice(SP_ * (h % 2), SP_ * (h % 2) + SP_)
                        mm = pe.matmul(ps_y[at, (h // 2) * P:(h // 2 + 1) * P], xdt[:, v, h * SP_:(h + 1) * SP_],
                                       mm_[:, v, h, :], start=False, stop=True, skip_group_check=True)
                    mm.then_inc(y_done, 1)

                def squares(n, g):
                    pe.wait_ge(sq_done, n + 1)
                    wait_from(pe, ss_kept, n)
                    for j in range(WT):
                        mm = pe.matmul(ps_q[:, 0:P], ones[:], sq[:, g % 2, j * P:(j + 1) * P],
                                       start=(j == 0), stop=(j == WT - 1))
                    mm.then_inc(ss_done, 1)

                def step(c, u, g):
                    turn(c, u, g)
                    if g > 0:
                        multiply(c, u, g - 1)
                    elif not isinstance(c, int) or c > 0:
                        multiply(c - 1, 1 - u, SG - 1)
                    if g > 1 or not isinstance(c, int) or c > 0:
                        squares(c * 4 + g - 2, (g - 2) % SG)

                pairs(pe, 0, CH, lambda c, u: [step(c, u, g) for g in range(SG)])
                multiply(CH - 1, (CH - 1) % 2, SG - 1)
                squares(LAST - 1, SG - 2)
                squares(LAST, SG - 1)

            @block.scalar
            def _(act):
                act.wait_ge(rows_loaded, 32)
                act.activation(a_row[:], a_row[:], ACT.Exp).then_inc(pre_act, 1)
                act.wait_ge(pre_dve, 5)
                act.activation(dec_out[:], neg_acs[:], ACT.Exp, scale=-1.0).then_inc(pre_act, 1)
                act.activation(dec_state[:], dec_state[:], ACT.Exp).then_inc(pre_act, 1)
                act.activation(dec_chunk[:], ps_cb[:, 0:CH * SH].rearrange("p (c h) -> p c h", h=SH), ACT.Exp
                               ).then_inc(pre_act, 1)

                def step(c, u, g):
                    n, v = c * 4 + g, g % 2
                    first = isinstance(c, int) and c == 0
                    act.wait_ge(turned, n + 1)
                    wait_from(act, pool_step, n * 4 - 4)
                    act.copy(xt[:, v], ps_x[:]).then_inc(xt_done, 1)
                    act.wait_ge(spread, n + 1)
                    wait_from(act, m_done, n)
                    alone(act, act_passed)
                    for h in range(SHG):
                        bias = neg_acs[:, bass.ds(c, 1), g * SHG + h:g * SHG + h + 1].rearrange("p a b -> p (a b)")
                        act.activation(ell[:, h, :], ps_l[:, h // 4, (h % 4) * P:(h % 4 + 1) * P], ACT.Exp, bias=bias
                                       ).then_inc(ell_done, 1)
                    if not first or g > 0:
                        square_of(c, u, g - 1) if g > 0 else square_of(c - 1, 1 - u, SG - 1)
                    if not first or g > 1:
                        keep_sum(c, g - 2) if g > 1 else keep_sum(c - 1, g + 2)

                def square_of(c, u, g):
                    n = c * 4 + g
                    act.wait_ge(yg_done, n + 1)
                    wait_from(act, ss_done, n - 1)
                    alone(act, act_passed)
                    act.activation(sq[:, g % 2].rearrange("p (k t) -> p k t", t=P), token_slice(y_all, g * WT, WT, c),
                                   ACT.Square).then_inc(sq_done, 1)

                def keep_sum(c, g):
                    act.wait_ge(ss_done, c * 4 + g + 1)
                    alone(act, act_passed)
                    act.copy(token_slice(ss_all, g, 1, c).rearrange("p o t -> p (o t)"), ps_q[:, 0:P]).then_inc(ss_kept, 1)

                pairs(act, 0, CH, lambda c, u: [step(c, u, g) for g in range(SG)])
                square_of(CH - 1, (CH - 1) % 2, SG - 1)
                keep_sum(CH - 1, SG - 2)
                keep_sum(CH - 1, SG - 1)
                act.wait_ge(ss_kept, CH * SG)
                act.activation(ss_all[:], ss_all[:], ACT.Sqrt, bias=eps[:], scale=1.0 / W).then_inc(end_act, 1)

            @block.vector
            def _(dve):
                dve.tensor_copy(tri_r[:], tri[:]).then_inc(pre_dve, 1)
                dve.tensor_copy(ident_b[:], ident[:]).then_inc(pre_dve, 1)
                dve.wait_ge(pre_act, 1)
                dve.scalar_tensor_tensor(da[:], dt_all, -1.0, a_row[:].unsqueeze(1).to_broadcast([P, CH, SH]),
                                         ALU.mult, ALU.mult).then_inc(pre_dve, 1)
                dve.wait_ge(pre_pe, 2)
                dve.tensor_scalar(neg_acs[:].rearrange("p c h -> p (c h)"), ps_x[:, 0:CH * SH], -1.0, None, ALU.mult
                                  ).then_inc(pre_dve, 1)
                dve.wait_ge(pre_dve, 4)
                dve.tensor_tensor(dec_state[:].rearrange("p c h -> p (c h)"), ps_cb[:, 0:CH * SH],
                                  neg_acs[:].rearrange("p c h -> p (c h)"), ALU.add).then_inc(pre_dve, 1)
                dve.wait_ge(pre_dve, 5)
                dve.engine_nop().then_inc(pre_dve, 1)
                dve.wait_ge(pre_act, 4)

                def da_hi_lo(c, u):
                    wait_from(dve, spread, c * 4 - 4)
                    src = da[:, bass.ds(c, 1), :].rearrange("p o h -> p (o h)")
                    dve.tensor_copy(da_cur[u][:, 0, :], src).then_inc(cur_ready, 1)
                    dve.wait_ge(cur_ready, c * 2 + 1)
                    dve.tensor_tensor(da_cur[u][:, 1, :], src, da_cur[u][:, 0, :].bitcast(F32), ALU.subtract
                                      ).then_inc(cur_ready, 1)

                def gate(c, u, g):
                    n = c * 4 + g
                    dve.wait_ge(y_done, n + 1)
                    dve.tensor_tensor(token_slice(y_all, g * WT, WT, c), ps_y[:].rearrange("p (k t) -> p k t", t=P),
                                      zc[:, u, g * WT:(g + 1) * WT, :], ALU.mult).then_inc(yg_done, 1)

                def add_up(c, u, g):
                    n, v = c * 4 + g, g % 2
                    dve.wait_ge(off_done, n + 1)
                    wait_from(dve, y_done, n - 1)
                    dve.tensor_tensor(heads(yo[:, v]), heads(ps_o[:]), per_head(dec_out, c, g), ALU.mult
                                      ).then_inc(yo_done, 1)
                    dve.wait_ge(yo_done, n * 2 + 1)
                    dve.wait_ge(pool_step, n * 4 + 4)
                    dve.tensor_tensor(yo[:, v], yo[:, v], x_d[:, v], ALU.add).then_inc(yo_done, 1)
                    dve.wait_ge(state_mm, n + 1)
                    dve.tensor_tensor(state[:, g], state_dec[:], ps_s[:], ALU.add).then_inc(state_done, 1)

                def step(c, u, g):
                    n, v = c * 4 + g, g % 2
                    first = isinstance(c, int) and c == 0
                    if g == 0 and not (isinstance(c, int) and c < 2):
                        da_hi_lo(c, u)
                    dve.wait_ge(turned, n + 1)
                    wait_from(dve, state_mm, n - 1)
                    dve.tensor_copy(bt[:, v], ps_cb[:, P:2 * P]).then_inc(bt_done, 1)
                    if not first or g > 0:
                        add_up(c, u, g - 1) if g > 0 else add_up(c - 1, 1 - u, SG - 1)
                    dve.wait_ge(ell_done, n * 8 + 8)
                    wait_from(dve, y_done, n - 1)
                    dve.tensor_tensor(mm_[:, v], ell[:], ps_cb[:, 0:P].unsqueeze(1).to_broadcast([P, SHG, P]),
                                      ALU.mult).then_inc(m_done, 1)
                    if not first or g > 0:
                        gate(c, u, g - 1) if g > 0 else gate(c - 1, 1 - u, SG - 1)

                da_hi_lo(0, 0)
                da_hi_lo(1, 1)
                pairs(dve, 0, CH, lambda c, u: [step(c, u, g) for g in range(SG)])
                add_up(CH - 1, (CH - 1) % 2, SG - 1)
                gate(CH - 1, (CH - 1) % 2, SG - 1)
                dve.wait_ge(end_act, 1)
                dve.reciprocal(ss_all[:], ss_all[:]).then_inc(end_dve, 1)
                dve.wait_ge(end_dve, 1)
                for k in range(SI // P):
                    w = VEC["ssd_norm_w"] + k
                    dve.scalar_tensor_tensor(y_all[:, k, :], y_all[:, k, :], cols[:, w:w + 1], ss_all[:, k // WT, :],
                                             ALU.mult, ALU.mult).then_inc(end_dve, 1)


def merge(m, inp, keep, scratch):
    nc = m.nc
    YK = KD + SI // P
    KINDS = YK // KD
    with ExitStack() as st:
        y_raw = m.sb(st, "y_raw", [P, 2, TH])
        y_hi = m.sb(st, "y_hi", [P, YK, TH], F32R)
        y_lo = m.sb(st, "y_lo", [P, YK, TH], F32R)
        w_raw = m.sb(st, "wo_raw", [P, 2, KD, P])
        w_hi = m.sb(st, "wo_hi", [P, 2, KD, P], F32R)
        w_lo = m.sb(st, "wo_lo", [P, 2, KD, P], F32R)
        gates = m.sb(st, "gates_sb", [P, 2, 2, TH])
        part = m.sb(st, "merge_part", [P, 2, TH])
        res = m.sb(st, "merged_sb", [P, 2, TH])
        ps = [[m.ps(st, f"p3_{u}{g}", [P, TH]) for g in range(2)] for u in range(2)]

        y_loaded = [m.sem(f"y_loaded{i}") for i in range(2)]
        w_loaded = [m.sem(f"wo_loaded{i}") for i in range(2)]
        g_loaded = [m.sem(f"gates_loaded{i}") for i in range(2)]
        y_hi_done, y_lo_done = m.sem("y_hi_done"), m.sem("y_lo_done")
        hi_done, lo_done, mm_done = m.sem("wo_hi_done"), m.sem("wo_lo_done"), m.sem("merge_mm")
        part_done, merged = m.sem("merge_parts"), m.sem("merge_sum")
        stored = [m.sem(f"merged_stored{i}") for i in range(2)]
        pool_passed = keep["pool_passed"]

        def tiles(eng, half, body):
            if half == 0:
                for n in range(2):
                    body(n, n, half)
            with eng.Fori(0 if half else 1, KD // 2) as p:
                for u in range(2):
                    body(p * 2 + u, u, half)

        with nc.Block() as block:
            @block.sync
            def _(sp):
                def load(n, u, half):
                    tile = n + half * KD
                    for kind in range(KINDS):
                        b, ub = tile * KINDS + kind, (u + kind) % 2
                        src = inp["w_lru_out"][0] if kind == 0 else inp["w_ssd_out"][0, (kind - 1) * D:kind * D, :]
                        wait_from(sp, lo_done, b - 1)
                        sp.dma_start(w_raw[:, ub], src[:, bass.ds(n * P, P)].rearrange("(k p) n -> p k n", p=P)
                                     ).then_inc(w_loaded[ub], 16)
                    wait_from(sp, merged, tile - 1)
                    for g in range(2):
                        sp.dma_start(gates[:, u, g], scratch["gates"][bass.ds(n * P + g * D, P), half * TH:(half + 1) * TH]
                                     ).then_inc(g_loaded[u], 16)

                for half in range(2):
                    for k in range(YK):
                        n = half * YK + k
                        wait_from(sp, y_lo_done, n - 1)
                        src = scratch["y_lru"] if k < KD else scratch["y_ssd"]
                        row = (k if k < KD else k - KD) * P
                        sp.dma_start(y_raw[:, k % 2], src[row:row + P, half * TH:(half + 1) * TH]
                                     ).then_inc(y_loaded[k % 2], 16)
                    tiles(sp, half, load)

            @block.gpsimd
            def _(pool):
                def cut(n, u, half):
                    tile = n + half * KD
                    for kind in range(KINDS):
                        b, ub = tile * KINDS + kind, (u + kind) % 2
                        pool.wait_ge(w_loaded[ub], of_buffer(b, ub) + 16)
                        wait_from(pool, mm_done, b - 1)
                        alone(pool, pool_passed)
                        pool.tensor_copy(w_hi[:, ub], w_raw[:, ub]).then_inc(hi_done, 1)
                        pool.wait_ge(hi_done, b + 1)
                        pool.tensor_tensor(w_lo[:, ub], w_raw[:, ub], w_hi[:, ub].bitcast(F32), ALU.subtract
                                           ).then_inc(lo_done, 1)

                for half in range(2):
                    tiles(pool, half, cut)

            @block.scalar
            def _(act):
                def store(n, u, half):
                    act.wait_ge(merged, n + half * KD + 1)
                    act.dma_start(scratch["merged"][bass.ds(n * P, P), half * TH:(half + 1) * TH], res[:, u]
                                  ).then_inc(stored[u], 16)

                for half in range(2):
                    for k in range(YK):
                        n = half * YK + k
                        act.wait_ge(y_loaded[k % 2], 16 * (n // 2 + 1))
                        if half:
                            act.wait_ge(mm_done, KD * KINDS)
                        act.copy(y_hi[:, k, :], y_raw[:, k % 2]).then_inc(y_hi_done, 1)
                    tiles(act, half, store)
                for u in range(2):
                    act.wait_ge(stored[u], 16 * KD)

            @block.vector
            def _(dve):
                def combine(n, u, half):
                    tile = n + half * KD
                    dve.wait_ge(g_loaded[u], of_buffer(tile, u) * 2 + 32)
                    wait_from(dve, merged, tile)
                    for g in range(2):
                        dve.wait_ge(mm_done, tile * KINDS + (1 if g == 0 else KINDS))
                        dve.tensor_tensor(part[:, g], ps[u][g][:], gates[:, u, g], ALU.mult).then_inc(part_done, 1)
                    dve.wait_ge(part_done, tile * 2 + 2)
                    wait_from(dve, stored[u], of_buffer(tile, u))
                    dve.tensor_tensor(res[:, u], part[:, 0], part[:, 1], ALU.add).then_inc(merged, 1)

                for half in range(2):
                    for k in range(YK):
                        n = half * YK + k
                        dve.wait_ge(y_hi_done, n + 1)
                        dve.tensor_tensor(y_lo[:, k, :], y_raw[:, k % 2], y_hi[:, k, :].bitcast(F32), ALU.subtract
                                          ).then_inc(y_lo_done, 1)
                    tiles(dve, half, combine)

            @block.tensor
            def _(pe):
                def tile(n, u, half):
                    t = n + half * KD
                    for kind in range(KINDS):
                        b, ub = t * KINDS + kind, (u + kind) % 2
                        pe.wait_ge(lo_done, b + 1)
                        bank = ps[u][min(kind, 1)]
                        if kind < 2:
                            wait_from(pe, part_done, (t - 2) * 2 + kind + 1)
                        j = 0
                        for k in range(KD):
                            for w, y in ((w_hi, y_hi), (w_hi, y_lo), (w_lo, y_hi)):
                                mm = pe.matmul(bank[:], w[:, ub, k, :], y[:, kind * KD + k, :],
                                               start=(j == 0 and kind < 2), stop=(j == 3 * KD - 1 and kind != 1))
                                j += 1
                        mm.then_inc(mm_done, 1)

                for half in range(2):
                    pe.wait_ge(y_lo_done, (half + 1) * YK)
                    tiles(pe, half, tile)


def post_mix(m, inp, keep, scratch):
    nc = m.nc
    ident, mod, gate_rows = keep["ident"], keep["mod"], keep["gate_rows"]
    DH = D // 2
    with ExitStack() as st:
        raw = m.sb(st, "pm_raw", [P, 2, T])
        mg = [m.sb(st, f"merged_{n}", [P, KD, T], F32R) for n in ("hi", "lo")]
        wo = [m.sb(st, f"w_o_{n}", [P, KD, D], F32R) for n in ("hi", "lo")]
        x_in = m.sb(st, "x_res", [P, 2, D])
        junk = m.sb(st, "pm_square", [P, D])
        x1 = m.sb(st, "x1_sb", [P, 2, D])
        xn = m.sb(st, "x1_normed", [P, D])
        h2 = m.sb(st, "h2_sb", [P, 2, KD, P])
        stat = m.sb(st, "pm_stat", [P, TB, 2, 3])
        eps = m.sb(st, "eps3", [P, 1])
        ps_o = [m.ps(st, f"p3b_o{i}", [P, 2, DH]) for i in range(2)]
        ps_t = m.ps(st, "p3b_t", [P, 2, 4, P])

        loaded = [m.sem(f"pm_loaded{i}") for i in range(2)]
        hi_done, lo_done = m.sem("pm_hi_done"), m.sem("pm_lo_done")
        x_loaded = [m.sem(f"x_res_loaded{i}") for i in range(2)]
        eps_set, mm_done, ssq_done, std_done = m.sem("eps3_set"), m.sem("w_o_done"), m.sem("pm_ssq"), m.sem("pm_std")
        rec_done, part_done, x1_done, xn_done = m.sem("pm_rstd"), m.sem("pm_part"), m.sem("x1_done"), m.sem("x1_normed_s")
        turned, h2_done = m.sem("x1_turned"), m.sem("h2_done")
        stored = [m.sem(f"pm_stored{i}") for i in range(2)]
        h_stored = [m.sem(f"h2_stored{i}") for i in range(2)]

        def slices():
            for n in range(2 * KD):
                which, k = n % 2, n // 2
                yield n, which, k

        with nc.Block() as block:
            @block.sync
            def _(sp):
                for n, which, k in slices():
                    if n >= 2:
                        sp.wait_ge(lo_done, n - 1)
                    src = scratch["merged"] if which == 0 else inp["w_o"][0]
                    sp.dma_start(raw[:, which], src[k * P:(k + 1) * P, :]).then_inc(loaded[which], 16)
                def load_x(t):
                    sp.dma_start(x_in[:, t % 2], inp["x"][0, t * P:(t + 1) * P, :]).then_inc(x_loaded[t % 2], 16)

                load_x(0)
                load_x(1)
                for t in range(TB):
                    sp.wait_ge(x1_done, t + 1)
                    sp.dma_start(scratch["x1"][t * P:(t + 1) * P, :], x1[:, t % 2]).then_inc(stored[t % 2], 16)
                    if t + 2 < TB:
                        load_x(t + 2)
                    sp.wait_ge(h2_done, KD * (t + 1))
                    sp.dma_start(scratch["h2"].rearrange("(k p) t -> p k t", p=P)[:, :, t * P:(t + 1) * P],
                                 h2[:, t % 2]).then_inc(h_stored[t % 2], 16)
                for u in range(2):
                    sp.wait_ge(stored[u], 8 * TB)
                    sp.wait_ge(h_stored[u], 8 * TB)

            @block.gpsimd
            def _(pool):
                pool.memset(eps[:], EPS).then_inc(eps_set, 1)
                for t in range(TB):
                    pool.wait_ge(x_loaded[t % 2], 16 * (t // 2 + 1))
                    pool.wait_ge(part_done, t + 1)
                    pool.tensor_tensor(x1[:, t % 2], x1[:, t % 2], x_in[:, t % 2], ALU.add).then_inc(x1_done, 1)

            @block.scalar
            def _(act):
                act.wait_ge(eps_set, 1)
                for n, which, k in slices():
                    act.wait_ge(loaded[which], 16 * (k + 1))
                    act.copy((mg, wo)[which][0][:, k, :], raw[:, which]).then_inc(hi_done, 1)
                for t in range(TB):
                    for which in range(2):
                        s = 2 * t + which
                        if which == 0:
                            act.wait_ge(mm_done, t + 1)
                            src = ps_o[t % 2][:].rearrange("p a b -> p (a b)")
                        else:
                            act.wait_ge(x1_done, t + 1)
                            src = x1[:, t % 2]
                        act.activation(junk[:], src, ACT.Square, accum_out=stat[:, t, which, 0:1]).then_inc(ssq_done, 1)
                        act.wait_ge(ssq_done, s + 1)
                        act.activation(stat[:, t, which, 1:2], stat[:, t, which, 0:1], ACT.Sqrt, bias=eps[:],
                                       scale=1.0 / D).then_inc(std_done, 1)
                    act.wait_ge(turned, t + 1)
                    if t >= 2:
                        act.wait_ge(h_stored[t % 2], 16 * (t // 2))
                    for k in range(KD):
                        act.activation(h2[:, t % 2, k, :], ps_t[:, k // 4, k % 4, :], ACT.Identity,
                                       bias=mod[:, 2, k:k + 1], scale=mod[:, 3, k:k + 1]).then_inc(h2_done, 1)

            @block.vector
            def _(dve):
                for n, which, k in slices():
                    dve.wait_ge(hi_done, n + 1)
                    hi, lo = (mg, wo)[which]
                    dve.tensor_tensor(lo[:, k, :], raw[:, which], hi[:, k, :].bitcast(F32), ALU.subtract
                                      ).then_inc(lo_done, 1)
                for t in range(TB):
                    for which in range(2):
                        dve.wait_ge(std_done, 2 * t + which + 1)
                        dve.reciprocal(stat[:, t, which, 2:3], stat[:, t, which, 1:2]).then_inc(rec_done, 1)
                        dve.wait_ge(rec_done, 2 * t + which + 1)
                        if which == 0:
                            if t >= 2:
                                dve.wait_ge(stored[t % 2], 16 * (t // 2))
                            dve.scalar_tensor_tensor(x1[:, t % 2], ps_o[t % 2][:].rearrange("p a b -> p (a b)"),
                                                     stat[:, t, 0, 2:3], gate_rows[:, 0, :], ALU.mult, ALU.mult
                                                     ).then_inc(part_done, 1)
                        else:
                            if t >= 1:
                                dve.wait_ge(turned, t)
                            dve.tensor_scalar(xn[:], x1[:, t % 2], stat[:, t, 1, 2:3], None, ALU.mult).then_inc(xn_done, 1)

            @block.tensor
            def _(pe):
                def turn(t):
                    pe.wait_ge(xn_done, t + 1)
                    if t >= 1:
                        pe.wait_ge(h2_done, KD * t)
                    for k in range(KD):
                        mm = pe.transpose(ps_t[:, k // 4, k % 4, :], xn[:, k * P:(k + 1) * P], ident[:])
                    mm.then_inc(turned, 1)

                pe.wait_ge(lo_done, 2 * KD)
                for t in range(TB):
                    if t >= 2:
                        pe.wait_ge(part_done, t - 1)
                    for half in range(2):
                        n = 0
                        for k in range(KD):
                            for a, b in ((0, 0), (0, 1), (1, 0)):
                                mm = pe.matmul(ps_o[t % 2][:, half, :], mg[a][:, k, t * P:(t + 1) * P],
                                               wo[b][:, k, half * DH:(half + 1) * DH],
                                               start=(n == 0), stop=(n == 3 * KD - 1))
                                n += 1
                    mm.then_inc(mm_done, 1)
                    if t >= 1:
                        turn(t - 1)
                turn(TB - 1)


PH, PK, TOPK = 8, 128, 16
HP = 2 * PH
SEL_STEPS = 17


def selection(m, st, tag):
    b = {}
    for name, shape, dt in (("cand", [P, TOPK, TOPK], F32), ("cand_rest", [P, TOPK, TOPK], F32),
                            ("cv", [P, TOPK], F32), ("ci", [P, TOPK], U32), ("ij", [P, 2, TOPK], U32),
                            ("ij_f", [P, 2, TOPK], F32), ("neg_max", [P, 1], F32),
                            ("exp", [P, TOPK], F32), ("exp_sum", [P, 1], F32), ("inv", [P, 1], F32)):
        b[name] = m.sb(st, f"{tag}_{name}", shape, dt)
    b["hit"] = b["cand"]
    return b


def select_dve(dve, b, step, exp_done, keep, n, tb, h, out):
    sv, si, iota = keep["key_scores"], keep["key_index"], keep["iota_row"]
    base = n * SEL_STEPS

    def pick(ap, p):
        return ap[:, bass.ds(tb, 1), bass.ds(h * 2 + p, 1), :].rearrange("p a b k -> p (a b k)")

    def after(k):
        dve.wait_ge(step, base + k)

    flat = lambda ap: ap[:].rearrange("p a b -> p (a b)")
    wait_from(dve, step, base)
    dve.tensor_tensor(b["cand"][:], pick(sv, 0).unsqueeze(2).to_broadcast([P, TOPK, TOPK]),
                      pick(sv, 1).unsqueeze(1).to_broadcast([P, TOPK, TOPK]), ALU.add).then_inc(step, 1)
    after(1)
    alone(dve, keep["dve_passed"])
    dve.max(b["cv"][:, 0:8], flat(b["cand"])).then_inc(step, 1)
    after(2)
    alone(dve, keep["dve_passed"])
    dve.max_index(b["ci"][:, 0:8], b["cv"][:, 0:8], flat(b["cand"])).then_inc(step, 1)
    dve.match_replace(flat(b["cand_rest"]), b["cv"][:, 0:8], flat(b["cand"]), -3.0e38).then_inc(step, 1)
    dve.tensor_scalar(b["neg_max"][:], b["cv"][:, 0:1], -1.0, None, ALU.mult).then_inc(step, 1)
    after(5)
    alone(dve, keep["dve_passed"])
    dve.max(b["cv"][:, 8:16], flat(b["cand_rest"])).then_inc(step, 1)
    after(6)
    alone(dve, keep["dve_passed"])
    dve.max_index(b["ci"][:, 8:16], b["cv"][:, 8:16], flat(b["cand_rest"])).then_inc(step, 1)
    after(7)
    dve.tensor_scalar(b["ij"][:, 0], b["ci"][:], 4, None, ALU.logical_shift_right).then_inc(step, 1)
    dve.tensor_scalar(b["ij"][:, 1], b["ci"][:], TOPK - 1, None, ALU.bitwise_and).then_inc(step, 1)
    after(9)
    dve.tensor_copy(b["ij_f"][:], b["ij"][:]).then_inc(step, 1)
    for p in range(2):
        after(10 + 3 * p)
        dve.tensor_tensor(b["hit"][:], b["ij_f"][:, p].unsqueeze(2).to_broadcast([P, TOPK, TOPK]),
                          iota[:, 0:TOPK].unsqueeze(1).to_broadcast([P, TOPK, TOPK]), ALU.is_equal).then_inc(step, 1)
        after(11 + 3 * p)
        dve.tensor_tensor(b["hit"][:], b["hit"][:], pick(si, p).unsqueeze(1).to_broadcast([P, TOPK, TOPK]),
                          ALU.mult).then_inc(step, 1)
        after(12 + 3 * p)
        dve.reduce_sum(out(1 + p), b["hit"][:], axis=AX.X).then_inc(step, 1)
    dve.wait_ge(exp_done, n + 1)
    dve.reciprocal(b["inv"][:], b["exp_sum"][:]).then_inc(step, 1)
    after(17)
    dve.tensor_scalar(out(0), b["exp"][:], b["inv"][:], None, ALU.mult).then_inc(keep["sel_done"], 1)


def select_act(act, b, step, exp_done, n):
    act.wait_ge(step, n * SEL_STEPS + 6)
    act.activation(b["exp"][:], b["cv"][:], ACT.Exp, bias=b["neg_max"][:], accum_out=b["exp_sum"][:]
                   ).then_inc(exp_done, 1)


def expert_keep(m, stack, keep):
    keep["iota_row"] = m.sb(stack, "iota_row", [P, P])
    keep["key_scores"] = m.sb(stack, "key_scores", [P, TB, HP, TOPK])
    keep["key_index"] = m.sb(stack, "key_index", [P, TB, HP, TOPK])
    keep["chosen"] = m.sb(stack, "chosen", [P, 3, P])
    keep["h2T"] = [m.sb(stack, "h2T_hi", [P, KD, T], F32R), m.sb(stack, "h2T_lo", [P, KD, T], F32R)]
    keep["dve_passed"] = m.kept_sem("dve_passed")
    keep["sel_done"] = m.kept_sem("sel_done")


def queries(m, inp, keep, scratch):
    nc = m.nc
    ident, h2 = keep["ident"], keep["h2T"]
    sv, si = keep["key_scores"], keep["key_index"]
    pool_passed = keep["pool_passed"]
    KEY_STEPS = 5 * TB + 2
    with ExitStack() as st:
        h_raw = m.sb(st, "h2_raw", [P, 2, T])
        iota_i = m.sb(st, "iota_i", [P, P], mybir.dt.int32)
        iota_set = m.sem("iota_set")
        keys = m.sb(st, "sub_keys", [P, HP, P])
        key_hi = m.sb(st, "keys_hi", [P, HP, P], F32R)
        key_lo = m.sb(st, "keys_lo", [P, HP, P], F32R)
        w_raw = m.sb(st, "wq_raw", [P, 2, KD, P])
        w_hi = m.sb(st, "wq_hi", [P, 2, KD, P], F32R)
        w_lo = m.sb(st, "wq_lo", [P, 2, KD, P], F32R)
        q_hi = m.sb(st, "q_hi", [P, T], F32R)
        q_lo = m.sb(st, "q_lo", [P, T], F32R)
        score = m.sb(st, "scores", [P, 2, TB, PK])
        rest = m.sb(st, "scores_rest", [P, TB, PK])
        top = m.sb(st, "key_top", [P, TB, TOPK])
        idx = m.sb(st, "key_idx", [P, TB, TOPK], U32)
        ps_q = m.ps(st, "p4_q", [P, 2, TH])
        ps_q2 = m.ps(st, "p4_q2", [P, 2, TH])
        ps_s = m.ps(st, "p4_s", [P, TB, PK])
        ps_k = m.ps(st, "p4_k", [P, 2, 4, P])
        ps_qs = (ps_q, ps_q2)
        sel = selection(m, st, "query_sel")

        h_loaded = [m.sem(f"h2_loaded{i}") for i in range(2)]
        h_hi, h_lo = m.sem("h2_hi_done"), m.sem("h2_lo_done")
        keys_loaded, keys_turned, keys_cut = m.sem("keys_loaded"), m.sem("keys_turned"), m.sem("keys_cut")
        w_loaded = [m.sem(f"wq_loaded{i}") for i in range(2)]
        hi_done, lo_done = m.sem("wq_hi_done"), m.sem("wq_lo_done")
        q_mm, q_hi_done, q_lo_done = m.sem("q_mm"), m.sem("q_hi_done"), m.sem("q_lo_done")
        s_mm, s_kept, key_step = m.sem("score_mm"), m.sem("scores_kept"), m.sem("key_step")
        step, exp_done = m.sem("q_sel_step"), m.sem("q_sel_exp")

        with nc.Block() as block:
            @block.sync
            def _(sp):
                sp.dma_start(keys[:], inp["peer_sub_keys"][0].rearrange("h p k d -> k (h p) d")).then_inc(keys_loaded, 16)
                for k in range(KD):
                    if k >= 2:
                        sp.wait_ge(h_lo, k - 1)
                    sp.dma_start(h_raw[:, k % 2], scratch["h2"][k * P:(k + 1) * P, :]).then_inc(h_loaded[k % 2], 16)

                def load(n, u):
                    wait_from(sp, lo_done, n - 1)
                    sp.dma_start(w_raw[:, u], inp["peer_wq"][0, :, bass.ds(n * P, P)].rearrange("(k p) n -> p k n", p=P)
                                 ).then_inc(w_loaded[u], 16)

                pairs(sp, 0, HP, load)

            @block.gpsimd
            def _(pool):
                pool.iota(iota_i[:], pattern=[[1, P]], base=0, channel_multiplier=0).then_inc(iota_set, 1)
                pool.wait_ge(iota_set, 1)
                pool.tensor_copy(keep["iota_row"][:], iota_i[:]).then_inc(iota_set, 1)

                def cut(n, u):
                    pool.wait_ge(w_loaded[u], of_buffer(n, u) + 16)
                    wait_from(pool, q_mm, n - 1)
                    alone(pool, pool_passed)
                    pool.tensor_copy(w_hi[:, u], w_raw[:, u]).then_inc(hi_done, 1)
                    pool.wait_ge(hi_done, n + 1)
                    pool.tensor_tensor(w_lo[:, u], w_raw[:, u], w_hi[:, u].bitcast(F32), ALU.subtract).then_inc(lo_done, 1)

                pairs(pool, 0, HP, cut)

            @block.tensor
            def _(pe):
                pe.wait_ge(keys_loaded, 16)
                for r in range(2):
                    if r:
                        pe.wait_ge(keys_cut, 2)
                    for j in range(HP // 2):
                        mm = pe.transpose(ps_k[:, j // 4, j % 4, :], keys[:, r * (HP // 2) + j, :], ident[:])
                    mm.then_inc(keys_turned, 1)
                pe.wait_ge(h_lo, KD)
                pe.wait_ge(keys_cut, 4)

                def query(n, u):
                    pe.wait_ge(lo_done, n + 1)
                    wait_from(pe, q_lo_done, n - 1)
                    for half in range(2):
                        j = 0
                        for k in range(KD):
                            for w, h in ((w_hi, 0), (w_hi, 1), (w_lo, 0)):
                                mm = pe.matmul(ps_qs[u][:, half, :], w[:, u, k, :], h2[h][:, k, half * TH:(half + 1) * TH],
                                               start=(j == 0), stop=(j == 3 * KD - 1))
                                j += 1
                    mm.then_inc(q_mm, 1)

                def scores(n):
                    pe.wait_ge(q_lo_done, n + 1)
                    wait_from(pe, s_kept, n)
                    for t in range(TB):
                        for j, (q, k) in enumerate(((q_hi, key_hi), (q_hi, key_lo), (q_lo, key_hi))):
                            mm = pe.matmul(ps_s[:, t, :], q[:, t * P:(t + 1) * P],
                                           k[:, bass.ds(n, 1), :].rearrange("p o k -> p (o k)"),
                                           start=(j == 0 and t % 4 == 0), stop=(j == 2), skip_group_check=True)
                    mm.then_inc(s_mm, 1)

                def tile(n, u):
                    query(n, u)
                    if not isinstance(n, int) or n > 0:
                        scores(n - 1)

                pairs(pe, 0, HP, tile)
                scores(HP - 1)

            @block.scalar
            def _(act):
                for k in range(KD):
                    act.wait_ge(h_loaded[k % 2], 16 * (k // 2 + 1))
                    act.copy(h2[0][:, k, :], h_raw[:, k % 2]).then_inc(h_hi, 1)
                for r in range(2):
                    act.wait_ge(keys_turned, r + 1)
                    act.copy(key_hi[:, r * 8:r * 8 + 8, :], ps_k[:].rearrange("p a b c -> p (a b) c")).then_inc(keys_cut, 1)
                    act.wait_ge(keys_cut, 2 * r + 2)

                def keep_scores(n, u):
                    act.wait_ge(s_mm, n + 1)
                    wait_from(act, key_step, (n - 1) * KEY_STEPS)
                    act.copy(score[:, u], ps_s[:]).then_inc(s_kept, 1)

                def tile(n, u):
                    act.wait_ge(q_mm, n + 1)
                    wait_from(act, s_mm, n)
                    act.copy(q_hi[:], ps_qs[u][:].rearrange("p a b -> p (a b)")).then_inc(q_hi_done, 1)
                    if not isinstance(n, int) or n > 0:
                        keep_scores(n - 1, 1 - u)

                tile(0, 0)
                tile(1, 1)
                with act.Fori(1, PH) as h:
                    tile(h * 2, 0)
                    select_act(act, sel, step, exp_done, h - 1)
                    tile(h * 2 + 1, 1)
                keep_scores(HP - 1, 1)
                select_act(act, sel, step, exp_done, PH - 1)

            @block.vector
            def _(dve):
                for k in range(KD):
                    dve.wait_ge(h_hi, k + 1)
                    dve.tensor_tensor(h2[1][:, k, :], h_raw[:, k % 2], h2[0][:, k, :].bitcast(F32), ALU.subtract
                                      ).then_inc(h_lo, 1)
                for r in range(2):
                    dve.wait_ge(keys_cut, 2 * r + 1)
                    part = slice(r * 8, r * 8 + 8)
                    dve.tensor_tensor(key_lo[:, part, :], ps_k[:].rearrange("p a b c -> p (a b) c"),
                                      key_hi[:, part, :].bitcast(F32), ALU.subtract).then_inc(keys_cut, 1)
                dve.wait_ge(iota_set, 2)

                def q_low(n, u):
                    dve.wait_ge(q_hi_done, n + 1)
                    dve.tensor_tensor(q_lo[:], ps_qs[u][:].rearrange("p a b -> p (a b)"), q_hi[:].bitcast(F32),
                                      ALU.subtract).then_inc(q_lo_done, 1)

                def top_keys(n, u):
                    base = n * KEY_STEPS
                    dve.wait_ge(s_kept, n + 1)
                    wait_from(dve, key_step, base)
                    alone(dve, keep["dve_passed"])
                    at = lambda ap, t, lo: ap[:, t, lo:lo + 8]
                    for t in range(TB):
                        dve.max(at(top, t, 0), score[:, u, t, :]).then_inc(key_step, 1)
                    dve.wait_ge(key_step, base + TB)
                    alone(dve, keep["dve_passed"])
                    for t in range(TB):
                        dve.max_index(idx[:, t, 0:8], at(top, t, 0), score[:, u, t, :]).then_inc(key_step, 1)
                        dve.match_replace(rest[:, t, :], at(top, t, 0), score[:, u, t, :], -3.0e38).then_inc(key_step, 1)
                    dve.wait_ge(key_step, base + 3 * TB)
                    alone(dve, keep["dve_passed"])
                    for t in range(TB):
                        dve.max(at(top, t, 8), rest[:, t, :]).then_inc(key_step, 1)
                    dve.wait_ge(key_step, base + 4 * TB)
                    alone(dve, keep["dve_passed"])
                    for t in range(TB):
                        dve.max_index(idx[:, t, 8:16], at(top, t, 8), rest[:, t, :]).then_inc(key_step, 1)
                    dve.wait_ge(key_step, base + 5 * TB)
                    for dst, src in ((sv, top), (si, idx)):
                        dve.tensor_copy(dst[:, :, bass.ds(n, 1), :].rearrange("p t o k -> p t (o k)"), src[:]
                                        ).then_inc(key_step, 1)

                def choose(h):
                    dve.wait_ge(key_step, (h + 1) * (2 * KEY_STEPS))
                    select_dve(dve, sel, step, exp_done, keep, h, 0, h,
                               lambda which: keep["chosen"][:, which, bass.ds(h * TOPK, TOPK)])

                def tile(n, u):
                    q_low(n, u)
                    if not isinstance(n, int) or n > 0:
                        top_keys(n - 1, 1 - u)

                tile(0, 0)
                tile(1, 1)
                with dve.Fori(1, PH) as h:
                    tile(h * 2, 0)
                    choose(h - 1)
                    tile(h * 2 + 1, 1)
                top_keys(HP - 1, 1)
                choose(PH - 1)


QB = 4
STEP_TOKENS = 16
STEPS = P // STEP_TOKENS
WT = 64
E1 = 128


def experts_down(m, inp, keep, scratch):
    nc = m.nc
    ident, h2, chosen, iota = keep["ident"], keep["h2T"], keep["chosen"], keep["iota_row"]
    sel_done = keep["sel_done"]
    with ExitStack() as st:
        raw = m.sb(st, "down_raw", [P, 2, D])
        d_hi = m.sb(st, "downT_hi", [P, 2, KD, P], F32R)
        d_lo = m.sb(st, "downT_lo", [P, 2, KD, P], F32R)
        gu = m.sb(st, "gelu_out", [P, 2, T])
        hit1 = m.sb(st, "hit_first", [P, 2, QB, P])
        a_hi = m.sb(st, "first_hi", [P, 2, QB, P], F32R)
        a_lo = m.sb(st, "first_lo", [P, 2, QB, P], F32R)
        b_ = m.sb(st, "hit_second", [P, 2, QB, P], F32R)
        wt = m.sb(st, "weights_out", [P, 2, E1, WT])
        pick_g_hi = m.sb(st, "pick_weight_hi", [P, P], F32R)
        pick_g_lo = m.sb(st, "pick_weight_lo", [P, P], F32R)
        pick_1, pick_2 = m.sb(st, "pick_first", [P, P]), m.sb(st, "pick_second", [P, P])
        sel = selection(m, st, "down_sel")
        ps_d = m.ps(st, "p5_down", [P, KD, P])
        ps_u = [m.ps(st, f"p5_u{i}", [P, TH]) for i in range(2)]
        ps_w = [m.ps(st, f"p5_w{i}", [P, QB, P]) for i in range(4)]

        loaded = [m.sem(f"down_loaded{i}") for i in range(2)]
        turned = [m.sem(f"down_turned{i}") for i in range(2)]
        hi_done, lo_done = m.sem("down_hi_done"), m.sem("down_lo_done")
        u_done = [m.sem(f"u_done{i}") for i in range(2)]
        gelu_done = [m.sem(f"gelu_done{i}") for i in range(2)]
        gu_stored = [m.sem(f"gelu_stored{i}") for i in range(2)]
        picks_turned, picks_ready = m.sem("picks_turned"), m.sem("picks_ready")
        hit1_ready, b_ready = m.sem("hit_first_ready"), m.sem("hit_second_ready")
        a_hi_ready, a_lo_ready = m.sem("first_hi_ready"), m.sem("first_lo_ready")
        w_mm = [m.sem(f"weights_mm{i}") for i in range(2)]
        w_kept = [m.sem(f"weights_kept{i}") for i in range(4)]
        w_stored = [m.sem(f"weights_stored{i}") for i in range(2)]
        step, exp_done = m.sem("d_sel_step"), m.sem("d_sel_exp")
        pe_passed = m.sem("pe_passed")
        down = inp["peer_down"][0].rearrange("(e p) d -> e p d", p=P)
        PIECES = 8
        PE1 = E1 // PIECES

        def blocks(eng, block):
            with eng.Fori(0, TB - 1) as o:
                block(o, False)
            block(TB - 1, True)

        def steps(eng, o, step_of):
            for hh in range(2):
                with eng.Fori(0, STEPS // 2) as r:
                    step_of(hh, r, o * STEPS + hh * (STEPS // 2) + r)

        with nc.Block() as block:
            @block.sync
            def _(sp):
                def store_piece(tile, hh, piece):
                    sp.dma_start(scratch["w"][bass.ds(tile, 1), :, bass.ds(piece * PE1, PE1), :].rearrange("o p e t -> (o p) e t"),
                                 wt[:, hh, bass.ds(piece * PE1, PE1), :]).then_inc(w_stored[hh], 16)

                def halves(o, first):
                    for hh in range(2):
                        with sp.Fori(0, STEPS // 2) as r:
                            s = o * STEPS + hh * (STEPS // 2) + r
                            for u in range(2):
                                sp.wait_ge(turned[u], s)
                                sp.dma_start(raw[:, u], down[bass.ds(s * 2 + u, 1)].rearrange("o p d -> (o p) d")
                                             ).then_inc(loaded[u], 16)
                            if not (first and hh == 0):
                                for b in range(4):
                                    sp.wait_ge(w_kept[b], (o * 2 + hh) * (STEPS // 2))
                                for u in range(2):
                                    store_piece(o * 2 + hh - 1, 1 - hh, r * 2 + u)

                halves(0, True)
                with sp.Fori(1, TB) as o:
                    halves(o, False)
                for b in range(4):
                    sp.wait_ge(w_kept[b], TB * STEPS)
                for piece in range(PIECES):
                    store_piece(2 * TB - 1, 1, piece)
                for hh in range(2):
                    sp.wait_ge(w_stored[hh], 16 * PIECES * TB)
                    sp.wait_ge(gu_stored[hh], 16 * E1 // 2)

            @block.gpsimd
            def _(pool):
                def first_low(hh, r, s):
                    for b in range(4):
                        pool.wait_ge(w_mm[b % 2], s * 2 + b // 2)
                        pool.wait_ge(hit1_ready, s * 4 + (b + 1))
                        alone(pool, keep["pool_passed"])
                        at = bass.ds(r * STEP_TOKENS + (hh * WT + b * QB), QB)
                        pool.tensor_tensor(a_lo[:, b % 2], hit1[:, b % 2],
                                           pick_g_lo[:, at].unsqueeze(2).to_broadcast([P, QB, P]).bitcast(F32), ALU.mult
                                           ).then_inc(a_lo_ready, 1)

                def of_block(o, last):
                    pool.wait_ge(picks_ready, o * 4 + 4)
                    alone(pool, keep["pool_passed"])
                    steps(pool, o, first_low)

                blocks(pool, of_block)

            @block.tensor
            def _(pe):
                def turn(s, u):
                    pe.wait_ge(loaded[u], s * 16 + 16)
                    pe.wait_ge(lo_done, s * 2 + u)
                    for k in range(KD):
                        mm = pe.transpose(ps_d[:, k, :], raw[:, u, k * P:(k + 1) * P], ident[:])
                    mm.then_inc(turned[u], 1)

                def products(s, u, half):
                    pe.wait_ge(lo_done, s * 2 + (u + 1))
                    pe.wait_ge(gelu_done[half], s * 2 + u)
                    n = 0
                    for k in range(KD):
                        for d, h in ((d_hi, 0), (d_hi, 1), (d_lo, 0)):
                            mm = pe.matmul(ps_u[half][:], d[:, u, k, :], h2[h][:, k, half * TH:(half + 1) * TH],
                                           start=(n == 0), stop=(n == 3 * KD - 1))
                            n += 1
                    mm.then_inc(u_done[half], 1)

                def weights(s, b):
                    pe.wait_ge(a_hi_ready, s * 4 + (b + 1))
                    pe.wait_ge(a_lo_ready, s * 4 + (b + 1))
                    pe.wait_ge(b_ready, s * 4 + (b + 1))
                    pe.wait_ge(w_kept[b], s)
                    for t in range(QB):
                        for j, a in enumerate((a_hi, a_lo)):
                            mm = pe.matmul(ps_w[b][:, t, :], b_[:, b % 2, t, :], a[:, b % 2, t, :],
                                           start=(j == 0 and t == 0), stop=(j == 1), skip_group_check=True)
                    mm.then_inc(w_mm[b % 2], 1)

                def of_step(hh, r, s):
                    turn(s, 0)
                    weights(s, 0)
                    weights(s, 1)
                    products(s, 0, 0)
                    turn(s, 1)
                    products(s, 0, 1)
                    weights(s, 2)
                    weights(s, 3)
                    products(s, 1, 0)
                    products(s, 1, 1)

                def of_block(o, last):
                    pe.wait_ge(sel_done, o * PH + PH)
                    pe.wait_ge(lo_done, o * (2 * STEPS))
                    for j in range(3):
                        mm = pe.transpose(ps_d[:, j, :], chosen[:, j, :], ident[:])
                    mm.then_inc(picks_turned, 1)
                    pe.wait_ge(picks_ready, o * 4 + 4)
                    alone(pe, pe_passed)
                    steps(pe, o, of_step)

                blocks(pe, of_block)

            @block.scalar
            def _(act):
                def cut(s, u):
                    act.wait_ge(turned[u], s + 1)
                    act.copy(d_hi[:, u], ps_d[:]).then_inc(hi_done, 1)

                def gelu(s, u, half):
                    act.wait_ge(u_done[half], s * 2 + (u + 1))
                    act.wait_ge(gu_stored[u], s * 16)
                    act.activation(gu[:, u, half * TH:(half + 1) * TH], ps_u[half][:], ACT.Gelu).then_inc(gelu_done[half], 1)

                def store(s, u):
                    for half in range(2):
                        act.wait_ge(gelu_done[half], s * 2 + (u + 1))
                    act.dma_start(scratch["gu"][bass.ds(s * 2 + u, 1)].rearrange("o p t -> (o p) t"), gu[:, u]
                                  ).then_inc(gu_stored[u], 16)

                def keep_weights(hh, r, s, b):
                    act.wait_ge(w_mm[b % 2], s * 2 + (b // 2 + 1))
                    alone(act, keep["act_passed"])
                    act.copy(wt[:, hh, :, bass.ds(r * STEP_TOKENS + b * QB, QB)],
                             ps_w[b][:].rearrange("p t e -> p e t")).then_inc(w_kept[b], 1)

                def of_block(o, last):
                    def of_step(hh, r, s):
                        cut(s, 0)
                        act.wait_ge(w_stored[hh], o * (16 * PIECES))
                        keep_weights(hh, r, s, 0)
                        keep_weights(hh, r, s, 1)
                        gelu(s, 0, 0)
                        cut(s, 1)
                        gelu(s, 0, 1)
                        store(s, 0)
                        keep_weights(hh, r, s, 2)
                        keep_weights(hh, r, s, 3)
                        if not last:
                            select_act(act, sel, step, exp_done, s)
                        gelu(s, 1, 0)
                        gelu(s, 1, 1)
                        store(s, 1)

                    steps(act, o, of_step)

                blocks(act, of_block)

            @block.vector
            def _(dve):
                def low(s, u):
                    dve.wait_ge(hi_done, s * 2 + (u + 1))
                    dve.tensor_tensor(d_lo[:, u], ps_d[:], d_hi[:, u].bitcast(F32), ALU.subtract).then_inc(lo_done, 1)

                def first(hh, r, s, b):
                    at = bass.ds(r * STEP_TOKENS + (hh * WT + b * QB), QB)
                    wide = lambda ap: ap[:, at].unsqueeze(2).to_broadcast([P, QB, P])
                    keys = iota[:].unsqueeze(1).to_broadcast([P, QB, P])
                    dve.wait_ge(w_mm[b % 2], s * 2 + b // 2)
                    dve.tensor_tensor(hit1[:, b % 2], wide(pick_1), keys, ALU.is_equal).then_inc(hit1_ready, 1)
                    dve.tensor_tensor(b_[:, b % 2], wide(pick_2), keys, ALU.is_equal).then_inc(b_ready, 1)
                    dve.wait_ge(hit1_ready, s * 4 + (b + 1))
                    dve.tensor_tensor(a_hi[:, b % 2], hit1[:, b % 2], wide(pick_g_hi).bitcast(F32), ALU.mult
                                      ).then_inc(a_hi_ready, 1)

                def of_block(o, last):
                    dve.wait_ge(picks_turned, o + 1)
                    dve.wait_ge(a_lo_ready, o * 32)
                    dve.wait_ge(a_hi_ready, o * 32)
                    dve.wait_ge(b_ready, o * 32)
                    dve.tensor_copy(pick_g_hi[:], ps_d[:, 0, :]).then_inc(picks_ready, 1)
                    dve.tensor_copy(pick_1[:], ps_d[:, 1, :]).then_inc(picks_ready, 1)
                    dve.tensor_copy(pick_2[:], ps_d[:, 2, :]).then_inc(picks_ready, 1)
                    dve.wait_ge(picks_ready, o * 4 + 3)
                    dve.tensor_tensor(pick_g_lo[:], ps_d[:, 0, :], pick_g_hi[:].bitcast(F32), ALU.subtract
                                      ).then_inc(picks_ready, 1)
                    dve.wait_ge(picks_ready, o * 4 + 4)
                    alone(dve, keep["dve_passed"])

                    def of_step(hh, r, s):
                        low(s, 0)
                        first(hh, r, s, 0)
                        first(hh, r, s, 1)
                        low(s, 1)
                        first(hh, r, s, 2)
                        first(hh, r, s, 3)
                        if not last:
                            h = r + hh * (STEPS // 2)
                            select_dve(dve, sel, step, exp_done, keep, s, o + 1, h,
                                       lambda which: chosen[:, which, bass.ds(h * TOPK, TOPK)])

                    steps(dve, o, of_step)

                blocks(dve, of_block)


GT = 4


def experts_up(m, inp, keep, scratch, out):
    nc = m.nc
    gate_rows = keep["gate_rows"]
    GROUPS = E1 // GT
    SLOTS = 2 * TB
    with ExitStack() as st:
        up_raw = m.sb(st, "up_raw", [P, 2, D])
        gu = m.sb(st, "gelu_in", [P, 2, T])
        w = m.sb(st, "weights_in", [P, 2, T])
        g_hi = m.sb(st, "coef_hi", [P, 2, GT, T], F32R)
        g_lo = m.sb(st, "coef_lo", [P, 2, GT, T], F32R)
        up_hi = m.sb(st, "up_hi", [P, 2, GT, D], F32R)
        up_lo = m.sb(st, "up_lo", [P, 2, GT, D], F32R)
        acc = m.sb(st, "y_acc", [P, TB, D])
        x1 = m.sb(st, "x1_in", [P, 2, D])
        stat = m.sb(st, "y_stat", [P, TB, 3])
        eps = m.sb(st, "eps6", [P, 1])
        ps_y = [m.ps(st, f"p6_y{i}", [P, TH]) for i in range(8)]

        gu_loaded = [m.sem(f"gelu_loaded{i}") for i in range(2)]
        w_loaded = [m.sem(f"weights_loaded{i}") for i in range(2)]
        up_loaded = [m.sem(f"up_loaded{i}") for i in range(2)]
        coef_ready, g_hi_done, g_lo_done = m.sem("coef_ready"), m.sem("coef_hi_done"), m.sem("coef_lo_done")
        up_hi_done, up_lo_done = m.sem("up_hi_done"), m.sem("up_lo_done")
        acc_zeroed, y_mm, added = m.sem("acc_zeroed"), m.sem("y_mm"), m.sem("y_added")
        x1_loaded = [m.sem(f"x1_in_loaded{i}") for i in range(2)]
        ssq, std, rstd, scaled, summed = (m.sem(f"y_{n}") for n in ("ssq", "std", "rstd", "scaled", "summed"))
        out_stored = m.sem("out_stored")
        up = inp["peer_up"][0].rearrange("(e p) d -> e p d", p=P)

        with nc.Block() as block:
            @block.sync
            def _(sp):
                def load(g, v):
                    for j in range(GT):
                        n, u = g * GT + j, j % 2
                        wait_from(sp, up_lo_done, n - 1)
                        sp.dma_start(up_raw[:, u], up[bass.ds(n, 1)].rearrange("o p d -> (o p) d")
                                     ).then_inc(up_loaded[u], 16)
                        wait_from(sp, g_lo_done, n - 1)
                        sp.dma_start(gu[:, u], scratch["gu"][bass.ds(n, 1)].rearrange("o p t -> (o p) t")
                                     ).then_inc(gu_loaded[u], 16)
                        sp.dma_start(w[:, u].rearrange("p (h t) -> p h t", t=WT),
                                     scratch["w"][:, :, bass.ds(n, 1), :].rearrange("h p o t -> p (h o) t")
                                     ).then_inc(w_loaded[u], 16)

                pairs(sp, 0, GROUPS, load)
                for t in range(TB):
                    if t >= 2:
                        sp.wait_ge(summed, t - 1)
                    sp.dma_start(x1[:, t % 2], scratch["x1"][t * P:(t + 1) * P, :]).then_inc(x1_loaded[t % 2], 16)
                    if t >= 1:
                        sp.wait_ge(summed, t)
                        sp.dma_start(out[0, (t - 1) * P:t * P, :], acc[:, t - 1, :]).then_inc(out_stored, 16)
                sp.wait_ge(summed, TB)
                sp.dma_start(out[0, (TB - 1) * P:TB * P, :], acc[:, TB - 1, :]).then_inc(out_stored, 16)
                sp.wait_ge(out_stored, 16 * TB)

            @block.gpsimd
            def _(pool):
                pool.memset(acc[:], 0.0).then_inc(acc_zeroed, 1)
                pool.memset(eps[:], EPS).then_inc(acc_zeroed, 1)

                def cut(g, v):
                    for j in range(GT):
                        n, u = g * GT + j, j % 2
                        pool.wait_ge(up_hi_done, n + 1)
                        pool.tensor_tensor(up_lo[:, v, j, :], up_raw[:, u], up_hi[:, v, j, :].bitcast(F32),
                                           ALU.subtract).then_inc(up_lo_done, 1)

                pairs(pool, 0, GROUPS, cut)

            @block.scalar
            def _(act):
                def cut(g, v):
                    wait_from(act, y_mm, (g - 1) * SLOTS)
                    for j in range(GT):
                        n, u = g * GT + j, j % 2
                        loads = g * (8 * GT) + 16 * (j // 2 + 1)
                        act.wait_ge(up_loaded[u], loads)
                        act.copy(up_hi[:, v, j, :], up_raw[:, u]).then_inc(up_hi_done, 1)
                        act.wait_ge(coef_ready, n + 1)
                        act.copy(g_hi[:, v, j, :], gu[:, u]).then_inc(g_hi_done, 1)

                pairs(act, 0, GROUPS, cut)
                act.wait_ge(acc_zeroed, 2)
                for t in range(TB):
                    act.wait_ge(added, SLOTS * (GROUPS - 1) + 2 * t + 2)
                    if t >= 1:
                        act.wait_ge(ssq, t)
                    act.activation(gu[:, 0], acc[:, t, :], ACT.Square, accum_out=stat[:, t, 0:1]).then_inc(ssq, 1)
                    act.wait_ge(ssq, t + 1)
                    act.activation(stat[:, t, 1:2], stat[:, t, 0:1], ACT.Sqrt, bias=eps[:], scale=1.0 / D).then_inc(std, 1)

            @block.vector
            def _(dve):
                def coef(g, v, j):
                    n, u = g * GT + j, j % 2
                    loads = g * (8 * GT) + 16 * (j // 2 + 1)
                    dve.wait_ge(gu_loaded[u], loads)
                    dve.wait_ge(w_loaded[u], loads)
                    dve.tensor_tensor(gu[:, u], gu[:, u], w[:, u], ALU.mult).then_inc(coef_ready, 1)
                    dve.wait_ge(g_hi_done, n + 1)
                    dve.tensor_tensor(g_lo[:, v, j, :], gu[:, u], g_hi[:, v, j, :].bitcast(F32), ALU.subtract
                                      ).then_inc(g_lo_done, 1)

                def add(g, s):
                    dve.wait_ge(y_mm, g * SLOTS + (s + 1))
                    wait_from(dve, added, g * SLOTS + (s + 1 - SLOTS))
                    part = acc[:, s // 2, (s % 2) * TH:(s % 2 + 1) * TH]
                    dve.tensor_tensor(part, ps_y[s % 8][:], part, ALU.add).then_inc(added, 1)

                def group(g, v):
                    for j in range(GT):
                        coef(g, v, j)
                        if not isinstance(g, int) or g > 0:
                            for s in range(4 * j, 4 * j + 4):
                                add(g - 1, s)

                dve.wait_ge(acc_zeroed, 1)
                pairs(dve, 0, GROUPS, group)

                def finish(t):
                    dve.wait_ge(std, t + 1)
                    dve.reciprocal(stat[:, t, 2:3], stat[:, t, 1:2]).then_inc(rstd, 1)
                    dve.wait_ge(rstd, t + 1)
                    dve.scalar_tensor_tensor(acc[:, t, :], acc[:, t, :], stat[:, t, 2:3], gate_rows[:, 1, :],
                                             ALU.mult, ALU.mult).then_inc(scaled, 1)
                    dve.wait_ge(scaled, t + 1)
                    dve.wait_ge(x1_loaded[t % 2], 16 * (t // 2 + 1))
                    dve.tensor_tensor(acc[:, t, :], acc[:, t, :], x1[:, t % 2], ALU.add).then_inc(summed, 1)

                for s in range(SLOTS):
                    add(GROUPS - 1, s)
                    if s % 2 and s > 1:
                        finish(s // 2 - 1)
                finish(TB - 1)

            @block.tensor
            def _(pe):
                def group(g, v):
                    pe.wait_ge(g_lo_done, g * GT + GT)
                    pe.wait_ge(up_lo_done, g * GT + GT)
                    for s in range(SLOTS):
                        t, half = divmod(s, 2)
                        wait_from(pe, added, g * SLOTS + (s - 7))
                        n = 0
                        for j in range(GT):
                            for a, b in ((g_hi, up_hi), (g_hi, up_lo), (g_lo, up_hi)):
                                mm = pe.matmul(ps_y[s % 8][:], a[:, v, j, t * P:(t + 1) * P],
                                               b[:, v, j, half * TH:(half + 1) * TH],
                                               start=(n == 0), stop=(n == 3 * GT - 1))
                                n += 1
                        mm.then_inc(y_mm, 1)

                pairs(pe, 0, GROUPS, group)


def build(nc, inp, out):
    scratch = {}
    for name, shape in (("xbc", [XBC, T]), ("z", [SI, T]), ("gates", [2 * D, T]), ("y_lru", [D, T]), ("y_ssd", [SI, T]),
                        ("merged", [D, T]), ("x1", [T, D]), ("h2", [D, T]), ("gu", [E1, P, T]),
                        ("w", [T // WT, P, E1, WT])):
        scratch[name] = nc.dram_tensor(f"scratch_{name}", shape, F32, kind="Internal").ap()
    with ExitStack() as stack:
        m = Machine(nc, stack)
        keep = {
            "ident": m.sb(stack, "ident", [P, P]),
            "mod": m.sb(stack, "mod", [P, 4, KD]),
            "gate_rows": m.sb(stack, "gate_rows", [P, 2, D]),
            "pool_passed": m.kept_sem("pool_passed"),
            "act_passed": m.kept_sem("act_passed"),
            "consts_ready": m.kept_sem("consts_ready"),
        }
        with ExitStack() as mix:
            keep["cols"] = m.sb(mix, "cols", [P, 272])
            keep["tri"] = m.sb(mix, "tri", [P, P])
            keep["mask"] = m.sb(mix, "mask", [P, 4, P], BF16)
            keep["ones"] = m.sb(mix, "ones", [P, P])
            keep["sp_in"] = m.sb(mix, "softplus_in", [P, KD + TB * SH])
            keep["sp_out"] = m.sb(mix, "softplus_out", [P, KD + TB * SH])
            with ExitStack() as project:
                keep["hT"] = [m.sb(project, "hT_hi", [P, KD, T], F32R), m.sb(project, "hT_lo", [P, KD, T], F32R)]
                vectors_and_norm(m, inp, keep)
                m.end_phase()
                project_in(m, inp, keep, scratch)
                m.end_phase()
            ssd(m, inp, keep, scratch)
            m.end_phase()
            merge(m, inp, keep, scratch)
            m.end_phase()
            post_mix(m, inp, keep, scratch)
            m.end_phase()
        with ExitStack() as picks:
            expert_keep(m, picks, keep)
            queries(m, inp, keep, scratch)
            m.end_phase()
            experts_down(m, inp, keep, scratch)
            m.end_phase()
        experts_up(m, inp, keep, scratch, out)


_INS = ["x", "c", "w_ada", "b_ada", "norm_pre_mix", "norm_post_mix", "norm_pre_ffn", "norm_post_ffn", "w_in",
        "lru_conv_w", "lru_conv_b", "lru_wa", "lru_ba", "lru_wx", "lru_bx", "lru_lambda", "ssd_conv_w", "ssd_conv_b",
        "ssd_dt_bias", "ssd_a_log", "ssd_d", "ssd_norm_w", "w_lru_out", "w_ssd_out", "w_o", "peer_wq",
        "peer_sub_keys", "peer_down", "peer_up"]
_OUTS = [((1, T, D), "float32")]


def kernel(**inputs):
    import numpy as _np
    import concourse.bacc as _bacc
    from concourse import mybir as _mybir
    from concourse.bass_utils import run_bass_kernel_spmd as _run

    nc = _bacc.Bacc("TRN2", target_bir_lowering=False, num_devices=1)
    arrays, inp = {}, {}
    for name in _INS:
        a = _np.ascontiguousarray(inputs[name])
        arrays[f"in_{name}_dram"] = a
        inp[name] = nc.dram_tensor(f"in_{name}_dram", a.shape, _mybir.dt.from_np(a.dtype), kind="ExternalInput").ap()
    shape, dtype = _OUTS[0]
    out = nc.dram_tensor("out_0_dram", shape, _mybir.dt.from_np(_np.dtype(dtype)), kind="ExternalOutput").ap()
    build(nc, inp, out)
    r = _run(nc, [arrays], core_ids=[0])
    return r.results[0]["out_0_dram"]
```

```python
from contextlib import ExitStack

import concourse.bass as bass
from concourse import mybir

F32 = mybir.dt.float32
F32R = mybir.dt.float32r
BF16 = mybir.dt.bfloat16
U32 = mybir.dt.uint32
ALU = mybir.AluOpType
ACT = mybir.ActivationFunctionType
AX = mybir.AxisListType

P = 128
T = 1024
TB = T // P
TH = 512
D = 1024
KD = D // P
CW = 4
EPS = 1e-6
LRU_C = 8.0
SI = 2048
SH = 32
SG = 4
SHG = SH // SG
SP_ = SI // SH
XBC = SI + 2 * SG * P
COL_LRU, COL_Z, COL_XBC = 0, D, D + SI
COL_DT = COL_XBC + XBC
COL_GATE = COL_DT + SH
NEG = -30000.0

VEC = {}
_row = 0
for _name, _n in (("b_ada", 48), ("norm_pre_mix", 8), ("norm_pre_ffn", 8), ("lru_conv_w", 32),
                  ("lru_conv_b", 8), ("lru_ba", 8), ("lru_bx", 8), ("lru_lambda", 8),
                  ("ssd_conv_w", 96), ("ssd_conv_b", 24), ("ssd_norm_w", 16), ("c", 8)):
    VEC[_name] = _row
    _row += _n
VEC_TILES = ((0, 128), (128, 120), (248, 24))
assert _row == 272 and VEC["ssd_norm_w"] == 248


class Machine:

    def __init__(self, nc, stack):
        self.nc, self.stack = nc, stack
        self.phase_sems = []

    def sb(self, stack, name, shape, dt=F32):
        return stack.enter_context(self.nc.sbuf_tensor(name, shape, dt))

    def ps(self, stack, name, shape, dt=F32):
        return stack.enter_context(self.nc.psum_tensor(name, shape, dt))

    def kept_sem(self, name):
        return self.stack.enter_context(self.nc.semaphore(name))

    def sem(self, name):
        self.phase_sems.append(self.nc.alloc_semaphore(name))
        return self.phase_sems[-1]

    def end_phase(self):
        self.nc.all_engine_barrier()
        self.nc.clear_and_free_semaphores(self.phase_sems)
        self.nc.all_engine_barrier()
        self.phase_sems = []


def vectors_and_norm(m, inp, keep):
    nc = m.nc
    with ExitStack() as st:
        rows = m.sb(st, "vec_rows", [P, 3, P])
        x_in = m.sb(st, "x_in", [P, TB, D])
        junk = m.sb(st, "square_out", [P, D])
        w_ada = m.sb(st, "w_ada_sb", [P, 4, KD, TH])
        diag = m.sb(st, "mod_diag", [P, 4, P])
        ssq = m.sb(st, "x_ssq", [P, TB])
        std = m.sb(st, "x_std", [P, TB])
        rstd = m.sb(st, "x_rstd", [P, TB])
        h_full = m.sb(st, "h_full", [P, 2, TH])
        mult1 = m.sb(st, "mult1", [P, KD])
        eps = m.sb(st, "eps0", [P, 1])
        c_cols = m.sb(st, "c_cols", [P, KD])
        c_wide = m.sb(st, "c_wide", [P, KD, P])
        norm_rows = m.sb(st, "norm_rows", [P, 2, D])
        ps_a = [m.ps(st, f"p0_a{i}", [P, 512]) for i in range(4)]
        ps_r = [m.ps(st, f"p0_r{i}", [P, TH]) for i in range(4)]
        ident, tri, mask, ones = keep["ident"], keep["tri"], keep["mask"], keep["ones"]
        cols, mod, gate_rows = keep["cols"], keep["mod"], keep["gate_rows"]
        hT = keep["hT"]

        consts_ready = keep["consts_ready"]
        consts_set = m.sem("consts_set")
        vec_loaded = m.sem("vec_loaded")
        row_vecs_loaded = m.sem("row_vecs_loaded")
        x_loaded = [m.sem(f"x_loaded{i}") for i in range(4)]
        ada_loaded = [m.sem(f"ada_loaded{i}") for i in range(4)]
        cols_turned = m.sem("cols_turned")
        cols_ready = m.sem("cols_ready")
        c_ready = m.sem("c_ready")
        ssq_ready = m.sem("ssq_ready")
        std_ready = m.sem("std_ready")
        rstd_ready = m.sem("rstd_ready")
        xn_ready = m.sem("xn_ready")
        piece_done = m.sem("mod_piece_done")
        piece_out = m.sem("mod_piece_out")
        mod_step = m.sem("mod_step")
        mult_ready = m.sem("mult_ready")
        turned = m.sem("x_turned")
        full_ready = m.sem("h_full_ready")
        hi_ready = m.sem("h_hi_ready")
        lo_ready = m.sem("h_lo_ready")
        rows_ready = m.sem("gate_rows_ready")

        VECS = len(VEC)

        def vec_parts():
            for name, shape in (("b_ada", "one (a b) -> (one a) b"), ("norm_pre_mix", None),
                                ("norm_pre_ffn", None), ("lru_conv_w", "w"), ("lru_conv_b", None),
                                ("lru_ba", None), ("lru_bx", None), ("lru_lambda", None),
                                ("ssd_conv_w", "w"), ("ssd_conv_b", None), ("ssd_norm_w", None),
                                ("c", None)):
                pattern = "o w (a b) -> (o w a) b" if shape == "w" else "o (a b) -> (o a) b"
                src = inp[name].rearrange(pattern, b=P)
                yield src, VEC[name]

        SEGS = (0, 1, 3, 4, 2, 5)
        PIECES = 2 * len(SEGS)
        FIRST = 4
        TURNS = 2 * KD

        with nc.Block() as block:
            @block.sync
            def _(sp):
                n = 0
                for src, row in vec_parts():
                    tile = (row >= VEC_TILES[1][0]) + (row >= VEC_TILES[2][0])
                    at = row - VEC_TILES[tile][0]
                    sp.dma_start(rows[at:at + src.shape[0], tile, :], src).then_inc(vec_loaded, 16)
                    n += 1
                assert n == VECS

                def piece(n):
                    i, half = divmod(n, 2)
                    if n >= 4:
                        sp.wait_ge(piece_done, n - 3)
                    at = SEGS[i] * D + half * TH
                    sp.dma_start(w_ada[:, n % 4], inp["w_ada"][0, :, at:at + TH].rearrange("(k p) n -> p k n", p=P)
                                 ).then_inc(ada_loaded[n % 4], 16)

                for n in range(FIRST):
                    piece(n)
                    for t in (2 * n, 2 * n + 1):
                        sp.dma_start(x_in[:, t, :], inp["x"][0, t * P:(t + 1) * P, :]).then_inc(x_loaded[t // 2], 16)
                for g, (seg, norm) in enumerate(((2, "norm_post_mix"), (5, "norm_post_ffn"))):
                    sp.dma_start(gate_rows[:, g, :], inp["b_ada"][0, seg * D:(seg + 1) * D].partition_broadcast(P)
                                 ).then_inc(row_vecs_loaded, 16)
                    sp.dma_start(norm_rows[:, g, :], inp[norm][0].partition_broadcast(P)).then_inc(row_vecs_loaded, 16)
                for n in range(FIRST, PIECES):
                    piece(n)

            @block.gpsimd
            def _(pool):
                pool.memset(ident[:], 0.0).then_inc(consts_set, 1)
                pool.memset(tri[:], 1.0).then_inc(consts_set, 1)
                pool.memset(mask[:], 0.0).then_inc(consts_set, 1)
                pool.memset(ones[:], 1.0).then_inc(consts_ready, 1)
                pool.memset(eps[:], EPS).then_inc(consts_ready, 1)
                pool.wait_ge(consts_set, 3)
                pool.affine_select(out=ident[:], in_=ident[:], compare_op=ALU.not_equal, fill=1.0, base=0,
                                   pattern=[[-1, P]], channel_multiplier=1).then_inc(consts_ready, 1)
                pool.affine_select(out=tri[:], in_=tri[:], compare_op=ALU.is_ge, fill=0.0, base=0,
                                   pattern=[[1, P]], channel_multiplier=-1).then_inc(consts_ready, 1)
                pool.affine_select(out=mask[:], in_=mask[:], compare_op=ALU.is_ge, fill=NEG, base=0,
                                   pattern=[[0, 4], [1, P]], channel_multiplier=-1).then_inc(consts_ready, 1)

            @block.scalar
            def _(act):
                act.wait_ge(consts_ready, 5)
                act.wait_ge(cols_ready, 3)
                act.activation(c_cols[:], cols[:, VEC["c"]:VEC["c"] + KD], ACT.Silu).then_inc(c_ready, 1)
                for t in range(TB):
                    act.wait_ge(x_loaded[t // 2], 32)
                    act.activation(junk[:], x_in[:, t, :], ACT.Square, accum_out=ssq[:, t:t + 1]).then_inc(ssq_ready, 1)
                    act.wait_ge(ssq_ready, t + 1)
                act.activation(std[:], ssq[:], ACT.Sqrt, bias=eps[:], scale=1.0 / D).then_inc(std_ready, 1)
                for n in range(TURNS):
                    k, half = divmod(n, 2)
                    act.wait_ge(full_ready, n + 1)
                    act.copy(hT[0][:, k, half * TH:(half + 1) * TH], h_full[:, n % 2, :]).then_inc(hi_ready, 1)

            @block.vector
            def _(dve):
                for t, (row, n) in enumerate(VEC_TILES):
                    dve.wait_ge(cols_turned, t + 1)
                    dve.tensor_copy(cols[:, row:row + n], ps_a[t % 2][:, 0:n]).then_inc(cols_ready, 1)
                dve.wait_ge(c_ready, 1)
                dve.tensor_copy(c_wide[:], c_cols[:].unsqueeze(2).to_broadcast([P, KD, P])).then_inc(c_ready, 1)
                dve.wait_ge(std_ready, 1)
                dve.reciprocal(rstd[:], std[:]).then_inc(rstd_ready, 1)
                dve.wait_ge(rstd_ready, 1)
                for t in range(TB):
                    dve.tensor_scalar(x_in[:, t, :], x_in[:, t, :], rstd[:, t:t + 1], None, ALU.mult).then_inc(xn_ready, 1)

                def piece(n):
                    i, half = divmod(n, 2)
                    dve.wait_ge(piece_done, n + 1)
                    if i < 4:
                        blocks = slice(half * 4, half * 4 + 4)
                        dve.wait_ge(mod_step, 2 * n)
                        dve.tensor_tensor(diag[:], ps_r[n % 4][:].rearrange("p (a b) -> p a b", b=P),
                                          ident[:].unsqueeze(1).to_broadcast([P, 4, P]), ALU.mult).then_inc(piece_out, 1)
                        dve.wait_ge(piece_out, n + 1)
                        dve.reduce_sum(mod[:, i, blocks], diag[:], axis=AX.X).then_inc(mod_step, 1)
                        dve.wait_ge(mod_step, 2 * n + 1)
                        at = SEGS[i] * KD + half * 4
                        dve.tensor_tensor(mod[:, i, blocks], mod[:, i, blocks], cols[:, at:at + 4], ALU.add
                                          ).then_inc(mod_step, 1)
                    else:
                        if n == 8:
                            dve.wait_ge(row_vecs_loaded, 16 * 4)
                        part = gate_rows[:, i - 4, half * TH:(half + 1) * TH]
                        dve.tensor_tensor(part, ps_r[n % 4][:], part, ALU.add).then_inc(piece_out, 1)

                for n in range(FIRST):
                    piece(n)
                dve.wait_ge(mod_step, 2 * FIRST)
                nw = VEC["norm_pre_mix"]
                dve.scalar_tensor_tensor(mult1[:], mod[:, 1, :], 1.0, cols[:, nw:nw + KD], ALU.add, ALU.mult
                                         ).then_inc(mult_ready, 1)
                dve.wait_ge(mult_ready, 1)

                def low(n):
                    k, half = divmod(n, 2)
                    sl = slice(half * TH, (half + 1) * TH)
                    dve.wait_ge(hi_ready, n + 1)
                    dve.tensor_tensor(hT[1][:, k, sl], h_full[:, n % 2, :], hT[0][:, k, sl].bitcast(F32), ALU.subtract
                                      ).then_inc(lo_ready, 1)

                for n in range(TURNS):
                    dve.wait_ge(turned, n + 1)
                    if n >= 2:
                        dve.wait_ge(lo_ready, n - 1)
                    dve.tensor_scalar(h_full[:, n % 2, :], ps_a[n % 4][:], mult1[:, n // 2:n // 2 + 1],
                                      mod[:, 0, n // 2:n // 2 + 1], ALU.mult, ALU.add).then_inc(full_ready, 1)
                    if n >= 1:
                        low(n - 1)
                    if n % 2:
                        piece(FIRST + n // 2)
                low(TURNS - 1)
                dve.wait_ge(mod_step, 16)
                nw = VEC["norm_pre_ffn"]
                dve.scalar_tensor_tensor(mod[:, 3, :], mod[:, 3, :], 1.0, cols[:, nw:nw + KD],
                                         ALU.add, ALU.mult).then_inc(mult_ready, 1)
                dve.wait_ge(piece_out, PIECES)
                dve.tensor_tensor(gate_rows[:], gate_rows[:], norm_rows[:], ALU.mult).then_inc(rows_ready, 1)

            @block.tensor
            def _(pe):
                pe.wait_ge(consts_ready, 5)
                pe.wait_ge(vec_loaded, 16 * VECS)
                for t, (row, n) in enumerate(VEC_TILES):
                    if t >= 2:
                        pe.wait_ge(cols_ready, t - 1)
                    pe.transpose(ps_a[t % 2][:, 0:n], rows[0:n, t, :], ident[0:n, 0:n]).then_inc(cols_turned, 1)
                pe.wait_ge(c_ready, 2)

                def piece(n):
                    pe.wait_ge(ada_loaded[n % 4], 16 * (n // 4 + 1))
                    if n >= 4:
                        pe.wait_ge(piece_out, n - 3)
                    for k in range(KD):
                        mm = pe.matmul(ps_r[n % 4][:], c_wide[:, k, :], w_ada[:, n % 4, k, :],
                                       start=(k == 0), stop=(k == KD - 1))
                    mm.then_inc(piece_done, 1)

                def turn(n):
                    k, half = divmod(n, 2)
                    if n >= 4:
                        pe.wait_ge(full_ready, n - 3)
                    for j in range(4):
                        mm = pe.transpose(ps_a[n % 4][:, j * P:(j + 1) * P],
                                          x_in[:, half * 4 + j, k * P:(k + 1) * P], ident[:])
                    mm.then_inc(turned, 1)

                for n in range(FIRST):
                    piece(n)
                pe.wait_ge(xn_ready, TB)
                pe.wait_ge(cols_ready, 3)
                for n in range(TURNS):
                    turn(n)
                    if n % 2:
                        piece(FIRST + n // 2)


def pairs(eng, lo, hi, body):
    assert lo % 2 == 0 and hi % 2 == 0
    if lo == 0:
        body(0, 0)
        body(1, 1)
        lo = 2
    with eng.Fori(lo // 2, hi // 2) as p:
        body(p * 2, 0)
        body(p * 2 + 1, 1)


def wait_from(eng, sem, value):
    if not isinstance(value, int) or value > 0:
        eng.wait_ge(sem, value)


def alone(eng, passed):
    eng.sem_inc(passed, 1)


def ahead(eng, *sems, by=1):
    for sem in sems:
        eng.sem_inc(sem, by)


def of_buffer(i, u):
    return (i - u) * 8


def project_in(m, inp, keep, scratch):
    nc = m.nc
    N_LRU, N_XBC, N_Z, N_GATE = KD, XBC // P, SI // P, 2 * KD
    B_XBC = N_LRU
    B_Z = B_XBC + N_XBC
    B_GATE = B_Z + N_Z
    TILES = B_GATE + N_GATE
    pool_passed, act_passed = keep["pool_passed"], keep["act_passed"]
    hT, cols, sp_in, sp_out = keep["hT"], keep["cols"], keep["sp_in"], keep["sp_out"]
    with ExitStack() as st:
        w_raw = m.sb(st, "w_raw", [P, 2, KD, P])
        w_hi = m.sb(st, "w_hi", [P, 2, KD, P], F32R)
        w_lo = m.sb(st, "w_lo", [P, 2, KD, P], F32R)
        dt_raw = m.sb(st, "w_dt_raw", [P, KD, SH])
        dt_hi = m.sb(st, "w_dt_hi", [P, KD, SH], F32R)
        dt_lo = m.sb(st, "w_dt_lo", [P, KD, SH], F32R)
        dt_bias = m.sb(st, "dt_bias", [P, SH])
        pre = m.sb(st, "conv_in", [P, 2, CW - 1 + T])
        acc = m.sb(st, "conv_out", [P, 2, T])
        fin = m.sb(st, "act_out", [P, 2, T])
        xl = m.sb(st, "lru_x", [P, KD, T])
        w_gate = m.sb(st, "lru_w", [P, 2, KD, P])
        w_cur = m.sb(st, "lru_w_cur", [P, 2, P])
        r_, i_, a_ = (m.sb(st, n, [P, T]) for n in ("lru_r", "lru_i", "lru_a"))
        th, v_, sq, ix, hl = (m.sb(st, n, [P, T]) for n in ("lru_tanh", "lru_v", "lru_sqrt", "lru_ix", "lru_h"))
        NS = KD + TB * SH
        s_abs, s_e, s_u, s_c = (m.sb(st, n, [P, NS]) for n in ("sp_abs", "sp_exp", "sp_one_plus", "sp_corr"))
        ps = [m.ps(st, f"p1_{i}", [P, 2, TH]) for i in range(2)]
        ps_g = m.ps(st, "p1_gates", [P, 2, TH])
        ps_dt = m.ps(st, "p1_dt", [P, 512])

        w_loaded = [m.sem(f"w_in_loaded{i}") for i in range(2)]
        small_loaded = m.sem("small_loaded")
        zeroed = m.sem("lru_w_zeroed")
        hi_done, lo_done = m.sem("w_hi_done"), m.sem("w_lo_done")
        dt_split, dt_done = m.sem("dt_split"), m.sem("dt_done")
        sp_dve, sp_act = m.sem("softplus_dve"), m.sem("softplus_act")
        mm_done, evac_done = m.sem("proj_done"), m.sem("proj_evacuated")
        conv_step, silu_done = m.sem("conv_step"), m.sem("silu_done")
        act_done = m.sem("act_done")
        stored = [m.sem(f"act_stored{i}") for i in range(2)]
        w_cur_ready, lru_mm, sig_done = m.sem("lru_w_ready"), m.sem("lru_products"), m.sem("lru_sigmoids")
        exp_done, v_done, sqrt_done = m.sem("lru_exp_tanh"), m.sem("lru_v_done"), m.sem("lru_sqrt_done")
        ix_done, u_done, scan_done = m.sem("lru_ix_done"), m.sem("lru_u_done"), m.sem("lru_scan_done")
        h_stored = m.sem("lru_h_stored")

        def w_in(col, j):
            return inp["w_in"][0, :, bass.ds(j * P + col, P)].rearrange("(k p) n -> p k n", p=P)

        SEGMENTS = ((0, B_XBC, COL_LRU), (B_XBC, B_Z, COL_XBC - B_XBC * P),
                    (B_Z, B_GATE, COL_Z - B_Z * P), (B_GATE, TILES, COL_GATE - B_GATE * P))

        def quads(eng, tile, lru):
            for seg in (2, 3):
                lo, hi, _ = SEGMENTS[seg]
                with eng.Fori(lo // 4, hi // 4) as p:
                    j = p - B_Z // 4
                    for q in range(4):
                        tile(p * 4 + q, q % 2, seg)
                        lru(j, q)

        with nc.Block() as block:
            @block.sync
            def _(sp):
                sp.dma_start(dt_raw[:], inp["w_in"][0, :, COL_DT:COL_DT + SH].rearrange("(k p) n -> p k n", p=P)
                             ).then_inc(small_loaded, 16)
                sp.dma_start(dt_bias[:], inp["ssd_dt_bias"][0].partition_broadcast(P)).then_inc(small_loaded, 16)

                def load(col):
                    def body(i, u):
                        wait_from(sp, lo_done, i - 1)
                        sp.dma_start(w_raw[:, u], w_in(col, i)).then_inc(w_loaded[u], 16)
                    return body

                pairs(sp, 0, B_XBC, load(SEGMENTS[0][2]))
                sp.wait_ge(zeroed, 1)
                for g, name in enumerate(("lru_wa", "lru_wx")):
                    for odd in range(2):
                        at = slice(64 * odd, 64 * odd + 64)
                        sp.dma_start(w_gate[at, g, :, at],
                                     inp[name][0].rearrange("(j two) a b -> two a j b", two=2)[odd]
                                     ).then_inc(small_loaded, 16)
                for lo, hi, col in SEGMENTS[1:]:
                    pairs(sp, lo, hi, load(col))

            @block.gpsimd
            def _(pool):
                pool.memset(w_gate[:], 0.0).then_inc(zeroed, 1)
                pool.memset(pre[:, :, 0:CW - 1], 0.0).then_inc(zeroed, 1)
                pool.wait_ge(small_loaded, 32)
                pool.tensor_copy(dt_hi[:], dt_raw[:]).then_inc(dt_split, 1)
                pool.wait_ge(dt_split, 1)
                pool.tensor_tensor(dt_lo[:], dt_raw[:], dt_hi[:].bitcast(F32), ALU.subtract).then_inc(dt_split, 1)

                def cut(i, u, seg=0):
                    pool.wait_ge(w_loaded[u], of_buffer(i, u) + 16)
                    wait_from(pool, mm_done, i - 1)
                    alone(pool, pool_passed)
                    pool.tensor_copy(w_hi[:, u], w_raw[:, u]).then_inc(hi_done, 1)
                    pool.wait_ge(hi_done, i + 1)
                    pool.tensor_tensor(w_lo[:, u], w_raw[:, u], w_hi[:, u].bitcast(F32), ALU.subtract
                                       ).then_inc(lo_done, 1)

                def lru(j, q):
                    if q == 0:
                        wait_from(pool, lru_mm, j * 2)
                        alone(pool, pool_passed)
                        pool.tensor_copy(w_cur[:], w_gate[:, :, bass.ds(j, 1), :].rearrange("p g o n -> p (g o) n")
                                         ).then_inc(w_cur_ready, 1)
                    if q == 3:
                        pool.wait_ge(sig_done, j * 4 + 4)
                        wait_from(pool, u_done, j)
                        pool.tensor_tensor(ix[:], i_[:], xl[:, bass.ds(j, 1), :].rearrange("p o n -> p (o n)"),
                                           ALU.mult).then_inc(ix_done, 1)

                pairs(pool, 0, B_XBC, cut)
                pairs(pool, B_XBC, B_Z, cut)
                pool.wait_ge(small_loaded, 96)
                quads(pool, cut, lru)

            @block.tensor
            def _(pe):
                pe.wait_ge(dt_split, 2)
                for t in range(TB):
                    n = 0
                    for k in range(KD):
                        for h, w in ((0, dt_hi), (0, dt_lo), (1, dt_hi)):
                            mm = pe.matmul(ps_dt[:, t * SH:(t + 1) * SH], hT[h][:, k, t * P:(t + 1) * P], w[:, k, :],
                                           start=(n == 0), stop=(n == 3 * KD - 1), skip_group_check=True)
                            n += 1
                mm.then_inc(dt_done, 1)

                def tile(i, u, seg=0):
                    pe.wait_ge(lo_done, i + 1)
                    wait_from(pe, evac_done, i - 1)
                    for half in range(2):
                        n = 0
                        for k in range(KD):
                            for w, h in ((w_hi, 0), (w_hi, 1), (w_lo, 0)):
                                mm = pe.matmul(ps[u][:, half, :], w[:, u, k, :], hT[h][:, k, half * TH:(half + 1) * TH],
                                               start=(n == 0), stop=(n == 3 * KD - 1))
                                n += 1
                    mm.then_inc(mm_done, 1)

                def lru(j, q):
                    if q > 1:
                        return
                    if q == 0:
                        pe.wait_ge(w_cur_ready, j + 1)
                    wait_from(pe, sig_done, j * 4 + 2 * q)
                    for g in range(2):
                        mm = pe.matmul(ps_g[:, g, :], w_cur[:, g, :],
                                       xl[:, bass.ds(j, 1), q * TH:(q + 1) * TH].rearrange("p o n -> p (o n)"),
                                       start=True, stop=True)
                    mm.then_inc(lru_mm, 1)

                pairs(pe, 0, B_XBC, tile)
                pairs(pe, B_XBC, B_Z, tile)
                pe.wait_ge(conv_step, 4 * B_XBC)
                quads(pe, tile, lru)

            @block.scalar
            def _(act):
                act.wait_ge(sp_dve, 2)
                act.activation(s_abs[:], sp_in[:], ACT.Abs).then_inc(sp_act, 1)
                act.wait_ge(sp_act, 1)
                act.activation(s_e[:], s_abs[:], ACT.Exp, scale=-1.0).then_inc(sp_act, 1)
                act.wait_ge(sp_dve, 3)
                act.activation(sp_out[:], s_u[:], ACT.Ln).then_inc(sp_act, 1)

                def conv(i, u, seg):
                    act.wait_ge(mm_done, i + 1)
                    wait_from(act, conv_step, i * 4 - 4)
                    act.copy(pre[:, u, CW - 1:], ps[u][:].rearrange("p h n -> p (h n)")).then_inc(evac_done, 1)
                    if seg == 1:
                        act.wait_ge(conv_step, i * 4 + 4)
                        wait_from(act, stored[u], of_buffer(i - B_XBC, u) if isinstance(i, int) else of_buffer(i, u) - 8 * B_XBC)
                        act.activation(fin[:, u], acc[:, u], ACT.Silu).then_inc(silu_done, 1)
                        act.wait_ge(silu_done, i - B_XBC + 1)
                        act.dma_start(scratch["xbc"][bass.ds((i - B_XBC) * P, P), :], fin[:, u]).then_inc(stored[u], 16)

                def direct(i, u, seg):
                    act.wait_ge(mm_done, i + 1)
                    act.wait_ge(stored[u], of_buffer(i, u) - 8 * B_XBC)
                    act.activation(fin[:, u], ps[u][:].rearrange("p h n -> p (h n)"),
                                   ACT.Silu if seg == 2 else ACT.Sigmoid).then_inc(evac_done, 1)
                    act.wait_ge(evac_done, i + 1)
                    dest = scratch["z" if seg == 2 else "gates"]
                    act.dma_start(dest[bass.ds((i - SEGMENTS[seg][0]) * P, P), :], fin[:, u]).then_inc(stored[u], 16)

                def lru(j, q):
                    if q < 2:
                        act.wait_ge(lru_mm, j * 2 + q + 1)
                        if q == 0:
                            wait_from(act, ix_done, j)
                            wait_from(act, exp_done, j * 2)
                        alone(act, act_passed)
                        for g, (dst, b) in enumerate(((r_, "lru_ba"), (i_, "lru_bx"))):
                            act.activation(dst[:, q * TH:(q + 1) * TH], ps_g[:, g, :], ACT.Sigmoid,
                                           bias=cols[:, bass.ds(j + VEC[b], 1)]).then_inc(sig_done, 1)
                    if q == 1:
                        act.wait_ge(sig_done, j * 4 + 4)
                        wait_from(act, scan_done, j)
                        alone(act, act_passed)
                        act.activation(a_[:], r_[:], ACT.Exp, scale=sp_out[:, bass.ds(j, 1)]).then_inc(exp_done, 1)
                        act.activation(th[:], r_[:], ACT.Tanh, scale=sp_in[:, bass.ds(j, 1)]).then_inc(exp_done, 1)
                    if q == 2:
                        act.wait_ge(v_done, j * 2 + 2)
                        act.activation(sq[:], v_[:], ACT.Sqrt).then_inc(sqrt_done, 1)
                    if q == 3:
                        act.wait_ge(scan_done, j + 1)
                        act.dma_start(scratch["y_lru"][bass.ds(j * P, P), :], hl[:]).then_inc(h_stored, 16)

                pairs(act, 0, B_XBC, lambda i, u: conv(i, u, 0))
                pairs(act, B_XBC, B_Z, lambda i, u: conv(i, u, 1))
                act.wait_ge(sp_dve, 9)
                quads(act, direct, lru)
                act.wait_ge(h_stored, 16 * KD)
                for u in range(2):
                    act.wait_ge(stored[u], 8 * (TILES - B_XBC))

            @block.vector
            def _(dve):
                dve.tensor_scalar(sp_in[:, 0:KD], cols[:, VEC["lru_lambda"]:VEC["lru_lambda"] + KD], -1.0, None,
                                  ALU.mult).then_inc(sp_dve, 1)
                dve.wait_ge(dt_done, 1)
                dve.tensor_tensor(sp_in[:, KD:].rearrange("p (t h) -> p t h", h=SH),
                                  ps_dt[:, 0:TB * SH].rearrange("p (t h) -> p t h", h=SH),
                                  dt_bias[:].unsqueeze(1).to_broadcast([P, TB, SH]), ALU.add).then_inc(sp_dve, 1)
                dve.wait_ge(sp_act, 2)
                dve.tensor_scalar(s_u[:], s_e[:], 1.0, None, ALU.add).then_inc(sp_dve, 1)
                dve.wait_ge(sp_dve, 3)
                dve.scalar_tensor_tensor(s_c[:], s_u[:], -1.0, s_e[:], ALU.add, ALU.subtract).then_inc(sp_dve, 1)
                dve.reciprocal(s_abs[:], s_u[:]).then_inc(sp_dve, 1)
                dve.wait_ge(sp_dve, 5)
                dve.tensor_tensor(s_c[:], s_c[:], s_abs[:], ALU.mult).then_inc(sp_dve, 1)
                dve.wait_ge(sp_dve, 6)
                dve.wait_ge(sp_act, 3)
                dve.tensor_tensor(sp_out[:], sp_out[:], s_c[:], ALU.subtract).then_inc(sp_dve, 1)
                dve.wait_ge(sp_dve, 7)
                dve.scalar_tensor_tensor(sp_out[:], sp_in[:], 0.0, sp_out[:], ALU.max, ALU.add).then_inc(sp_dve, 1)
                dve.wait_ge(sp_dve, 8)
                dve.tensor_scalar(sp_in[:, 0:KD], sp_out[:, 0:KD], LRU_C, None, ALU.mult).then_inc(sp_dve, 1)
                dve.wait_ge(sp_dve, 9)
                dve.tensor_scalar(sp_out[:, 0:KD], sp_in[:, 0:KD], -1.0, None, ALU.mult).then_inc(sp_dve, 1)

                dve.wait_ge(zeroed, 2)

                def conv(i, u, seg):
                    w, b, first, n = (("lru_conv_w", "lru_conv_b", 0, KD) if seg == 0 else
                                      ("ssd_conv_w", "ssd_conv_b", B_XBC, XBC // P))
                    j = i - first
                    if seg == 0:
                        dst = xl[:, j, :] if isinstance(j, int) else xl[:, bass.ds(j, 1), :].rearrange("p o n -> p (o n)")
                    else:
                        dst = acc[:, u, :]
                        wait_from(dve, silu_done, j - 1)
                    dve.wait_ge(evac_done, i + 1)
                    col = lambda c: cols[:, bass.ds(j + c, 1)]
                    dve.tensor_scalar(dst, pre[:, u, CW - 1:], col(VEC[w] + (CW - 1) * n), col(VEC[b]),
                                      ALU.mult, ALU.add).then_inc(conv_step, 1)
                    for s in range(1, CW):
                        tap = CW - 1 - s
                        dve.wait_ge(conv_step, i * 4 + s)
                        dve.scalar_tensor_tensor(dst, pre[:, u, tap:tap + T], col(VEC[w] + tap * n), dst,
                                                 ALU.mult, ALU.add).then_inc(conv_step, 1)

                pairs(dve, 0, B_XBC, lambda i, u: conv(i, u, 0))
                conv(B_XBC, 0, 1)
                conv(B_XBC + 1, 1, 1)
                pairs(dve, B_XBC + 2, B_Z, lambda i, u: conv(i, u, 1))
                with dve.Fori(0, KD) as j:
                    dve.wait_ge(exp_done, j * 2 + 2)
                    dve.tensor_tensor(v_[:], a_[:], a_[:], ALU.mult).then_inc(v_done, 1)
                    dve.wait_ge(v_done, j * 2 + 1)
                    dve.scalar_tensor_tensor(v_[:], v_[:], 1.0, th[:], ALU.add, ALU.mult).then_inc(v_done, 1)
                    dve.wait_ge(sqrt_done, j + 1)
                    dve.wait_ge(ix_done, j + 1)
                    dve.tensor_tensor(v_[:], sq[:], ix[:], ALU.mult).then_inc(u_done, 1)
                    dve.wait_ge(u_done, j + 1)
                    dve.wait_ge(h_stored, j * 16)
                    dve.tensor_tensor_scan(hl[:], a_[:], v_[:], 0.0, ALU.mult, ALU.add).then_inc(scan_done, 1)


def ssd(m, inp, keep, scratch):
    nc = m.nc
    CH = T // P
    W = SHG * SP_
    WT = W // P
    cols = keep["cols"]
    ident, tri, mask, ones = keep["ident"], keep["tri"], keep["mask"], keep["ones"]
    dt_all = keep["sp_out"][:, KD:].rearrange("p (c h) -> p c h", h=SH)
    act_passed, pool_passed = keep["act_passed"], keep["pool_passed"]
    with ExitStack() as st:
        xbc = m.sb(st, "xbc_chunk", [P, 2, XBC // P, P])
        zc = m.sb(st, "z_chunk", [P, 2, SI // P, P])
        a_row = m.sb(st, "a_row", [P, SH])
        d_row = m.sb(st, "d_row", [P, SH])
        da = m.sb(st, "da", [P, CH, SH])
        da_cur = [m.sb(st, f"da_cur{i}", [P, 2, SH], F32R) for i in range(2)]
        tri_r = m.sb(st, "tri_r", [P, P], F32R)
        ident_b = m.sb(st, "ident_b", [P, P], BF16)
        neg_acs = m.sb(st, "neg_acs", [P, CH, SH])
        dec_out = m.sb(st, "decay_out", [P, CH, SH])
        dec_state = m.sb(st, "decay_state", [P, CH, SH])
        dec_chunk = m.sb(st, "decay_chunk", [P, CH, SH])
        state = m.sb(st, "state", [P, SG, W])
        state_dec = m.sb(st, "state_dec", [P, W])
        xt = m.sb(st, "x_tok", [P, 2, W])
        xdt = m.sb(st, "x_dt", [P, 2, W])
        xdd = m.sb(st, "x_dt_decay", [P, 2, W])
        x_d = m.sb(st, "x_skip", [P, 2, W])
        bt = m.sb(st, "b_tok", [P, 2, P])
        ell = m.sb(st, "decay_ls", [P, SHG, P])
        mm_ = m.sb(st, "cb_decay", [P, 2, SHG, P])
        yo = m.sb(st, "y_tok", [P, 2, W])
        sq = m.sb(st, "y_sq", [P, 2, W])
        y_ch = m.sb(st, "y_chunk", [P, 2, SI // P, P])
        ss_all = keep["y_squares"]
        ps_x = m.ps(st, "p2_x", [P, 512])
        ps_cb = m.ps(st, "p2_cb", [P, 512])
        ps_l = m.ps(st, "p2_l", [P, 2, 512])
        ps_o = m.ps(st, "p2_o", [P, 512])
        ps_s = m.ps(st, "p2_s", [P, 512])
        ps_y = m.ps(st, "p2_y", [P, 512])
        ps_q = m.ps(st, "p2_q", [P, 512])

        loaded = [m.sem(f"chunk_loaded{i}") for i in range(2)]
        rows_loaded, pre_dve, pre_act = m.sem("ssd_rows_loaded"), m.sem("ssd_pre_dve"), m.sem("ssd_pre_act")
        pre_pe, pre_pool = m.sem("ssd_pre_pe"), m.sem("ssd_pre_pool")
        cur_ready = m.sem("da_cur_ready")
        turned, spread = m.sem("ssd_turned"), m.sem("acs_spread")
        off_done, state_mm, y_done, ss_done = m.sem("y_off_done"), m.sem("state_mm"), m.sem("y_done"), m.sem("ss_done")
        xt_done, ell_done, sq_done, ss_kept = m.sem("x_tok_done"), m.sem("decay_ls_done"), m.sem("sq_done"), m.sem("ss_kept")
        bt_done, yo_done, state_done = m.sem("b_tok_done"), m.sem("y_tok_done"), m.sem("state_done")
        m_done, yg_done = m.sem("cb_decay_done"), m.sem("y_gated")
        pool_step = m.sem("ssd_pool_step")
        y_stored = [m.sem(f"y_stored{i}") for i in range(2)]

        LAST = CH * SG - 1

        def heads(ap):
            return ap.rearrange("p (h q) -> p h q", q=SP_)

        def per_head(ap, c, g):
            part = ap[:, bass.ds(c, 1), g * SHG:(g + 1) * SHG].rearrange("p o h -> p (o h)")
            return part.unsqueeze(2).to_broadcast([P, SHG, SP_])

        def token_slice(ap, lo, n, c):
            return ap[:, lo:lo + n, bass.ds(c * P, P)]

        with nc.Block() as block:
            @block.sync
            def _(sp):
                sp.dma_start(a_row[:], inp["ssd_a_log"][0].partition_broadcast(P)).then_inc(rows_loaded, 16)
                sp.dma_start(d_row[:], inp["ssd_d"][0].partition_broadcast(P)).then_inc(rows_loaded, 16)

                def load(c, u):
                    wait_from(sp, yg_done, c * 4 - 4)
                    sp.dma_start(xbc[:, u], scratch["xbc"].rearrange("(k p) t -> p k t", p=P)[:, :, bass.ds(c * P, P)]
                                 ).then_inc(loaded[u], 16)
                    sp.dma_start(zc[:, u], scratch["z"].rearrange("(k p) t -> p k t", p=P)[:, :, bass.ds(c * P, P)]
                                 ).then_inc(loaded[u], 16)

                def store(c, u):
                    sp.dma_start(scratch["y_ssd"].rearrange("(k p) t -> p k t", p=P)[:, :, bass.ds(c * P, P)], y_ch[:, u]
                                 ).then_inc(y_stored[u], 16)

                def chunk(c, u):
                    load(c, u)
                    if not isinstance(c, int) or c > 1:
                        store(c - 2, u)

                pairs(sp, 0, CH, chunk)
                for c in (CH - 2, CH - 1):
                    sp.wait_ge(yg_done, c * 4 + 4)
                    store(c, c % 2)
                for u in range(2):
                    sp.wait_ge(y_stored[u], 8 * CH)

            @block.gpsimd
            def _(pool):
                pool.memset(state[:], 0.0).then_inc(pre_pool, 1)
                pool.wait_ge(rows_loaded, 32)
                pool.wait_ge(pre_act, 4)
                pool.wait_ge(pre_pool, 1)

                def step(c, u, g):
                    n, v = c * 4 + g, g % 2
                    pool.wait_ge(xt_done, n + 1)
                    wait_from(pool, y_done, n - 1)
                    alone(pool, pool_passed)
                    pool.tensor_tensor(heads(xdt[:, v]), heads(xt[:, v]), per_head(dt_all, c, g), ALU.mult
                                       ).then_inc(pool_step, 1)
                    pool.wait_ge(pool_step, n * 4 + 1)
                    wait_from(pool, state_mm, n - 1)
                    alone(pool, pool_passed)
                    pool.tensor_tensor(heads(xdd[:, v]), heads(xdt[:, v]), per_head(dec_state, c, g), ALU.mult
                                       ).then_inc(pool_step, 1)
                    wait_from(pool, yo_done, n * 2 - 2)
                    pool.tensor_tensor(heads(x_d[:, v]), heads(xt[:, v]),
                                       d_row[:, g * SHG:(g + 1) * SHG].unsqueeze(2).to_broadcast([P, SHG, SP_]),
                                       ALU.mult).then_inc(pool_step, 1)
                    wait_from(pool, state_done, n)
                    alone(pool, pool_passed)
                    pool.tensor_tensor(heads(state_dec[:]), heads(state[:, g]), per_head(dec_chunk, c, g), ALU.mult
                                       ).then_inc(pool_step, 1)

                pairs(pool, 0, CH, lambda c, u: [step(c, u, g) for g in range(SG)])

            @block.tensor
            def _(pe):
                pe.wait_ge(pre_dve, 3)
                pe.matmul(ps_x[:, 0:CH * SH], tri[:], da[:].rearrange("p c h -> p (c h)"), start=True, stop=True
                          ).then_inc(pre_pe, 1)
                pe.matmul(ps_cb[:, 0:CH * SH], ones[:], da[:].rearrange("p c h -> p (c h)"), start=True, stop=True
                          ).then_inc(pre_pe, 1)
                pe.wait_ge(pre_act, 4)
                pe.wait_ge(pre_dve, 6)
                pe.wait_ge(pre_pool, 1)

                def turn(c, u, g):
                    n = c * 4 + g
                    if g == 0:
                        pe.wait_ge(loaded[u], of_buffer(c, u) * 2 + 32)
                        pe.wait_ge(cur_ready, c * 2 + 2)
                    wait_from(pe, xt_done, n)
                    for j in range(WT):
                        pe.transpose(ps_x[:, j * P:(j + 1) * P], xbc[:, u, g * WT + j, :], ident[:])
                    wait_from(pe, m_done, n)
                    b_tile, c_tile = xbc[:, u, SI // P + g, :], xbc[:, u, SI // P + SG + g, :]
                    pe.matmul(ps_cb[:, 0:P], b_tile, c_tile, start=True, stop=True, skip_group_check=True)
                    pe.transpose(ps_cb[:, P:2 * P], b_tile, ident[:]).then_inc(turned, 1)
                    wait_from(pe, ell_done, n * 8)
                    for q in range(2):
                        pe.matmul(ps_l[:, q, :], ident_b[:], mask[:].rearrange("p a b -> p (a b)"), start=True,
                                  stop=False, skip_group_check=True)
                        for h in range(SHG // 2):
                            head = g * SHG + q * (SHG // 2) + h
                            for part in range(2):
                                mm = pe.matmul(ps_l[:, q, h * P:(h + 1) * P],
                                               da_cur[u][:, part, head:head + 1].to_broadcast([P, P]), tri_r[:],
                                               start=False, stop=(part == 1), skip_group_check=True)
                    mm.then_inc(spread, 1)

                def multiply(c, u, g):
                    n, v = c * 4 + g, g % 2
                    wait_from(pe, state_done, n - 3)
                    wait_from(pe, yo_done, n * 2)
                    pe.matmul(ps_o[:], xbc[:, u, SI // P + SG + g, :], state[:, g], start=True, stop=True
                              ).then_inc(off_done, 1)
                    pe.wait_ge(bt_done, n + 1)
                    pe.wait_ge(pool_step, n * 4 + 2)
                    wait_from(pe, state_done, n)
                    pe.matmul(ps_s[:], bt[:, v], xdd[:, v], start=True, stop=True).then_inc(state_mm, 1)
                    pe.wait_ge(yo_done, n * 2 + 2)
                    wait_from(pe, yg_done, n)
                    for j in range(WT):
                        pe.matmul(ps_y[:, j * P:(j + 1) * P], yo[:, v, j * P:(j + 1) * P], ident[:],
                                  start=(j == 0), stop=False, skip_group_check=True)
                    pe.wait_ge(m_done, n + 1)
                    for h in range(SHG):
                        at = slice(SP_ * (h % 2), SP_ * (h % 2) + SP_)
                        mm = pe.matmul(ps_y[at, (h // 2) * P:(h // 2 + 1) * P], xdt[:, v, h * SP_:(h + 1) * SP_],
                                       mm_[:, v, h, :], start=False, stop=True, skip_group_check=True)
                    mm.then_inc(y_done, 1)

                def squares(n, g):
                    pe.wait_ge(sq_done, n + 1)
                    wait_from(pe, ss_kept, n)
                    for j in range(WT):
                        mm = pe.matmul(ps_q[:, 0:P], ones[:], sq[:, g % 2, j * P:(j + 1) * P],
                                       start=(j == 0), stop=(j == WT - 1))
                    mm.then_inc(ss_done, 1)

                def step(c, u, g):
                    turn(c, u, g)
                    if g > 0:
                        multiply(c, u, g - 1)
                    elif not isinstance(c, int) or c > 0:
                        multiply(c - 1, 1 - u, SG - 1)
                    if g > 1 or not isinstance(c, int) or c > 0:
                        squares(c * 4 + g - 2, (g - 2) % SG)

                pairs(pe, 0, CH, lambda c, u: [step(c, u, g) for g in range(SG)])
                multiply(CH - 1, (CH - 1) % 2, SG - 1)
                squares(LAST - 1, SG - 2)
                squares(LAST, SG - 1)

            @block.scalar
            def _(act):
                act.wait_ge(rows_loaded, 32)
                act.activation(a_row[:], a_row[:], ACT.Exp).then_inc(pre_act, 1)
                act.wait_ge(pre_dve, 5)
                act.activation(dec_out[:], neg_acs[:], ACT.Exp, scale=-1.0).then_inc(pre_act, 1)
                act.activation(dec_state[:], dec_state[:], ACT.Exp).then_inc(pre_act, 1)
                act.activation(dec_chunk[:], ps_cb[:, 0:CH * SH].rearrange("p (c h) -> p c h", h=SH), ACT.Exp
                               ).then_inc(pre_act, 1)

                def step(c, u, g):
                    n, v = c * 4 + g, g % 2
                    first = isinstance(c, int) and c == 0
                    act.wait_ge(turned, n + 1)
                    wait_from(act, pool_step, n * 4 - 4)
                    act.copy(xt[:, v], ps_x[:]).then_inc(xt_done, 1)
                    act.wait_ge(spread, n + 1)
                    wait_from(act, m_done, n)
                    alone(act, act_passed)
                    for h in range(SHG):
                        bias = neg_acs[:, bass.ds(c, 1), g * SHG + h:g * SHG + h + 1].rearrange("p a b -> p (a b)")
                        act.activation(ell[:, h, :], ps_l[:, h // 4, (h % 4) * P:(h % 4 + 1) * P], ACT.Exp, bias=bias
                                       ).then_inc(ell_done, 1)
                    if not first or g > 0:
                        square_of(c, u, g - 1) if g > 0 else square_of(c - 1, 1 - u, SG - 1)
                    if not first or g > 1:
                        keep_sum(c, g - 2) if g > 1 else keep_sum(c - 1, g + 2)

                def square_of(c, u, g):
                    n = c * 4 + g
                    act.wait_ge(yg_done, n + 1)
                    wait_from(act, ss_done, n - 1)
                    alone(act, act_passed)
                    act.activation(sq[:, g % 2].rearrange("p (k t) -> p k t", t=P), y_ch[:, u, g * WT:(g + 1) * WT, :],
                                   ACT.Square).then_inc(sq_done, 1)

                def keep_sum(c, g):
                    act.wait_ge(ss_done, c * 4 + g + 1)
                    alone(act, act_passed)
                    act.copy(token_slice(ss_all, g, 1, c).rearrange("p o t -> p (o t)"), ps_q[:, 0:P]).then_inc(ss_kept, 1)

                pairs(act, 0, CH, lambda c, u: [step(c, u, g) for g in range(SG)])
                square_of(CH - 1, (CH - 1) % 2, SG - 1)
                keep_sum(CH - 1, SG - 2)
                keep_sum(CH - 1, SG - 1)

            @block.vector
            def _(dve):
                dve.tensor_copy(tri_r[:], tri[:]).then_inc(pre_dve, 1)
                dve.tensor_copy(ident_b[:], ident[:]).then_inc(pre_dve, 1)
                dve.wait_ge(pre_act, 1)
                dve.scalar_tensor_tensor(da[:], dt_all, -1.0, a_row[:].unsqueeze(1).to_broadcast([P, CH, SH]),
                                         ALU.mult, ALU.mult).then_inc(pre_dve, 1)
                dve.wait_ge(pre_pe, 2)
                dve.tensor_scalar(neg_acs[:].rearrange("p c h -> p (c h)"), ps_x[:, 0:CH * SH], -1.0, None, ALU.mult
                                  ).then_inc(pre_dve, 1)
                dve.wait_ge(pre_dve, 4)
                dve.tensor_tensor(dec_state[:].rearrange("p c h -> p (c h)"), ps_cb[:, 0:CH * SH],
                                  neg_acs[:].rearrange("p c h -> p (c h)"), ALU.add).then_inc(pre_dve, 1)
                dve.wait_ge(pre_dve, 5)
                dve.engine_nop().then_inc(pre_dve, 1)
                dve.wait_ge(pre_act, 4)

                def da_hi_lo(c, u):
                    wait_from(dve, spread, c * 4 - 4)
                    src = da[:, bass.ds(c, 1), :].rearrange("p o h -> p (o h)")
                    dve.tensor_copy(da_cur[u][:, 0, :], src).then_inc(cur_ready, 1)
                    dve.wait_ge(cur_ready, c * 2 + 1)
                    dve.tensor_tensor(da_cur[u][:, 1, :], src, da_cur[u][:, 0, :].bitcast(F32), ALU.subtract
                                      ).then_inc(cur_ready, 1)

                def gate(c, u, g):
                    n = c * 4 + g
                    wait_from(dve, y_stored[u], of_buffer(c, u))
                    wait_from(dve, sq_done, n - 7)
                    dve.wait_ge(y_done, n + 1)
                    dve.tensor_tensor(y_ch[:, u, g * WT:(g + 1) * WT, :], ps_y[:].rearrange("p (k t) -> p k t", t=P),
                                      zc[:, u, g * WT:(g + 1) * WT, :], ALU.mult).then_inc(yg_done, 1)

                def add_up(c, u, g):
                    n, v = c * 4 + g, g % 2
                    dve.wait_ge(off_done, n + 1)
                    wait_from(dve, y_done, n - 1)
                    dve.tensor_tensor(heads(yo[:, v]), heads(ps_o[:]), per_head(dec_out, c, g), ALU.mult
                                      ).then_inc(yo_done, 1)
                    dve.wait_ge(yo_done, n * 2 + 1)
                    dve.wait_ge(pool_step, n * 4 + 4)
                    dve.tensor_tensor(yo[:, v], yo[:, v], x_d[:, v], ALU.add).then_inc(yo_done, 1)
                    dve.wait_ge(state_mm, n + 1)
                    dve.tensor_tensor(state[:, g], state_dec[:], ps_s[:], ALU.add).then_inc(state_done, 1)

                def step(c, u, g):
                    n, v = c * 4 + g, g % 2
                    first = isinstance(c, int) and c == 0
                    if g == 0 and not (isinstance(c, int) and c < 2):
                        da_hi_lo(c, u)
                    dve.wait_ge(turned, n + 1)
                    wait_from(dve, state_mm, n - 1)
                    dve.tensor_copy(bt[:, v], ps_cb[:, P:2 * P]).then_inc(bt_done, 1)
                    if not first or g > 0:
                        add_up(c, u, g - 1) if g > 0 else add_up(c - 1, 1 - u, SG - 1)
                    dve.wait_ge(ell_done, n * 8 + 8)
                    wait_from(dve, y_done, n - 1)
                    dve.tensor_tensor(mm_[:, v], ell[:], ps_cb[:, 0:P].unsqueeze(1).to_broadcast([P, SHG, P]),
                                      ALU.mult).then_inc(m_done, 1)
                    if not first or g > 0:
                        gate(c, u, g - 1) if g > 0 else gate(c - 1, 1 - u, SG - 1)

                da_hi_lo(0, 0)
                da_hi_lo(1, 1)
                pairs(dve, 0, CH, lambda c, u: [step(c, u, g) for g in range(SG)])
                add_up(CH - 1, (CH - 1) % 2, SG - 1)
                gate(CH - 1, (CH - 1) % 2, SG - 1)


def merge(m, inp, keep, scratch):
    nc = m.nc
    KINDS = 1 + SI // D
    STAGES = 2 * KINDS
    GW = SI // SG
    cols, rstd = keep["cols"], keep["y_squares"]
    acc, w_o = keep["merged"], keep["w_o"]
    pool_passed, act_passed = keep["pool_passed"], keep["act_passed"]
    with ExitStack() as st:
        y_raw = m.sb(st, "y_raw", [P, 4, TH])
        y_hi = [m.sb(st, f"y_hi{i}", [P, KD, TH], F32R) for i in range(2)]
        y_lo = [m.sb(st, f"y_lo{i}", [P, KD, TH], F32R) for i in range(2)]
        w_raw = m.sb(st, "wo_raw", [P, 2, KD, P])
        w_hi = m.sb(st, "wo_hi", [P, 4, KD, P], F32R)
        w_lo = m.sb(st, "wo_lo", [P, 2, KD, P], F32R)
        gates = m.sb(st, "gates_sb", [P, 4, TH])
        part = m.sb(st, "merge_part", [P, TH])
        eps = m.sb(st, "eps2", [P, 1])
        ps = [m.ps(st, f"p3_{j}", [P, TH]) for j in range(4)]

        y_loaded = [m.sem(f"y_loaded{i}") for i in range(4)]
        w_loaded = [m.sem(f"wo_loaded{i}") for i in range(2)]
        g_loaded = [m.sem(f"gates_loaded{i}") for i in range(4)]
        eps_set, root_done, rstd_done = m.sem("eps2_set"), m.sem("y_root_done"), m.sem("y_rstd_done")
        y_normed, y_hi_done, y_lo_done = m.sem("y_normed"), m.sem("y_hi_done"), m.sem("y_lo_done")
        hi_done, lo_done, mm_done = m.sem("wo_hi_done"), m.sem("wo_lo_done"), m.sem("merge_mm")
        part_done, add_done = m.sem("merge_parts"), m.sem("merge_sums")
        w_o_loaded, sp_passed = m.sem("w_o_loaded"), m.sem("sp_passed")

        def stages(eng, start, step, early=None):
            for q in range(STAGES):
                half, kind = divmod(q, KINDS)
                start(q, half, kind)
                with eng.Fori(0, KD // 4) as gg:
                    if early:
                        early(q, half, kind, gg, 0)
                    for j in range(4):
                        if early and j < 3:
                            early(q, half, kind, gg, j + 1)
                        step(q, half, kind, gg, j)

        def nothing(q, half, kind):
            pass

        with nc.Block() as block:
            @block.sync
            def _(sp):
                def load_y(q, n, j):
                    half, kind = divmod(q, KINDS)
                    src = scratch["y_lru"] if kind == 0 else scratch["y_ssd"]
                    row = n * P + (0 if kind == 0 else (kind - 1) * D)
                    sp.wait_ge(y_lo_done, q * KD + n + 1)
                    alone(sp, sp_passed)
                    sp.dma_start(y_raw[:, j], src[bass.ds(row, P), half * TH:(half + 1) * TH]).then_inc(y_loaded[j], 16)

                def step(q, half, kind, gg, j):
                    n, u = gg * 4 + j, j % 2
                    b = n + q * KD
                    if q + 1 < STAGES:
                        load_y(q + 1, n, j)
                    w = inp["w_lru_out"][0] if kind == 0 else inp["w_ssd_out"][0, (kind - 1) * D:kind * D, :]
                    sp.wait_ge(lo_done, b + 1)
                    alone(sp, sp_passed)
                    sp.dma_start(w_raw[:, u], w[:, bass.ds(n * P, P)].rearrange("(k p) n -> p k n", p=P)
                                 ).then_inc(w_loaded[u], 16)
                    sp.wait_ge(part_done, b + 1)
                    alone(sp, sp_passed)
                    sp.dma_start(gates[:, j], scratch["gates"][bass.ds(n * P + min(kind, 1) * D, P),
                                                               half * TH:(half + 1) * TH]).then_inc(g_loaded[j], 16)
                    if q == STAGES - 2:
                        sp.dma_start(w_o[:, bass.ds(n, 1), :].rearrange("p o d -> p (o d)").bitcast(F32),
                                     inp["w_o"][0, bass.ds(n * P, P), :]).then_inc(w_o_loaded, 16)

                for n in range(KD):
                    load_y(0, n, n % 4)
                stages(sp, nothing, step)
                sp.wait_ge(w_o_loaded, 16 * KD)

            @block.gpsimd
            def _(pool):
                pool.memset(eps[:], EPS).then_inc(eps_set, 1)
                ahead(pool, lo_done, by=2)

                def step(q, half, kind, gg, j):
                    u, b = j % 2, gg * 4 + (q * KD + j)
                    pool.wait_ge(hi_done, b + 1)
                    pool.wait_ge(mm_done, b + 3)
                    pool.tensor_tensor(w_lo[:, u], w_raw[:, u], w_hi[:, j].bitcast(F32), ALU.subtract).then_inc(lo_done, 1)

                stages(pool, nothing, step)

            @block.scalar
            def _(act):
                def high(q, n, j):
                    s = n + q * KD
                    half, kind = divmod(q, KINDS)
                    if kind == 0:
                        act.wait_ge(y_loaded[j], (s - j) * 4 + 16)
                    else:
                        act.wait_ge(y_normed, n + (q - 1 - half) * KD + 1)
                    alone(act, act_passed)
                    act.copy(y_hi[q % 2][:, bass.ds(n, 1), :].rearrange("p o t -> p (o t)"), y_raw[:, j]
                             ).then_inc(y_hi_done, 1)

                def cut(q, half, kind, gg, j):
                    u, b = j % 2, gg * 4 + (q * KD + j)
                    act.wait_ge(w_loaded[u], (b - u) * 8 + 16)
                    act.wait_ge(mm_done, b + 1)
                    act.copy(w_hi[:, j], w_raw[:, u]).then_inc(hi_done, 1)

                def step(q, half, kind, gg, j):
                    if q + 1 < STAGES:
                        high(q + 1, gg * 4 + j, j)

                def start(q, half, kind):
                    if q:
                        act.wait_ge(mm_done, q * KD + 4)
                        alone(act, act_passed)

                def roots(half):
                    p = rstd[:, :, half * TH:(half + 1) * TH]
                    act.activation(p, p, ACT.Sqrt, bias=eps[:], scale=1.0 / GW).then_inc(root_done, 1)

                act.wait_ge(eps_set, 1)
                roots(0)
                for n in range(KD):
                    high(0, n, n % 4)
                roots(1)
                stages(act, start, step, early=cut)

            @block.vector
            def _(dve):
                ahead(dve, y_lo_done, part_done, by=4)
                ahead(dve, add_done)

                def low(q, n, j):
                    s = n + q * KD
                    at = lambda ap: ap[q % 2][:, bass.ds(n, 1), :].rearrange("p o t -> p (o t)")
                    dve.wait_ge(y_hi_done, s + 1)
                    dve.tensor_tensor(at(y_lo), y_raw[:, j], at(y_hi).bitcast(F32), ALU.subtract).then_inc(y_lo_done, 1)

                LATER = ((0, 2), (1, 0), (1, 2))
                PIECE = TH // 4

                def invert(q, gg, j):
                    of, group = LATER[q]
                    at = slice(of * TH + j * PIECE, of * TH + (j + 1) * PIECE)
                    p = rstd[:, bass.ds(gg + group, 1), at].rearrange("p o t -> p (o t)")
                    dve.reciprocal(p, p).then_inc(rstd_done, 1)

                def start(q, half, kind):
                    if q in (1, 2, 3):
                        dve.wait_ge(rstd_done, 1 + KD * q)
                        alone(dve, keep["dve_passed"])

                def norm(q, half, kind, gg, j):
                    if q + 1 < STAGES and (kind + 1) % KINDS:
                        n = gg * 4 + j
                        s = n + (q + 1) * KD
                        w = n + (VEC["ssd_norm_w"] + kind * KD)
                        dve.wait_ge(y_loaded[j], (s - j) * 4 + 16)
                        dve.scalar_tensor_tensor(y_raw[:, j], y_raw[:, j], cols[:, bass.ds(w, 1)],
                                                 rstd[:, bass.ds(gg + 2 * kind, 1), half * TH:(half + 1) * TH].rearrange(
                                                     "p o t -> p (o t)"), ALU.mult, ALU.mult).then_inc(y_normed, 1)

                def step(q, half, kind, gg, j):
                    n, u = gg * 4 + j, j % 2
                    b = n + q * KD
                    into = acc[:, bass.ds(n, 1), half * TH:(half + 1) * TH].rearrange("p o t -> p (o t)")
                    dve.wait_ge(g_loaded[j], (b - j) * 4 + 16)
                    dve.wait_ge(mm_done, b + 5)
                    if kind == 0:
                        dve.tensor_tensor(into, ps[j][:], gates[:, j], ALU.mult).then_inc(part_done, 1)
                    else:
                        adds = n + (q - 1 - half) * KD
                        dve.wait_ge(add_done, adds + 1)
                        dve.tensor_tensor(part[:], ps[j][:], gates[:, j], ALU.mult).then_inc(part_done, 1)
                        dve.wait_ge(part_done, b + 5)
                        dve.tensor_tensor(into, part[:], into, ALU.add).then_inc(add_done, 1)
                    if q + 1 < STAGES:
                        low(q + 1, n, j)
                    if q < len(LATER):
                        invert(q, gg, j)

                dve.wait_ge(root_done, 1)
                dve.reciprocal(rstd[:, 0:2, 0:TH], rstd[:, 0:2, 0:TH]).then_inc(rstd_done, 1)
                for n in range(KD):
                    low(0, n, n % 4)
                dve.wait_ge(rstd_done, 1)
                dve.wait_ge(root_done, 2)
                alone(dve, keep["dve_passed"])
                stages(dve, start, step, early=norm)

            @block.tensor
            def _(pe):
                ahead(pe, mm_done, by=4)

                def start(q, half, kind):
                    pe.wait_ge(y_lo_done, (q + 1) * KD + 4)

                def step(q, half, kind, gg, j):
                    u, b = j % 2, gg * 4 + (q * KD + j)
                    pe.wait_ge(lo_done, b + 3)
                    pe.wait_ge(part_done, b + 1)
                    n = 0
                    for k in range(KD):
                        for w, y in ((w_hi[:, j], y_hi), (w_hi[:, j], y_lo), (w_lo[:, u], y_hi)):
                            mm = pe.matmul(ps[j][:], w[:, k, :], y[q % 2][:, k, :],
                                           start=(n == 0), stop=(n == 3 * KD - 1))
                            n += 1
                    mm.then_inc(mm_done, 1)

                stages(pe, start, step)


def post_mix(m, inp, keep, scratch):
    nc = m.nc
    ident, mod, gate_rows = keep["ident"], keep["mod"], keep["gate_rows"]
    DH = D // 2
    with ExitStack() as st:
        mg = [m.sb(st, "merged_hi", [P, KD, T], F32R), keep["merged_lo"]]
        wo = [m.sb(st, "w_o_hi", [P, KD, D], F32R), keep["w_o"]]
        x_in = m.sb(st, "x_res", [P, 2, D])
        junk = m.sb(st, "pm_square", [P, D])
        x1 = m.sb(st, "x1_sb", [P, 2, D])
        xn = m.sb(st, "x1_normed", [P, D])
        h2 = m.sb(st, "h2_sb", [P, 2, KD, P])
        stat = m.sb(st, "pm_stat", [P, TB, 2, 3])
        eps = m.sb(st, "eps3", [P, 1])
        ps_o = [m.ps(st, f"p3b_o{i}", [P, 2, DH]) for i in range(2)]
        ps_t = m.ps(st, "p3b_t", [P, 2, 4, P])

        hi_done, lo_done = m.sem("pm_hi_done"), [m.sem("merged_lo_done"), m.sem("w_o_lo_done")]
        x_loaded = [m.sem(f"x_res_loaded{i}") for i in range(2)]
        eps_set, mm_done, ssq_done, std_done = m.sem("eps3_set"), m.sem("w_o_done"), m.sem("pm_ssq"), m.sem("pm_std")
        rec_done, part_done, x1_done, xn_done = m.sem("pm_rstd"), m.sem("pm_part"), m.sem("x1_done"), m.sem("x1_normed_s")
        turned, h2_done = m.sem("x1_turned"), m.sem("h2_done")
        stored = [m.sem(f"pm_stored{i}") for i in range(2)]
        h_stored = [m.sem(f"h2_stored{i}") for i in range(2)]

        def slices():
            for n in range(2 * KD):
                which, k = n % 2, n // 2
                yield n, which, k

        def low(eng, which, k):
            hi, lo = (mg, wo)[which]
            eng.wait_ge(hi_done, 2 * k + which + 1)
            eng.tensor_tensor(lo[:, k, :], lo[:, k, :].bitcast(F32), hi[:, k, :].bitcast(F32), ALU.subtract
                              ).then_inc(lo_done[which], 1)

        with nc.Block() as block:
            @block.sync
            def _(sp):
                def load_x(t):
                    sp.dma_start(x_in[:, t % 2], inp["x"][0, t * P:(t + 1) * P, :]).then_inc(x_loaded[t % 2], 16)

                load_x(0)
                load_x(1)
                for t in range(TB):
                    sp.wait_ge(x1_done, t + 1)
                    sp.dma_start(scratch["x1"][t * P:(t + 1) * P, :], x1[:, t % 2]).then_inc(stored[t % 2], 16)
                    if t + 2 < TB:
                        load_x(t + 2)
                    sp.wait_ge(h2_done, KD * (t + 1))
                    sp.dma_start(scratch["h2"].rearrange("(k p) t -> p k t", p=P)[:, :, t * P:(t + 1) * P],
                                 h2[:, t % 2]).then_inc(h_stored[t % 2], 16)
                for u in range(2):
                    sp.wait_ge(stored[u], 8 * TB)
                    sp.wait_ge(h_stored[u], 8 * TB)

            @block.gpsimd
            def _(pool):
                pool.memset(eps[:], EPS).then_inc(eps_set, 1)
                for k in range(KD):
                    low(pool, 1, k)
                for t in range(TB):
                    pool.wait_ge(x_loaded[t % 2], 16 * (t // 2 + 1))
                    pool.wait_ge(part_done, t + 1)
                    pool.tensor_tensor(x1[:, t % 2], x1[:, t % 2], x_in[:, t % 2], ALU.add).then_inc(x1_done, 1)

            @block.scalar
            def _(act):
                act.wait_ge(eps_set, 1)
                for n, which, k in slices():
                    hi, lo = (mg, wo)[which]
                    act.copy(hi[:, k, :], lo[:, k, :].bitcast(F32)).then_inc(hi_done, 1)
                for t in range(TB):
                    for which in range(2):
                        s = 2 * t + which
                        if which == 0:
                            act.wait_ge(mm_done, t + 1)
                            src = ps_o[t % 2][:].rearrange("p a b -> p (a b)")
                        else:
                            act.wait_ge(x1_done, t + 1)
                            src = x1[:, t % 2]
                        act.activation(junk[:], src, ACT.Square, accum_out=stat[:, t, which, 0:1]).then_inc(ssq_done, 1)
                        act.wait_ge(ssq_done, s + 1)
                        act.activation(stat[:, t, which, 1:2], stat[:, t, which, 0:1], ACT.Sqrt, bias=eps[:],
                                       scale=1.0 / D).then_inc(std_done, 1)
                    act.wait_ge(turned, t + 1)
                    if t >= 2:
                        act.wait_ge(h_stored[t % 2], 16 * (t // 2))
                    for k in range(KD):
                        act.activation(h2[:, t % 2, k, :], ps_t[:, k // 4, k % 4, :], ACT.Identity,
                                       bias=mod[:, 2, k:k + 1], scale=mod[:, 3, k:k + 1]).then_inc(h2_done, 1)

            @block.vector
            def _(dve):
                for k in range(KD):
                    low(dve, 0, k)
                for t in range(TB):
                    for which in range(2):
                        dve.wait_ge(std_done, 2 * t + which + 1)
                        dve.reciprocal(stat[:, t, which, 2:3], stat[:, t, which, 1:2]).then_inc(rec_done, 1)
                        dve.wait_ge(rec_done, 2 * t + which + 1)
                        if which == 0:
                            if t >= 2:
                                dve.wait_ge(stored[t % 2], 16 * (t // 2))
                            dve.scalar_tensor_tensor(x1[:, t % 2], ps_o[t % 2][:].rearrange("p a b -> p (a b)"),
                                                     stat[:, t, 0, 2:3], gate_rows[:, 0, :], ALU.mult, ALU.mult
                                                     ).then_inc(part_done, 1)
                        else:
                            if t >= 1:
                                dve.wait_ge(turned, t)
                            dve.tensor_scalar(xn[:], x1[:, t % 2], stat[:, t, 1, 2:3], None, ALU.mult).then_inc(xn_done, 1)

            @block.tensor
            def _(pe):
                def turn(t):
                    pe.wait_ge(xn_done, t + 1)
                    if t >= 1:
                        pe.wait_ge(h2_done, KD * t)
                    for k in range(KD):
                        mm = pe.transpose(ps_t[:, k // 4, k % 4, :], xn[:, k * P:(k + 1) * P], ident[:])
                    mm.then_inc(turned, 1)

                for t in range(TB):
                    if t >= 2:
                        pe.wait_ge(part_done, t - 1)
                    for half in range(2):
                        n = 0
                        for k in range(KD):
                            if t == 0 and half == 0:
                                for which in range(2):
                                    pe.wait_ge(lo_done[which], k + 1)
                            for a, b in ((0, 0), (0, 1), (1, 0)):
                                mm = pe.matmul(ps_o[t % 2][:, half, :], mg[a][:, k, t * P:(t + 1) * P],
                                               wo[b][:, k, half * DH:(half + 1) * DH],
                                               start=(n == 0), stop=(n == 3 * KD - 1))
                                n += 1
                    mm.then_inc(mm_done, 1)
                    if t >= 1:
                        turn(t - 1)
                turn(TB - 1)


PH, PK, TOPK = 8, 128, 16
HP = 2 * PH
SEL_STEPS = 17


def selection(m, st, tag):
    b = {}
    for name, shape, dt in (("cand", [P, TOPK, TOPK], F32), ("cand_rest", [P, TOPK, TOPK], F32),
                            ("cv", [P, TOPK], F32), ("ci", [P, TOPK], U32), ("ij", [P, 2, TOPK], U32),
                            ("ij_f", [P, 2, TOPK], F32), ("neg_max", [P, 1], F32),
                            ("exp", [P, TOPK], F32), ("exp_sum", [P, 1], F32), ("inv", [P, 1], F32)):
        b[name] = m.sb(st, f"{tag}_{name}", shape, dt)
    b["hit"] = b["cand"]
    return b


def select_dve(dve, b, step, exp_done, keep, n, tb, h, out):
    sv, si, iota = keep["key_scores"], keep["key_index"], keep["iota_row"]
    base = n * SEL_STEPS

    def pick(ap, p):
        return ap[:, bass.ds(tb, 1), bass.ds(h * 2 + p, 1), :].rearrange("p a b k -> p (a b k)")

    def after(k):
        dve.wait_ge(step, base + (k + 1))

    flat = lambda ap: ap[:].rearrange("p a b -> p (a b)")
    after(0)
    dve.tensor_tensor(b["cand"][:], pick(sv, 0).unsqueeze(2).to_broadcast([P, TOPK, TOPK]),
                      pick(sv, 1).unsqueeze(1).to_broadcast([P, TOPK, TOPK]), ALU.add).then_inc(step, 1)
    after(1)
    alone(dve, keep["dve_passed"])
    dve.max(b["cv"][:, 0:8], flat(b["cand"])).then_inc(step, 1)
    after(2)
    alone(dve, keep["dve_passed"])
    dve.max_index(b["ci"][:, 0:8], b["cv"][:, 0:8], flat(b["cand"])).then_inc(step, 1)
    dve.match_replace(flat(b["cand_rest"]), b["cv"][:, 0:8], flat(b["cand"]), -3.0e38).then_inc(step, 1)
    dve.tensor_scalar(b["neg_max"][:], b["cv"][:, 0:1], -1.0, None, ALU.mult).then_inc(step, 1)
    after(5)
    alone(dve, keep["dve_passed"])
    dve.max(b["cv"][:, 8:16], flat(b["cand_rest"])).then_inc(step, 1)
    after(6)
    alone(dve, keep["dve_passed"])
    dve.max_index(b["ci"][:, 8:16], b["cv"][:, 8:16], flat(b["cand_rest"])).then_inc(step, 1)
    after(7)
    dve.tensor_scalar(b["ij"][:, 0], b["ci"][:], 4, None, ALU.logical_shift_right).then_inc(step, 1)
    dve.tensor_scalar(b["ij"][:, 1], b["ci"][:], TOPK - 1, None, ALU.bitwise_and).then_inc(step, 1)
    after(9)
    dve.tensor_copy(b["ij_f"][:], b["ij"][:]).then_inc(step, 1)
    for p in range(2):
        after(10 + 3 * p)
        dve.tensor_tensor(b["hit"][:], b["ij_f"][:, p].unsqueeze(2).to_broadcast([P, TOPK, TOPK]),
                          iota[:, 0:TOPK].unsqueeze(1).to_broadcast([P, TOPK, TOPK]), ALU.is_equal).then_inc(step, 1)
        after(11 + 3 * p)
        dve.tensor_tensor(b["hit"][:], b["hit"][:], pick(si, p).unsqueeze(1).to_broadcast([P, TOPK, TOPK]),
                          ALU.mult).then_inc(step, 1)
        after(12 + 3 * p)
        dve.reduce_sum(out(1 + p), b["hit"][:], axis=AX.X).then_inc(step, 1)
    dve.wait_ge(exp_done, n + 1)
    dve.reciprocal(b["inv"][:], b["exp_sum"][:]).then_inc(step, 1)
    after(17)
    dve.tensor_scalar(out(0), b["exp"][:], b["inv"][:], None, ALU.mult).then_inc(keep["sel_done"], 1)


def select_act(act, b, step, exp_done, n):
    act.wait_ge(step, n * SEL_STEPS + 7)
    act.activation(b["exp"][:], b["cv"][:], ACT.Exp, bias=b["neg_max"][:], accum_out=b["exp_sum"][:]
                   ).then_inc(exp_done, 1)


def expert_keep(m, stack, keep):
    keep["iota_row"] = m.sb(stack, "iota_row", [P, P])
    keep["key_scores"] = m.sb(stack, "key_scores", [P, TB, HP, TOPK])
    keep["key_index"] = m.sb(stack, "key_index", [P, TB, HP, TOPK])
    keep["chosen"] = m.sb(stack, "chosen", [P, 3, P])
    keep["h2T"] = [m.sb(stack, "h2T_hi", [P, KD, T], F32R), m.sb(stack, "h2T_lo", [P, KD, T], F32R)]
    keep["sel_done"] = m.kept_sem("sel_done")


def queries(m, inp, keep, scratch):
    nc = m.nc
    ident, h2 = keep["ident"], keep["h2T"]
    sv, si = keep["key_scores"], keep["key_index"]
    pool_passed = keep["pool_passed"]
    KEY_STEPS = 5 * TB + 2
    with ExitStack() as st:
        h_raw = m.sb(st, "h2_raw", [P, 2, T])
        iota_i = m.sb(st, "iota_i", [P, P], mybir.dt.int32)
        iota_set = m.sem("iota_set")
        keys = m.sb(st, "sub_keys", [P, HP, P])
        key_hi = m.sb(st, "keys_hi", [P, HP, P], F32R)
        key_lo = m.sb(st, "keys_lo", [P, HP, P], F32R)
        w_raw = m.sb(st, "wq_raw", [P, 2, KD, P])
        w_hi = m.sb(st, "wq_hi", [P, 2, KD, P], F32R)
        w_lo = m.sb(st, "wq_lo", [P, 2, KD, P], F32R)
        q_hi = m.sb(st, "q_hi", [P, T], F32R)
        q_lo = m.sb(st, "q_lo", [P, T], F32R)
        score = m.sb(st, "scores", [P, 2, TB, PK])
        rest = m.sb(st, "scores_rest", [P, TB, PK])
        top = m.sb(st, "key_top", [P, TB, TOPK])
        idx = m.sb(st, "key_idx", [P, TB, TOPK], U32)
        ps_q = m.ps(st, "p4_q", [P, 2, TH])
        ps_q2 = m.ps(st, "p4_q2", [P, 2, TH])
        ps_s = m.ps(st, "p4_s", [P, TB, PK])
        ps_k = m.ps(st, "p4_k", [P, 2, 4, P])
        ps_qs = (ps_q, ps_q2)
        sel = selection(m, st, "query_sel")

        h_loaded = [m.sem(f"h2_loaded{i}") for i in range(2)]
        h_hi, h_lo = m.sem("h2_hi_done"), m.sem("h2_lo_done")
        keys_loaded, keys_turned, keys_cut = m.sem("keys_loaded"), m.sem("keys_turned"), m.sem("keys_cut")
        w_loaded = [m.sem(f"wq_loaded{i}") for i in range(2)]
        hi_done, lo_done = m.sem("wq_hi_done"), m.sem("wq_lo_done")
        q_mm, q_hi_done, q_lo_done = m.sem("q_mm"), m.sem("q_hi_done"), m.sem("q_lo_done")
        s_mm, s_kept, key_step = m.sem("score_mm"), m.sem("scores_kept"), m.sem("key_step")
        step, exp_done = m.sem("q_sel_step"), m.sem("q_sel_exp")

        with nc.Block() as block:
            @block.sync
            def _(sp):
                sp.dma_start(keys[:], inp["peer_sub_keys"][0].rearrange("h p k d -> k (h p) d")).then_inc(keys_loaded, 16)
                for k in range(KD):
                    if k >= 2:
                        sp.wait_ge(h_lo, k - 1)
                    sp.dma_start(h_raw[:, k % 2], scratch["h2"][k * P:(k + 1) * P, :]).then_inc(h_loaded[k % 2], 16)

                def load(n, u):
                    wait_from(sp, lo_done, n - 1)
                    sp.dma_start(w_raw[:, u], inp["peer_wq"][0, :, bass.ds(n * P, P)].rearrange("(k p) n -> p k n", p=P)
                                 ).then_inc(w_loaded[u], 16)

                pairs(sp, 0, HP, load)

            @block.gpsimd
            def _(pool):
                pool.iota(iota_i[:], pattern=[[1, P]], base=0, channel_multiplier=0).then_inc(iota_set, 1)
                pool.wait_ge(iota_set, 1)
                pool.tensor_copy(keep["iota_row"][:], iota_i[:]).then_inc(iota_set, 1)

                def cut(n, u):
                    pool.wait_ge(w_loaded[u], of_buffer(n, u) + 16)
                    wait_from(pool, q_mm, n - 1)
                    alone(pool, pool_passed)
                    pool.tensor_copy(w_hi[:, u], w_raw[:, u]).then_inc(hi_done, 1)
                    pool.wait_ge(hi_done, n + 1)
                    pool.tensor_tensor(w_lo[:, u], w_raw[:, u], w_hi[:, u].bitcast(F32), ALU.subtract).then_inc(lo_done, 1)

                pairs(pool, 0, HP, cut)

            @block.tensor
            def _(pe):
                pe.wait_ge(keys_loaded, 16)
                for r in range(2):
                    if r:
                        pe.wait_ge(keys_cut, 2)
                    for j in range(HP // 2):
                        mm = pe.transpose(ps_k[:, j // 4, j % 4, :], keys[:, r * (HP // 2) + j, :], ident[:])
                    mm.then_inc(keys_turned, 1)
                pe.wait_ge(h_lo, KD)
                pe.wait_ge(keys_cut, 4)

                def query(n, u):
                    pe.wait_ge(lo_done, n + 1)
                    wait_from(pe, q_lo_done, n - 1)
                    for half in range(2):
                        j = 0
                        for k in range(KD):
                            for w, h in ((w_hi, 0), (w_hi, 1), (w_lo, 0)):
                                mm = pe.matmul(ps_qs[u][:, half, :], w[:, u, k, :], h2[h][:, k, half * TH:(half + 1) * TH],
                                               start=(j == 0), stop=(j == 3 * KD - 1))
                                j += 1
                    mm.then_inc(q_mm, 1)

                def scores(n):
                    pe.wait_ge(q_lo_done, n + 1)
                    wait_from(pe, s_kept, n)
                    for t in range(TB):
                        for j, (q, k) in enumerate(((q_hi, key_hi), (q_hi, key_lo), (q_lo, key_hi))):
                            mm = pe.matmul(ps_s[:, t, :], q[:, t * P:(t + 1) * P],
                                           k[:, bass.ds(n, 1), :].rearrange("p o k -> p (o k)"),
                                           start=(j == 0 and t % 4 == 0), stop=(j == 2), skip_group_check=True)
                    mm.then_inc(s_mm, 1)

                def tile(n, u):
                    query(n, u)
                    if not isinstance(n, int) or n > 0:
                        scores(n - 1)

                pairs(pe, 0, HP, tile)
                scores(HP - 1)

            @block.scalar
            def _(act):
                for k in range(KD):
                    act.wait_ge(h_loaded[k % 2], 16 * (k // 2 + 1))
                    act.copy(h2[0][:, k, :], h_raw[:, k % 2]).then_inc(h_hi, 1)
                for r in range(2):
                    act.wait_ge(keys_turned, r + 1)
                    act.copy(key_hi[:, r * 8:r * 8 + 8, :], ps_k[:].rearrange("p a b c -> p (a b) c")).then_inc(keys_cut, 1)
                    act.wait_ge(keys_cut, 2 * r + 2)

                def keep_scores(n, u):
                    act.wait_ge(s_mm, n + 1)
                    wait_from(act, key_step, (n - 1) * KEY_STEPS)
                    act.copy(score[:, u], ps_s[:]).then_inc(s_kept, 1)

                def tile(n, u):
                    act.wait_ge(q_mm, n + 1)
                    wait_from(act, s_mm, n)
                    act.copy(q_hi[:], ps_qs[u][:].rearrange("p a b -> p (a b)")).then_inc(q_hi_done, 1)
                    if not isinstance(n, int) or n > 0:
                        keep_scores(n - 1, 1 - u)

                tile(0, 0)
                tile(1, 1)
                with act.Fori(1, PH) as h:
                    tile(h * 2, 0)
                    select_act(act, sel, step, exp_done, h - 1)
                    tile(h * 2 + 1, 1)
                keep_scores(HP - 1, 1)
                select_act(act, sel, step, exp_done, PH - 1)

            @block.vector
            def _(dve):
                ahead(dve, step)
                for k in range(KD):
                    dve.wait_ge(h_hi, k + 1)
                    dve.tensor_tensor(h2[1][:, k, :], h_raw[:, k % 2], h2[0][:, k, :].bitcast(F32), ALU.subtract
                                      ).then_inc(h_lo, 1)
                for r in range(2):
                    dve.wait_ge(keys_cut, 2 * r + 1)
                    part = slice(r * 8, r * 8 + 8)
                    dve.tensor_tensor(key_lo[:, part, :], ps_k[:].rearrange("p a b c -> p (a b) c"),
                                      key_hi[:, part, :].bitcast(F32), ALU.subtract).then_inc(keys_cut, 1)
                dve.wait_ge(iota_set, 2)

                def q_low(n, u):
                    dve.wait_ge(q_hi_done, n + 1)
                    dve.tensor_tensor(q_lo[:], ps_qs[u][:].rearrange("p a b -> p (a b)"), q_hi[:].bitcast(F32),
                                      ALU.subtract).then_inc(q_lo_done, 1)

                def top_keys(n, u):
                    base = n * KEY_STEPS
                    dve.wait_ge(s_kept, n + 1)
                    wait_from(dve, key_step, base)
                    alone(dve, keep["dve_passed"])
                    at = lambda ap, t, lo: ap[:, t, lo:lo + 8]
                    for t in range(TB):
                        dve.max(at(top, t, 0), score[:, u, t, :]).then_inc(key_step, 1)
                    dve.wait_ge(key_step, base + TB)
                    alone(dve, keep["dve_passed"])
                    for t in range(TB):
                        dve.max_index(idx[:, t, 0:8], at(top, t, 0), score[:, u, t, :]).then_inc(key_step, 1)
                        dve.match_replace(rest[:, t, :], at(top, t, 0), score[:, u, t, :], -3.0e38).then_inc(key_step, 1)
                    dve.wait_ge(key_step, base + 3 * TB)
                    alone(dve, keep["dve_passed"])
                    for t in range(TB):
                        dve.max(at(top, t, 8), rest[:, t, :]).then_inc(key_step, 1)
                    dve.wait_ge(key_step, base + 4 * TB)
                    alone(dve, keep["dve_passed"])
                    for t in range(TB):
                        dve.max_index(idx[:, t, 8:16], at(top, t, 8), rest[:, t, :]).then_inc(key_step, 1)
                    dve.wait_ge(key_step, base + 5 * TB)
                    for dst, src in ((sv, top), (si, idx)):
                        dve.tensor_copy(dst[:, :, bass.ds(n, 1), :].rearrange("p t o k -> p t (o k)"), src[:]
                                        ).then_inc(key_step, 1)

                def choose(h):
                    dve.wait_ge(key_step, (h + 1) * (2 * KEY_STEPS))
                    select_dve(dve, sel, step, exp_done, keep, h, 0, h,
                               lambda which: keep["chosen"][:, which, bass.ds(h * TOPK, TOPK)])

                def tile(n, u):
                    q_low(n, u)
                    if not isinstance(n, int) or n > 0:
                        top_keys(n - 1, 1 - u)

                tile(0, 0)
                tile(1, 1)
                with dve.Fori(1, PH) as h:
                    tile(h * 2, 0)
                    choose(h - 1)
                    tile(h * 2 + 1, 1)
                top_keys(HP - 1, 1)
                choose(PH - 1)


QB = 4
STEP_TOKENS = 16
STEPS = P // STEP_TOKENS
WT = 64
E1 = 128


def experts_down(m, inp, keep, scratch):
    nc = m.nc
    ident, h2, chosen, iota = keep["ident"], keep["h2T"], keep["chosen"], keep["iota_row"]
    sel_done = keep["sel_done"]
    with ExitStack() as st:
        raw = m.sb(st, "down_raw", [P, 2, D])
        d_hi = m.sb(st, "downT_hi", [P, 2, KD, P], F32R)
        d_lo = m.sb(st, "downT_lo", [P, 2, KD, P], F32R)
        gu = m.sb(st, "gelu_out", [P, 2, T])
        hit1 = m.sb(st, "hit_first", [P, 2, QB, P])
        a_hi = m.sb(st, "first_hi", [P, 2, QB, P], F32R)
        a_lo = m.sb(st, "first_lo", [P, 2, QB, P], F32R)
        b_ = m.sb(st, "hit_second", [P, 2, QB, P], F32R)
        wt = m.sb(st, "weights_out", [P, 2, E1, WT])
        pick_g_hi = m.sb(st, "pick_weight_hi", [P, P], F32R)
        pick_g_lo = m.sb(st, "pick_weight_lo", [P, P], F32R)
        pick_1, pick_2 = m.sb(st, "pick_first", [P, P]), m.sb(st, "pick_second", [P, P])
        sel = selection(m, st, "down_sel")
        ps_d = m.ps(st, "p5_down", [P, KD, P])
        ps_u = [m.ps(st, f"p5_u{i}", [P, TH]) for i in range(2)]
        ps_w = [m.ps(st, f"p5_w{i}", [P, QB, P]) for i in range(4)]

        loaded = [m.sem(f"down_loaded{i}") for i in range(2)]
        turned = [m.sem(f"down_turned{i}") for i in range(2)]
        hi_done, lo_done = m.sem("down_hi_done"), m.sem("down_lo_done")
        u_done = [m.sem(f"u_done{i}") for i in range(2)]
        gelu_done = [m.sem(f"gelu_done{i}") for i in range(2)]
        gu_stored = [m.sem(f"gelu_stored{i}") for i in range(2)]
        picks_turned, picks_ready = m.sem("picks_turned"), m.sem("picks_ready")
        hit1_ready, b_ready = m.sem("hit_first_ready"), m.sem("hit_second_ready")
        a_hi_ready, a_lo_ready = m.sem("first_hi_ready"), m.sem("first_lo_ready")
        w_mm = [m.sem(f"weights_mm{i}") for i in range(2)]
        w_kept = [m.sem(f"weights_kept{i}") for i in range(4)]
        w_stored = [m.sem(f"weights_stored{i}") for i in range(2)]
        step, exp_done = m.sem("d_sel_step"), m.sem("d_sel_exp")
        pe_passed = m.sem("pe_passed")
        down = inp["peer_down"][0].rearrange("(e p) d -> e p d", p=P)
        PIECES = 8
        PE1 = E1 // PIECES

        def blocks(eng, block):
            with eng.Fori(0, TB - 1) as o:
                block(o, False)
            block(TB - 1, True)

        def steps(eng, o, last, step_of):
            half = STEPS // 2
            for hh in range(2):
                end = last and hh == 1
                with eng.Fori(0, half - end) as r:
                    step_of(hh, r, o * STEPS + hh * half + r, True)
            if last:
                step_of(1, half - 1, TB * STEPS - 1, False)

        with nc.Block() as block:
            @block.sync
            def _(sp):
                def load(s, u):
                    sp.wait_ge(turned[u], s + 1)
                    sp.dma_start(raw[:, u], down[bass.ds(s * 2 + u, 1)].rearrange("o p d -> (o p) d")
                                 ).then_inc(loaded[u], 16)

                def store_piece(tile, hh, piece):
                    sp.dma_start(scratch["w"][bass.ds(tile, 1), :, bass.ds(piece * PE1, PE1), :].rearrange("o p e t -> (o p) e t"),
                                 wt[:, hh, bass.ds(piece * PE1, PE1), :]).then_inc(w_stored[hh], 16)

                def halves(o, first):
                    for hh in range(2):
                        with sp.Fori(0, STEPS // 2) as r:
                            s = o * STEPS + hh * (STEPS // 2) + r
                            for u in range(2):
                                load(s, u)
                            if not (first and hh == 0):
                                for b in range(4):
                                    sp.wait_ge(w_kept[b], (o * 2 + hh) * (STEPS // 2) + 1)
                                for u in range(2):
                                    store_piece(o * 2 + hh - 1, 1 - hh, r * 2 + u)

                halves(0, True)
                with sp.Fori(1, TB) as o:
                    halves(o, False)
                for b in range(4):
                    sp.wait_ge(w_kept[b], TB * STEPS + 1)
                for piece in range(PIECES):
                    store_piece(2 * TB - 1, 1, piece)
                for hh in range(2):
                    sp.wait_ge(w_stored[hh], 16 * (PIECES * TB + 1))
                    sp.wait_ge(gu_stored[hh], 16 * (E1 // 2 + 1))

            @block.gpsimd
            def _(pool):
                ahead(pool, a_lo_ready)

                def first_low(hh, r, s, more):
                    for b in range(4):
                        pool.wait_ge(w_mm[b % 2], s * 2 + (b // 2 + 1))
                        pool.wait_ge(hit1_ready, s * 4 + (b + 1))
                        alone(pool, keep["pool_passed"])
                        at = bass.ds(r * STEP_TOKENS + (hh * WT + b * QB), QB)
                        pool.tensor_tensor(a_lo[:, b % 2], hit1[:, b % 2],
                                           pick_g_lo[:, at].unsqueeze(2).to_broadcast([P, QB, P]).bitcast(F32), ALU.mult
                                           ).then_inc(a_lo_ready, 1)

                def of_block(o, last):
                    pool.wait_ge(picks_ready, o * 4 + 4)
                    alone(pool, keep["pool_passed"])
                    steps(pool, o, last, first_low)

                blocks(pool, of_block)

            @block.tensor
            def _(pe):
                ahead(pe, *turned, *w_mm)

                def turn(s, u):
                    pe.wait_ge(loaded[u], s * 16 + 16)
                    pe.wait_ge(lo_done, s * 2 + (u + 1))
                    for k in range(KD):
                        mm = pe.transpose(ps_d[:, k, :], raw[:, u, k * P:(k + 1) * P], ident[:])
                    mm.then_inc(turned[u], 1)

                def products(s, u, half):
                    pe.wait_ge(lo_done, s * 2 + (u + 2))
                    pe.wait_ge(gelu_done[half], s * 2 + (u + 1))
                    n = 0
                    for k in range(KD):
                        for d, h in ((d_hi, 0), (d_hi, 1), (d_lo, 0)):
                            mm = pe.matmul(ps_u[half][:], d[:, u, k, :], h2[h][:, k, half * TH:(half + 1) * TH],
                                           start=(n == 0), stop=(n == 3 * KD - 1))
                            n += 1
                    mm.then_inc(u_done[half], 1)

                def weights(s, b):
                    pe.wait_ge(a_hi_ready, s * 4 + (b + 2))
                    pe.wait_ge(a_lo_ready, s * 4 + (b + 2))
                    pe.wait_ge(b_ready, s * 4 + (b + 2))
                    pe.wait_ge(w_kept[b], s + 1)
                    for t in range(QB):
                        for j, a in enumerate((a_hi, a_lo)):
                            mm = pe.matmul(ps_w[b][:, t, :], b_[:, b % 2, t, :], a[:, b % 2, t, :],
                                           start=(j == 0 and t == 0), stop=(j == 1), skip_group_check=True)
                    mm.then_inc(w_mm[b % 2], 1)

                def of_step(hh, r, s, more):
                    products(s, 0, 0)
                    turn(s, 1)
                    products(s, 0, 1)
                    weights(s, 0)
                    weights(s, 1)
                    products(s, 1, 0)
                    if more:
                        turn(s + 1, 0)
                    products(s, 1, 1)
                    weights(s, 2)
                    weights(s, 3)

                def of_block(o, last):
                    pe.wait_ge(sel_done, o * PH + PH)
                    pe.wait_ge(w_kept[0], o * STEPS + 1)
                    for j in range(3):
                        mm = pe.transpose(ps_w[0][:, j, :], chosen[:, j, :], ident[:])
                    mm.then_inc(picks_turned, 1)
                    pe.wait_ge(picks_ready, o * 4 + 4)
                    alone(pe, pe_passed)
                    steps(pe, o, last, of_step)

                turn(0, 0)
                blocks(pe, of_block)

            @block.scalar
            def _(act):
                ahead(act, *gelu_done, *w_kept)
                ahead(act, *gu_stored, *w_stored, by=16)

                def cut(s, u):
                    act.wait_ge(turned[u], s + 2)
                    act.copy(d_hi[:, u], ps_d[:]).then_inc(hi_done, 1)

                def gelu(s, u, half):
                    act.wait_ge(u_done[half], s * 2 + (u + 1))
                    act.wait_ge(gu_stored[u], s * 16 + 16)
                    act.activation(gu[:, u, half * TH:(half + 1) * TH], ps_u[half][:], ACT.Gelu).then_inc(gelu_done[half], 1)

                def store(s, u):
                    for half in range(2):
                        act.wait_ge(gelu_done[half], s * 2 + (u + 2))
                    act.dma_start(scratch["gu"][bass.ds(s * 2 + u, 1)].rearrange("o p t -> (o p) t"), gu[:, u]
                                  ).then_inc(gu_stored[u], 16)

                def keep_weights(hh, r, s, b):
                    act.wait_ge(w_mm[b % 2], s * 2 + (b // 2 + 2))
                    alone(act, keep["act_passed"])
                    act.copy(wt[:, hh, :, bass.ds(r * STEP_TOKENS + b * QB, QB)],
                             ps_w[b][:].rearrange("p t e -> p e t")).then_inc(w_kept[b], 1)

                def of_block(o, last):
                    def of_step(hh, r, s, more):
                        gelu(s, 0, 0)
                        cut(s, 1)
                        gelu(s, 0, 1)
                        store(s, 0)
                        act.wait_ge(w_stored[hh], o * (16 * PIECES) + 16)
                        keep_weights(hh, r, s, 0)
                        keep_weights(hh, r, s, 1)
                        if not last:
                            select_act(act, sel, step, exp_done, s)
                        gelu(s, 1, 0)
                        if more:
                            cut(s + 1, 0)
                        gelu(s, 1, 1)
                        store(s, 1)
                        keep_weights(hh, r, s, 2)
                        keep_weights(hh, r, s, 3)

                    steps(act, o, last, of_step)

                cut(0, 0)
                blocks(act, of_block)

            @block.vector
            def _(dve):
                ahead(dve, lo_done, b_ready, a_hi_ready, step)

                def low(s, u):
                    dve.wait_ge(hi_done, s * 2 + (u + 1))
                    dve.tensor_tensor(d_lo[:, u], ps_d[:], d_hi[:, u].bitcast(F32), ALU.subtract).then_inc(lo_done, 1)

                def first(hh, r, s, b):
                    at = bass.ds(r * STEP_TOKENS + (hh * WT + b * QB), QB)
                    wide = lambda ap: ap[:, at].unsqueeze(2).to_broadcast([P, QB, P])
                    keys = iota[:].unsqueeze(1).to_broadcast([P, QB, P])
                    dve.wait_ge(w_mm[b % 2], s * 2 + (b // 2 + 1))
                    dve.tensor_tensor(hit1[:, b % 2], wide(pick_1), keys, ALU.is_equal).then_inc(hit1_ready, 1)
                    dve.tensor_tensor(b_[:, b % 2], wide(pick_2), keys, ALU.is_equal).then_inc(b_ready, 1)
                    dve.wait_ge(hit1_ready, s * 4 + (b + 1))
                    dve.tensor_tensor(a_hi[:, b % 2], hit1[:, b % 2], wide(pick_g_hi).bitcast(F32), ALU.mult
                                      ).then_inc(a_hi_ready, 1)

                def of_block(o, last):
                    dve.wait_ge(picks_turned, o + 1)
                    for ready in (a_lo_ready, a_hi_ready, b_ready):
                        dve.wait_ge(ready, o * (4 * STEPS) + 1)
                    dve.tensor_copy(pick_g_hi[:], ps_w[0][:, 0, :]).then_inc(picks_ready, 1)
                    dve.tensor_copy(pick_1[:], ps_w[0][:, 1, :]).then_inc(picks_ready, 1)
                    dve.tensor_copy(pick_2[:], ps_w[0][:, 2, :]).then_inc(picks_ready, 1)
                    dve.wait_ge(picks_ready, o * 4 + 3)
                    dve.tensor_tensor(pick_g_lo[:], ps_w[0][:, 0, :], pick_g_hi[:].bitcast(F32), ALU.subtract
                                      ).then_inc(picks_ready, 1)
                    dve.wait_ge(picks_ready, o * 4 + 4)
                    alone(dve, keep["dve_passed"])

                    def of_step(hh, r, s, more):
                        first(hh, r, s, 0)
                        first(hh, r, s, 1)
                        low(s, 1)
                        if not last:
                            h = r + hh * (STEPS // 2)
                            select_dve(dve, sel, step, exp_done, keep, s, o + 1, h,
                                       lambda which: chosen[:, which, bass.ds(h * TOPK, TOPK)])
                        first(hh, r, s, 2)
                        first(hh, r, s, 3)
                        if more:
                            low(s + 1, 0)

                    steps(dve, o, last, of_step)

                low(0, 0)
                blocks(dve, of_block)


GT = 4


def experts_up(m, inp, keep, scratch, out):
    nc = m.nc
    gate_rows = keep["gate_rows"]
    GROUPS = E1 // GT
    SLOTS = 2 * TB
    with ExitStack() as st:
        up_raw = m.sb(st, "up_raw", [P, 2, D])
        gu = m.sb(st, "gelu_in", [P, 2, T])
        w = m.sb(st, "weights_in", [P, 2, T])
        g_hi = m.sb(st, "coef_hi", [P, 2, GT, T], F32R)
        g_lo = m.sb(st, "coef_lo", [P, 2, GT, T], F32R)
        up_hi = m.sb(st, "up_hi", [P, 2, GT, D], F32R)
        up_lo = m.sb(st, "up_lo", [P, 2, GT, D], F32R)
        acc = m.sb(st, "y_acc", [P, TB, D])
        x1 = m.sb(st, "x1_in", [P, 2, D])
        stat = m.sb(st, "y_stat", [P, TB, 3])
        eps = m.sb(st, "eps6", [P, 1])
        ps_y = [m.ps(st, f"p6_y{i}", [P, TH]) for i in range(8)]

        gu_loaded = [m.sem(f"gelu_loaded{i}") for i in range(2)]
        w_loaded = [m.sem(f"weights_loaded{i}") for i in range(2)]
        up_loaded = [m.sem(f"up_loaded{i}") for i in range(2)]
        coef_ready, g_hi_done, g_lo_done = m.sem("coef_ready"), m.sem("coef_hi_done"), m.sem("coef_lo_done")
        up_hi_done, up_lo_done = m.sem("up_hi_done"), m.sem("up_lo_done")
        acc_zeroed, y_mm, added = m.sem("acc_zeroed"), m.sem("y_mm"), m.sem("y_added")
        x1_loaded = [m.sem(f"x1_in_loaded{i}") for i in range(2)]
        ssq, std, rstd, scaled, summed = (m.sem(f"y_{n}") for n in ("ssq", "std", "rstd", "scaled", "summed"))
        out_stored = m.sem("out_stored")
        up = inp["peer_up"][0].rearrange("(e p) d -> e p d", p=P)

        with nc.Block() as block:
            @block.sync
            def _(sp):
                def load(g, v):
                    for j in range(GT):
                        n, u = g * GT + j, j % 2
                        wait_from(sp, up_lo_done, n - 1)
                        sp.dma_start(up_raw[:, u], up[bass.ds(n, 1)].rearrange("o p d -> (o p) d")
                                     ).then_inc(up_loaded[u], 16)
                        wait_from(sp, g_lo_done, n - 1)
                        sp.dma_start(gu[:, u], scratch["gu"][bass.ds(n, 1)].rearrange("o p t -> (o p) t")
                                     ).then_inc(gu_loaded[u], 16)
                        sp.dma_start(w[:, u].rearrange("p (h t) -> p h t", t=WT),
                                     scratch["w"][:, :, bass.ds(n, 1), :].rearrange("h p o t -> p (h o) t")
                                     ).then_inc(w_loaded[u], 16)

                pairs(sp, 0, GROUPS, load)
                for t in range(TB):
                    if t >= 2:
                        sp.wait_ge(summed, t - 1)
                    sp.dma_start(x1[:, t % 2], scratch["x1"][t * P:(t + 1) * P, :]).then_inc(x1_loaded[t % 2], 16)
                    if t >= 1:
                        sp.wait_ge(summed, t)
                        sp.dma_start(out[0, (t - 1) * P:t * P, :], acc[:, t - 1, :]).then_inc(out_stored, 16)
                sp.wait_ge(summed, TB)
                sp.dma_start(out[0, (TB - 1) * P:TB * P, :], acc[:, TB - 1, :]).then_inc(out_stored, 16)
                sp.wait_ge(out_stored, 16 * TB)

            @block.gpsimd
            def _(pool):
                pool.memset(acc[:], 0.0).then_inc(acc_zeroed, 1)
                pool.memset(eps[:], EPS).then_inc(acc_zeroed, 1)

                def cut(g, v):
                    for j in range(GT):
                        n, u = g * GT + j, j % 2
                        pool.wait_ge(up_hi_done, n + 1)
                        pool.tensor_tensor(up_lo[:, v, j, :], up_raw[:, u], up_hi[:, v, j, :].bitcast(F32),
                                           ALU.subtract).then_inc(up_lo_done, 1)

                pairs(pool, 0, GROUPS, cut)

            @block.scalar
            def _(act):
                def cut(g, v):
                    wait_from(act, y_mm, (g - 1) * SLOTS)
                    for j in range(GT):
                        n, u = g * GT + j, j % 2
                        loads = g * (8 * GT) + 16 * (j // 2 + 1)
                        act.wait_ge(up_loaded[u], loads)
                        act.copy(up_hi[:, v, j, :], up_raw[:, u]).then_inc(up_hi_done, 1)
                        act.wait_ge(coef_ready, n + 1)
                        act.copy(g_hi[:, v, j, :], gu[:, u]).then_inc(g_hi_done, 1)

                pairs(act, 0, GROUPS, cut)
                act.wait_ge(acc_zeroed, 2)
                for t in range(TB):
                    act.wait_ge(added, SLOTS * (GROUPS - 1) + 2 * t + 2)
                    if t >= 1:
                        act.wait_ge(ssq, t)
                    act.activation(gu[:, 0], acc[:, t, :], ACT.Square, accum_out=stat[:, t, 0:1]).then_inc(ssq, 1)
                    act.wait_ge(ssq, t + 1)
                    act.activation(stat[:, t, 1:2], stat[:, t, 0:1], ACT.Sqrt, bias=eps[:], scale=1.0 / D).then_inc(std, 1)

            @block.vector
            def _(dve):
                def coef(g, v, j):
                    n, u = g * GT + j, j % 2
                    loads = g * (8 * GT) + 16 * (j // 2 + 1)
                    dve.wait_ge(gu_loaded[u], loads)
                    dve.wait_ge(w_loaded[u], loads)
                    dve.tensor_tensor(gu[:, u], gu[:, u], w[:, u], ALU.mult).then_inc(coef_ready, 1)
                    dve.wait_ge(g_hi_done, n + 1)
                    dve.tensor_tensor(g_lo[:, v, j, :], gu[:, u], g_hi[:, v, j, :].bitcast(F32), ALU.subtract
                                      ).then_inc(g_lo_done, 1)

                def add(g, s):
                    dve.wait_ge(y_mm, g * SLOTS + (s + 1))
                    wait_from(dve, added, g * SLOTS + (s + 1 - SLOTS))
                    part = acc[:, s // 2, (s % 2) * TH:(s % 2 + 1) * TH]
                    dve.tensor_tensor(part, ps_y[s % 8][:], part, ALU.add).then_inc(added, 1)

                def group(g, v):
                    for j in range(GT):
                        coef(g, v, j)
                        if not isinstance(g, int) or g > 0:
                            for s in range(4 * j, 4 * j + 4):
                                add(g - 1, s)

                dve.wait_ge(acc_zeroed, 1)
                pairs(dve, 0, GROUPS, group)

                def finish(t):
                    dve.wait_ge(std, t + 1)
                    dve.reciprocal(stat[:, t, 2:3], stat[:, t, 1:2]).then_inc(rstd, 1)
                    dve.wait_ge(rstd, t + 1)
                    dve.scalar_tensor_tensor(acc[:, t, :], acc[:, t, :], stat[:, t, 2:3], gate_rows[:, 1, :],
                                             ALU.mult, ALU.mult).then_inc(scaled, 1)
                    dve.wait_ge(scaled, t + 1)
                    dve.wait_ge(x1_loaded[t % 2], 16 * (t // 2 + 1))
                    dve.tensor_tensor(acc[:, t, :], acc[:, t, :], x1[:, t % 2], ALU.add).then_inc(summed, 1)

                for s in range(SLOTS):
                    add(GROUPS - 1, s)
                    if s % 2 and s > 1:
                        finish(s // 2 - 1)
                finish(TB - 1)

            @block.tensor
            def _(pe):
                def group(g, v):
                    pe.wait_ge(g_lo_done, g * GT + GT)
                    pe.wait_ge(up_lo_done, g * GT + GT)
                    for s in range(SLOTS):
                        t, half = divmod(s, 2)
                        wait_from(pe, added, g * SLOTS + (s - 7))
                        n = 0
                        for j in range(GT):
                            for a, b in ((g_hi, up_hi), (g_hi, up_lo), (g_lo, up_hi)):
                                mm = pe.matmul(ps_y[s % 8][:], a[:, v, j, t * P:(t + 1) * P],
                                               b[:, v, j, half * TH:(half + 1) * TH],
                                               start=(n == 0), stop=(n == 3 * GT - 1))
                                n += 1
                        mm.then_inc(y_mm, 1)

                pairs(pe, 0, GROUPS, group)


def build(nc, inp, out):
    scratch = {}
    for name, shape in (("xbc", [XBC, T]), ("z", [SI, T]), ("gates", [2 * D, T]), ("y_lru", [D, T]), ("y_ssd", [SI, T]),
                        ("x1", [T, D]), ("h2", [D, T]), ("gu", [E1, P, T]),
                        ("w", [T // WT, P, E1, WT])):
        scratch[name] = nc.dram_tensor(f"scratch_{name}", shape, F32, kind="Internal").ap()
    with ExitStack() as stack:
        m = Machine(nc, stack)
        keep = {
            "ident": m.sb(stack, "ident", [P, P]),
            "mod": m.sb(stack, "mod", [P, 4, KD]),
            "gate_rows": m.sb(stack, "gate_rows", [P, 2, D]),
            "pool_passed": m.kept_sem("pool_passed"),
            "act_passed": m.kept_sem("act_passed"),
            "dve_passed": m.kept_sem("dve_passed"),
            "consts_ready": m.kept_sem("consts_ready"),
        }
        with ExitStack() as mix:
            keep["cols"] = m.sb(mix, "cols", [P, 272])
            keep["tri"] = m.sb(mix, "tri", [P, P])
            keep["mask"] = m.sb(mix, "mask", [P, 4, P], BF16)
            keep["ones"] = m.sb(mix, "ones", [P, P])
            keep["sp_in"] = m.sb(mix, "softplus_in", [P, KD + TB * SH])
            keep["sp_out"] = m.sb(mix, "softplus_out", [P, KD + TB * SH])
            with ExitStack() as project:
                keep["hT"] = [m.sb(project, "hT_hi", [P, KD, T], F32R), m.sb(project, "hT_lo", [P, KD, T], F32R)]
                vectors_and_norm(m, inp, keep)
                m.end_phase()
                project_in(m, inp, keep, scratch)
                m.end_phase()
            keep["y_squares"] = m.sb(mix, "y_squares", [P, SG, T])
            ssd(m, inp, keep, scratch)
            m.end_phase()
            with ExitStack() as merged:
                keep["merged_lo"] = m.sb(merged, "merged_lo", [P, KD, T], F32R)
                keep["merged"] = keep["merged_lo"][:].bitcast(F32)
                keep["w_o"] = m.sb(merged, "w_o_lo", [P, KD, D], F32R)
                merge(m, inp, keep, scratch)
                m.end_phase()
                post_mix(m, inp, keep, scratch)
                m.end_phase()
        with ExitStack() as picks:
            expert_keep(m, picks, keep)
            queries(m, inp, keep, scratch)
            m.end_phase()
            experts_down(m, inp, keep, scratch)
            m.end_phase()
        experts_up(m, inp, keep, scratch, out)


_INS = ["x", "c", "w_ada", "b_ada", "norm_pre_mix", "norm_post_mix", "norm_pre_ffn", "norm_post_ffn", "w_in",
        "lru_conv_w", "lru_conv_b", "lru_wa", "lru_ba", "lru_wx", "lru_bx", "lru_lambda", "ssd_conv_w", "ssd_conv_b",
        "ssd_dt_bias", "ssd_a_log", "ssd_d", "ssd_norm_w", "w_lru_out", "w_ssd_out", "w_o", "peer_wq",
        "peer_sub_keys", "peer_down", "peer_up"]
_OUTS = [((1, T, D), "float32")]


def kernel(**inputs):
    import numpy as _np
    import concourse.bacc as _bacc
    from concourse import mybir as _mybir
    from concourse.bass_utils import run_bass_kernel_spmd as _run

    nc = _bacc.Bacc("TRN2", target_bir_lowering=False, num_devices=1)
    arrays, inp = {}, {}
    for name in _INS:
        a = _np.ascontiguousarray(inputs[name])
        arrays[f"in_{name}_dram"] = a
        inp[name] = nc.dram_tensor(f"in_{name}_dram", a.shape, _mybir.dt.from_np(a.dtype), kind="ExternalInput").ap()
    shape, dtype = _OUTS[0]
    out = nc.dram_tensor("out_0_dram", shape, _mybir.dt.from_np(_np.dtype(dtype)), kind="ExternalOutput").ap()
    build(nc, inp, out)
    r = _run(nc, [arrays], core_ids=[0])
    return r.results[0]["out_0_dram"]
```

```python
from contextlib import ExitStack

import concourse.bass as bass
from concourse import mybir

F32 = mybir.dt.float32
F32R = mybir.dt.float32r
BF16 = mybir.dt.bfloat16
U32 = mybir.dt.uint32
ALU = mybir.AluOpType
ACT = mybir.ActivationFunctionType
AX = mybir.AxisListType

P = 128
T = 1024
TB = T // P
TH = 512
D = 1024
KD = D // P
CW = 4
EPS = 1e-6
LRU_C = 8.0
SI = 2048
SH = 32
SG = 4
SHG = SH // SG
SP_ = SI // SH
XBC = SI + 2 * SG * P
COL_LRU, COL_Z, COL_XBC = 0, D, D + SI
COL_DT = COL_XBC + XBC
COL_GATE = COL_DT + SH
NEG = -30000.0

VEC = {}
_row = 0
for _name, _n in (("b_ada", 48), ("norm_pre_mix", 8), ("norm_pre_ffn", 8), ("lru_conv_w", 32),
                  ("lru_conv_b", 8), ("lru_ba", 8), ("lru_bx", 8), ("lru_lambda", 8),
                  ("ssd_conv_w", 96), ("ssd_conv_b", 24), ("ssd_norm_w", 16), ("c", 8)):
    VEC[_name] = _row
    _row += _n
VEC_TILES = ((0, 128), (128, 120), (248, 24))
assert _row == 272 and VEC["ssd_norm_w"] == 248


class Machine:

    def __init__(self, nc, stack):
        self.nc, self.stack = nc, stack
        self.phase_sems = []

    def sb(self, stack, name, shape, dt=F32):
        return stack.enter_context(self.nc.sbuf_tensor(name, shape, dt))

    def ps(self, stack, name, shape, dt=F32):
        return stack.enter_context(self.nc.psum_tensor(name, shape, dt))

    def kept_sem(self, name):
        return self.stack.enter_context(self.nc.semaphore(name))

    def sem(self, name):
        self.phase_sems.append(self.nc.alloc_semaphore(name))
        return self.phase_sems[-1]

    def end_phase(self):
        self.nc.all_engine_barrier()
        self.nc.clear_and_free_semaphores(self.phase_sems)
        self.nc.all_engine_barrier()
        self.phase_sems = []


def vectors_and_norm(m, inp, keep):
    nc = m.nc
    with ExitStack() as st:
        rows = m.sb(st, "vec_rows", [P, 3, P])
        x_in = m.sb(st, "x_in", [P, TB, D])
        junk = m.sb(st, "square_out", [P, D])
        w_ada = m.sb(st, "w_ada_sb", [P, 4, KD, TH])
        diag = m.sb(st, "mod_diag", [P, 4, P])
        ssq = m.sb(st, "x_ssq", [P, TB])
        std = m.sb(st, "x_std", [P, TB])
        rstd = m.sb(st, "x_rstd", [P, TB])
        h_full = m.sb(st, "h_full", [P, 2, TH])
        mult1 = m.sb(st, "mult1", [P, KD])
        eps = m.sb(st, "eps0", [P, 1])
        c_cols = m.sb(st, "c_cols", [P, KD])
        c_wide = m.sb(st, "c_wide", [P, KD, P])
        norm_rows = m.sb(st, "norm_rows", [P, 2, D])
        ps_a = [m.ps(st, f"p0_a{i}", [P, 512]) for i in range(4)]
        ps_r = [m.ps(st, f"p0_r{i}", [P, TH]) for i in range(4)]
        ident, tri, mask, ones = keep["ident"], keep["tri"], keep["mask"], keep["ones"]
        cols, mod, gate_rows = keep["cols"], keep["mod"], keep["gate_rows"]
        hT = keep["hT"]

        consts_ready = keep["consts_ready"]
        consts_set = m.sem("consts_set")
        vec_loaded = m.sem("vec_loaded")
        row_vecs_loaded = m.sem("row_vecs_loaded")
        x_loaded = [m.sem(f"x_loaded{i}") for i in range(4)]
        ada_loaded = [m.sem(f"ada_loaded{i}") for i in range(4)]
        cols_turned = m.sem("cols_turned")
        cols_ready = m.sem("cols_ready")
        c_ready = m.sem("c_ready")
        ssq_ready = m.sem("ssq_ready")
        std_ready = m.sem("std_ready")
        rstd_ready = m.sem("rstd_ready")
        xn_ready = m.sem("xn_ready")
        piece_done = m.sem("mod_piece_done")
        piece_out = m.sem("mod_piece_out")
        mod_step = m.sem("mod_step")
        mult_ready = m.sem("mult_ready")
        turned = m.sem("x_turned")
        full_ready = m.sem("h_full_ready")
        hi_ready = m.sem("h_hi_ready")
        lo_ready = m.sem("h_lo_ready")
        rows_ready = m.sem("gate_rows_ready")

        VECS = len(VEC)

        def vec_parts():
            for name, shape in (("b_ada", "one (a b) -> (one a) b"), ("norm_pre_mix", None),
                                ("norm_pre_ffn", None), ("lru_conv_w", "w"), ("lru_conv_b", None),
                                ("lru_ba", None), ("lru_bx", None), ("lru_lambda", None),
                                ("ssd_conv_w", "w"), ("ssd_conv_b", None), ("ssd_norm_w", None),
                                ("c", None)):
                pattern = "o w (a b) -> (o w a) b" if shape == "w" else "o (a b) -> (o a) b"
                src = inp[name].rearrange(pattern, b=P)
                yield src, VEC[name]

        SEGS = (0, 1, 3, 4, 2, 5)
        MOD_PIECES = 2 * len(SEGS)
        FIRST = 4
        TURNS = 2 * KD

        with nc.Block() as block:
            @block.sync
            def _(sp):
                n = 0
                for src, row in vec_parts():
                    tile = (row >= VEC_TILES[1][0]) + (row >= VEC_TILES[2][0])
                    at = row - VEC_TILES[tile][0]
                    sp.dma_start(rows[at:at + src.shape[0], tile, :], src).then_inc(vec_loaded, 16)
                    n += 1
                assert n == VECS

                def piece(n):
                    i, half = divmod(n, 2)
                    if n >= 4:
                        sp.wait_ge(piece_done, n - 3)
                    at = SEGS[i] * D + half * TH
                    sp.dma_start(w_ada[:, n % 4], inp["w_ada"][0, :, at:at + TH].rearrange("(k p) n -> p k n", p=P)
                                 ).then_inc(ada_loaded[n % 4], 16)

                for n in range(FIRST):
                    piece(n)
                    for t in (2 * n, 2 * n + 1):
                        sp.dma_start(x_in[:, t, :], inp["x"][0, t * P:(t + 1) * P, :]).then_inc(x_loaded[t // 2], 16)
                for g, (seg, norm) in enumerate(((2, "norm_post_mix"), (5, "norm_post_ffn"))):
                    sp.dma_start(gate_rows[:, g, :], inp["b_ada"][0, seg * D:(seg + 1) * D].partition_broadcast(P)
                                 ).then_inc(row_vecs_loaded, 16)
                    sp.dma_start(norm_rows[:, g, :], inp[norm][0].partition_broadcast(P)).then_inc(row_vecs_loaded, 16)
                for n in range(FIRST, MOD_PIECES):
                    piece(n)

            @block.gpsimd
            def _(pool):
                pool.memset(ident[:], 0.0).then_inc(consts_set, 1)
                pool.memset(tri[:], 1.0).then_inc(consts_set, 1)
                pool.memset(mask[:], 0.0).then_inc(consts_set, 1)
                pool.memset(ones[:], 1.0).then_inc(consts_ready, 1)
                pool.memset(eps[:], EPS).then_inc(consts_ready, 1)
                pool.wait_ge(consts_set, 3)
                pool.affine_select(out=ident[:], in_=ident[:], compare_op=ALU.not_equal, fill=1.0, base=0,
                                   pattern=[[-1, P]], channel_multiplier=1).then_inc(consts_ready, 1)
                pool.affine_select(out=tri[:], in_=tri[:], compare_op=ALU.is_ge, fill=0.0, base=0,
                                   pattern=[[1, P]], channel_multiplier=-1).then_inc(consts_ready, 1)
                pool.affine_select(out=mask[:], in_=mask[:], compare_op=ALU.is_ge, fill=NEG, base=0,
                                   pattern=[[0, 4], [1, P]], channel_multiplier=-1).then_inc(consts_ready, 1)

            @block.scalar
            def _(act):
                act.wait_ge(consts_ready, 5)
                act.wait_ge(cols_ready, 3)
                act.activation(c_cols[:], cols[:, VEC["c"]:VEC["c"] + KD], ACT.Silu).then_inc(c_ready, 1)
                for t in range(TB):
                    act.wait_ge(x_loaded[t // 2], 32)
                    act.activation(junk[:], x_in[:, t, :], ACT.Square, accum_out=ssq[:, t:t + 1]).then_inc(ssq_ready, 1)
                    act.wait_ge(ssq_ready, t + 1)
                act.activation(std[:], ssq[:], ACT.Sqrt, bias=eps[:], scale=1.0 / D).then_inc(std_ready, 1)
                for n in range(TURNS):
                    k, half = divmod(n, 2)
                    act.wait_ge(full_ready, n + 1)
                    act.copy(hT[0][:, k, half * TH:(half + 1) * TH], h_full[:, n % 2, :]).then_inc(hi_ready, 1)

            @block.vector
            def _(dve):
                for t, (row, n) in enumerate(VEC_TILES):
                    dve.wait_ge(cols_turned, t + 1)
                    dve.tensor_copy(cols[:, row:row + n], ps_a[t % 2][:, 0:n]).then_inc(cols_ready, 1)
                dve.wait_ge(c_ready, 1)
                dve.tensor_copy(c_wide[:], c_cols[:].unsqueeze(2).to_broadcast([P, KD, P])).then_inc(c_ready, 1)
                dve.wait_ge(std_ready, 1)
                dve.reciprocal(rstd[:], std[:]).then_inc(rstd_ready, 1)
                dve.wait_ge(rstd_ready, 1)
                for t in range(TB):
                    dve.tensor_scalar(x_in[:, t, :], x_in[:, t, :], rstd[:, t:t + 1], None, ALU.mult).then_inc(xn_ready, 1)

                def piece(n):
                    i, half = divmod(n, 2)
                    dve.wait_ge(piece_done, n + 1)
                    if i < 4:
                        blocks = slice(half * 4, half * 4 + 4)
                        dve.wait_ge(mod_step, 2 * n)
                        dve.tensor_tensor(diag[:], ps_r[n % 4][:].rearrange("p (a b) -> p a b", b=P),
                                          ident[:].unsqueeze(1).to_broadcast([P, 4, P]), ALU.mult).then_inc(piece_out, 1)
                        dve.wait_ge(piece_out, n + 1)
                        dve.reduce_sum(mod[:, i, blocks], diag[:], axis=AX.X).then_inc(mod_step, 1)
                        dve.wait_ge(mod_step, 2 * n + 1)
                        at = SEGS[i] * KD + half * 4
                        dve.tensor_tensor(mod[:, i, blocks], mod[:, i, blocks], cols[:, at:at + 4], ALU.add
                                          ).then_inc(mod_step, 1)
                    else:
                        if n == 8:
                            dve.wait_ge(row_vecs_loaded, 16 * 4)
                        part = gate_rows[:, i - 4, half * TH:(half + 1) * TH]
                        dve.tensor_tensor(part, ps_r[n % 4][:], part, ALU.add).then_inc(piece_out, 1)

                for n in range(FIRST):
                    piece(n)
                dve.wait_ge(mod_step, 2 * FIRST)
                nw = VEC["norm_pre_mix"]
                dve.scalar_tensor_tensor(mult1[:], mod[:, 1, :], 1.0, cols[:, nw:nw + KD], ALU.add, ALU.mult
                                         ).then_inc(mult_ready, 1)
                dve.wait_ge(mult_ready, 1)

                def low(n):
                    k, half = divmod(n, 2)
                    sl = slice(half * TH, (half + 1) * TH)
                    dve.wait_ge(hi_ready, n + 1)
                    dve.tensor_tensor(hT[1][:, k, sl], h_full[:, n % 2, :], hT[0][:, k, sl].bitcast(F32), ALU.subtract
                                      ).then_inc(lo_ready, 1)

                for n in range(TURNS):
                    dve.wait_ge(turned, n + 1)
                    if n >= 2:
                        dve.wait_ge(lo_ready, n - 1)
                    dve.tensor_scalar(h_full[:, n % 2, :], ps_a[n % 4][:], mult1[:, n // 2:n // 2 + 1],
                                      mod[:, 0, n // 2:n // 2 + 1], ALU.mult, ALU.add).then_inc(full_ready, 1)
                    if n >= 1:
                        low(n - 1)
                    if n % 2:
                        piece(FIRST + n // 2)
                low(TURNS - 1)
                dve.wait_ge(mod_step, 16)
                nw = VEC["norm_pre_ffn"]
                dve.scalar_tensor_tensor(mod[:, 3, :], mod[:, 3, :], 1.0, cols[:, nw:nw + KD],
                                         ALU.add, ALU.mult).then_inc(mult_ready, 1)
                dve.wait_ge(piece_out, MOD_PIECES)
                dve.tensor_tensor(gate_rows[:], gate_rows[:], norm_rows[:], ALU.mult).then_inc(rows_ready, 1)

            @block.tensor
            def _(pe):
                pe.wait_ge(consts_ready, 5)
                pe.wait_ge(vec_loaded, 16 * VECS)
                for t, (row, n) in enumerate(VEC_TILES):
                    if t >= 2:
                        pe.wait_ge(cols_ready, t - 1)
                    pe.transpose(ps_a[t % 2][:, 0:n], rows[0:n, t, :], ident[0:n, 0:n]).then_inc(cols_turned, 1)
                pe.wait_ge(c_ready, 2)

                def piece(n):
                    pe.wait_ge(ada_loaded[n % 4], 16 * (n // 4 + 1))
                    if n >= 4:
                        pe.wait_ge(piece_out, n - 3)
                    for k in range(KD):
                        mm = pe.matmul(ps_r[n % 4][:], c_wide[:, k, :], w_ada[:, n % 4, k, :],
                                       start=(k == 0), stop=(k == KD - 1))
                    mm.then_inc(piece_done, 1)

                def turn(n):
                    k, half = divmod(n, 2)
                    if n >= 4:
                        pe.wait_ge(full_ready, n - 3)
                    for j in range(4):
                        mm = pe.transpose(ps_a[n % 4][:, j * P:(j + 1) * P],
                                          x_in[:, half * 4 + j, k * P:(k + 1) * P], ident[:])
                    mm.then_inc(turned, 1)

                for n in range(FIRST):
                    piece(n)
                pe.wait_ge(xn_ready, TB)
                pe.wait_ge(cols_ready, 3)
                for n in range(TURNS):
                    turn(n)
                    if n % 2:
                        piece(FIRST + n // 2)


def pairs(eng, lo, hi, body):
    assert lo % 2 == 0 and hi % 2 == 0
    if lo == 0:
        body(0, 0)
        body(1, 1)
        lo = 2
    with eng.Fori(lo // 2, hi // 2) as p:
        body(p * 2, 0)
        body(p * 2 + 1, 1)


def wait_from(eng, sem, value):
    if not isinstance(value, int) or value > 0:
        eng.wait_ge(sem, value)


def alone(eng, passed):
    eng.sem_inc(passed, 1)


def ahead(eng, *sems, by=1):
    for sem in sems:
        eng.sem_inc(sem, by)


def of_buffer(i, u):
    return (i - u) * 8


def project_in(m, inp, keep, scratch):
    nc = m.nc
    N_LRU, N_XBC, N_Z, N_GATE = KD, XBC // P, SI // P, 2 * KD
    B_XBC = N_LRU
    B_Z = B_XBC + N_XBC
    B_GATE = B_Z + N_Z
    TILES = B_GATE + N_GATE
    pool_passed, act_passed = keep["pool_passed"], keep["act_passed"]
    ident, hT, cols, sp_in, sp_out = keep["ident"], keep["hT"], keep["cols"], keep["sp_in"], keep["sp_out"]
    with ExitStack() as st:
        w_raw = m.sb(st, "w_raw", [P, 2, KD, P])
        w_hi = m.sb(st, "w_hi", [P, 2, KD, P], F32R)
        w_lo = m.sb(st, "w_lo", [P, 2, KD, P], F32R)
        dt_raw = m.sb(st, "w_dt_raw", [P, KD, SH])
        dt_hi = m.sb(st, "w_dt_hi", [P, KD, SH], F32R)
        dt_lo = m.sb(st, "w_dt_lo", [P, KD, SH], F32R)
        dt_bias = m.sb(st, "dt_bias", [P, SH])
        pre = m.sb(st, "conv_in", [P, 2, CW - 1 + T])
        acc = m.sb(st, "conv_out", [P, 2, T])
        fin = m.sb(st, "act_out", [P, 2, T])
        xl = m.sb(st, "lru_x", [P, KD, T])
        w_gate = m.sb(st, "lru_w", [P, 2, KD, P])
        w_cur = m.sb(st, "lru_w_cur", [P, 2, P])
        r_, i_, a_ = (m.sb(st, n, [P, T]) for n in ("lru_r", "lru_i", "lru_a"))
        th, v_, sq, ix, hl = (m.sb(st, n, [P, T]) for n in ("lru_tanh", "lru_v", "lru_sqrt", "lru_ix", "lru_h"))
        NS = KD + TB * SH
        s_abs, s_e, s_u, s_c = (m.sb(st, n, [P, NS]) for n in ("sp_abs", "sp_exp", "sp_one_plus", "sp_corr"))
        ps = [m.ps(st, f"p1_{i}", [P, 2, TH]) for i in range(2)]
        ps_g = m.ps(st, "p1_gates", [P, 2, TH])
        ps_dt = m.ps(st, "p1_dt", [P, 512])

        w_loaded = [m.sem(f"w_in_loaded{i}") for i in range(2)]
        small_loaded = m.sem("small_loaded")
        zeroed = m.sem("lru_w_zeroed")
        hi_done, lo_done = m.sem("w_hi_done"), m.sem("w_lo_done")
        dt_split, dt_done = m.sem("dt_split"), m.sem("dt_done")
        sp_dve, sp_act = m.sem("softplus_dve"), m.sem("softplus_act")
        mm_done, evac_done = m.sem("proj_done"), m.sem("proj_evacuated")
        conv_step, silu_done = m.sem("conv_step"), m.sem("silu_done")
        stored = [m.sem(f"act_stored{i}") for i in range(2)]
        w_cur_ready, lru_mm, sig_done = m.sem("lru_w_ready"), m.sem("lru_products"), m.sem("lru_sigmoids")
        exp_done, v_done, sqrt_done = m.sem("lru_exp_tanh"), m.sem("lru_v_done"), m.sem("lru_sqrt_done")
        ix_done, u_done, scan_done = m.sem("lru_ix_done"), m.sem("lru_u_done"), m.sem("lru_scan_done")
        h_stored = m.sem("lru_h_stored")

        def w_in(col, j):
            return inp["w_in"][0, :, bass.ds(j * P + col, P)].rearrange("(k p) n -> p k n", p=P)

        SEGMENTS = ((0, B_XBC, COL_LRU), (B_XBC, B_Z, COL_XBC - B_XBC * P),
                    (B_Z, B_GATE, COL_Z - B_Z * P), (B_GATE, TILES, COL_GATE - B_GATE * P))

        def quads(eng, tile, lru):
            for seg in (2, 3):
                lo, hi, _ = SEGMENTS[seg]
                with eng.Fori(lo // 4, hi // 4) as p:
                    j = p - B_Z // 4
                    for q in range(4):
                        tile(p * 4 + q, q % 2, seg)
                        lru(j, q)

        with nc.Block() as block:
            @block.sync
            def _(sp):
                sp.dma_start(dt_raw[:], inp["w_in"][0, :, COL_DT:COL_DT + SH].rearrange("(k p) n -> p k n", p=P)
                             ).then_inc(small_loaded, 16)
                sp.dma_start(dt_bias[:], inp["ssd_dt_bias"][0].partition_broadcast(P)).then_inc(small_loaded, 16)

                def load(col):
                    def body(i, u):
                        wait_from(sp, lo_done, i - 1)
                        sp.dma_start(w_raw[:, u], w_in(col, i)).then_inc(w_loaded[u], 16)
                    return body

                pairs(sp, 0, B_XBC, load(SEGMENTS[0][2]))
                sp.wait_ge(zeroed, 1)
                for g, name in enumerate(("lru_wa", "lru_wx")):
                    for odd in range(2):
                        at = slice(64 * odd, 64 * odd + 64)
                        sp.dma_start(w_gate[at, g, :, at],
                                     inp[name][0].rearrange("(j two) a b -> two a j b", two=2)[odd]
                                     ).then_inc(small_loaded, 16)
                for lo, hi, col in SEGMENTS[1:]:
                    pairs(sp, lo, hi, load(col))

            @block.gpsimd
            def _(pool):
                ahead(pool, ix_done)
                pool.memset(w_gate[:], 0.0).then_inc(zeroed, 1)
                pool.memset(pre[:, :, 0:CW - 1], 0.0).then_inc(zeroed, 1)
                pool.wait_ge(small_loaded, 32)
                pool.tensor_copy(dt_hi[:], dt_raw[:]).then_inc(dt_split, 1)
                pool.wait_ge(dt_split, 1)
                pool.tensor_tensor(dt_lo[:], dt_raw[:], dt_hi[:].bitcast(F32), ALU.subtract).then_inc(dt_split, 1)

                def cut(i, u, seg=0):
                    pool.wait_ge(w_loaded[u], of_buffer(i, u) + 16)
                    wait_from(pool, mm_done, i - 1)
                    alone(pool, pool_passed)
                    pool.tensor_copy(w_hi[:, u], w_raw[:, u]).then_inc(hi_done, 1)
                    pool.wait_ge(hi_done, i + 1)
                    pool.tensor_tensor(w_lo[:, u], w_raw[:, u], w_hi[:, u].bitcast(F32), ALU.subtract
                                       ).then_inc(lo_done, 1)

                def lru(j, q):
                    if q == 0:
                        pool.wait_ge(lru_mm, j * 2 + 1)
                        alone(pool, pool_passed)
                        pool.tensor_copy(w_cur[:], w_gate[:, :, bass.ds(j, 1), :].rearrange("p g o n -> p (g o) n")
                                         ).then_inc(w_cur_ready, 1)
                    if q == 3:
                        pool.wait_ge(sig_done, j * 4 + 5)
                        pool.wait_ge(u_done, j + 1)
                        pool.tensor_tensor(ix[:], i_[:], xl[:, bass.ds(j, 1), :].rearrange("p o n -> p (o n)"),
                                           ALU.mult).then_inc(ix_done, 1)

                pairs(pool, 0, B_XBC, cut)
                pairs(pool, B_XBC, B_Z, cut)
                pool.wait_ge(small_loaded, 96)
                quads(pool, cut, lru)

            @block.tensor
            def _(pe):
                ahead(pe, lru_mm)
                pe.wait_ge(dt_split, 2)
                for half in range(2):
                    n = 0
                    for k in range(KD):
                        for w, h in ((dt_hi, 0), (dt_hi, 1), (dt_lo, 0)):
                            mm = pe.matmul(ps_g[0:SH, half, :], w[:, k, :], hT[h][:, k, half * TH:(half + 1) * TH],
                                           start=(n == 0), stop=(n == 3 * KD - 1))
                            n += 1
                mm.then_inc(dt_done, 1)
                pe.wait_ge(dt_done, 2)
                for t in range(TB):
                    mm = pe.transpose(ps_dt[:, t * SH:(t + 1) * SH], fin[0:SH, 0, t * P:(t + 1) * P], ident[0:SH, 0:SH])
                mm.then_inc(dt_done, 1)

                def tile(i, u, seg=0):
                    pe.wait_ge(lo_done, i + 1)
                    wait_from(pe, evac_done, i - 1)
                    for half in range(2):
                        n = 0
                        for k in range(KD):
                            for w, h in ((w_hi, 0), (w_hi, 1), (w_lo, 0)):
                                mm = pe.matmul(ps[u][:, half, :], w[:, u, k, :], hT[h][:, k, half * TH:(half + 1) * TH],
                                               start=(n == 0), stop=(n == 3 * KD - 1))
                                n += 1
                    mm.then_inc(mm_done, 1)

                def lru(j, q):
                    if q > 1:
                        return
                    if q == 0:
                        pe.wait_ge(w_cur_ready, j + 1)
                    pe.wait_ge(sig_done, j * 4 + (2 * q + 1))
                    for g in range(2):
                        mm = pe.matmul(ps_g[:, g, :], w_cur[:, g, :],
                                       xl[:, bass.ds(j, 1), q * TH:(q + 1) * TH].rearrange("p o n -> p (o n)"),
                                       start=True, stop=True)
                    mm.then_inc(lru_mm, 1)

                pairs(pe, 0, B_XBC, tile)
                pairs(pe, B_XBC, B_Z, tile)
                pe.wait_ge(conv_step, 4 * B_XBC)
                quads(pe, tile, lru)

            @block.scalar
            def _(act):
                ahead(act, sig_done, exp_done)
                ahead(act, h_stored, *stored, by=16)
                act.wait_ge(dt_done, 1)
                act.copy(fin[0:SH, 0, :], ps_g[0:SH].rearrange("p a b -> p (a b)")).then_inc(dt_done, 1)
                act.wait_ge(sp_dve, 2)
                act.activation(s_abs[:], sp_in[:], ACT.Abs).then_inc(sp_act, 1)
                act.wait_ge(sp_act, 1)
                act.activation(s_e[:], s_abs[:], ACT.Exp, scale=-1.0).then_inc(sp_act, 1)
                act.wait_ge(sp_dve, 3)
                act.activation(sp_out[:], s_u[:], ACT.Ln).then_inc(sp_act, 1)

                def conv(i, u, seg):
                    act.wait_ge(mm_done, i + 1)
                    wait_from(act, conv_step, i * 4 - 4)
                    act.copy(pre[:, u, CW - 1:], ps[u][:].rearrange("p h n -> p (h n)")).then_inc(evac_done, 1)
                    if seg == 1:
                        act.wait_ge(conv_step, i * 4 + 4)
                        act.wait_ge(stored[u], of_buffer(i, u) + (16 - 8 * B_XBC))
                        act.activation(fin[:, u], acc[:, u], ACT.Silu).then_inc(silu_done, 1)
                        act.wait_ge(silu_done, i - B_XBC + 1)
                        act.dma_start(scratch["xbc"][bass.ds((i - B_XBC) * P, P), :], fin[:, u]).then_inc(stored[u], 16)

                def direct(i, u, seg):
                    act.wait_ge(mm_done, i + 1)
                    act.wait_ge(stored[u], of_buffer(i, u) + (16 - 8 * B_XBC))
                    act.activation(fin[:, u], ps[u][:].rearrange("p h n -> p (h n)"),
                                   ACT.Silu if seg == 2 else ACT.Sigmoid).then_inc(evac_done, 1)
                    act.wait_ge(evac_done, i + 1)
                    dest = scratch["z" if seg == 2 else "gates"]
                    act.dma_start(dest[bass.ds((i - SEGMENTS[seg][0]) * P, P), :], fin[:, u]).then_inc(stored[u], 16)

                def lru(j, q):
                    if q < 2:
                        act.wait_ge(lru_mm, j * 2 + q + 2)
                        if q == 0:
                            act.wait_ge(ix_done, j + 1)
                            act.wait_ge(exp_done, j * 2 + 1)
                        alone(act, act_passed)
                        for g, (dst, b) in enumerate(((r_, "lru_ba"), (i_, "lru_bx"))):
                            act.activation(dst[:, q * TH:(q + 1) * TH], ps_g[:, g, :], ACT.Sigmoid,
                                           bias=cols[:, bass.ds(j + VEC[b], 1)]).then_inc(sig_done, 1)
                    if q == 1:
                        act.wait_ge(sig_done, j * 4 + 5)
                        act.wait_ge(scan_done, j + 1)
                        alone(act, act_passed)
                        act.activation(a_[:], r_[:], ACT.Exp, scale=sp_out[:, bass.ds(j, 1)]).then_inc(exp_done, 1)
                        act.activation(th[:], r_[:], ACT.Tanh, scale=sp_in[:, bass.ds(j, 1)]).then_inc(exp_done, 1)
                    if q == 2:
                        act.wait_ge(v_done, j * 2 + 2)
                        act.activation(sq[:], v_[:], ACT.Sqrt).then_inc(sqrt_done, 1)
                    if q == 3:
                        act.wait_ge(scan_done, j + 2)
                        act.dma_start(scratch["y_lru"][bass.ds(j * P, P), :], hl[:]).then_inc(h_stored, 16)

                pairs(act, 0, B_XBC, lambda i, u: conv(i, u, 0))
                pairs(act, B_XBC, B_Z, lambda i, u: conv(i, u, 1))
                act.wait_ge(sp_dve, 9)
                quads(act, direct, lru)
                act.wait_ge(h_stored, 16 * (KD + 1))
                for u in range(2):
                    act.wait_ge(stored[u], 8 * (TILES - B_XBC) + 16)

            @block.vector
            def _(dve):
                ahead(dve, u_done, scan_done)
                dve.tensor_scalar(sp_in[:, 0:KD], cols[:, VEC["lru_lambda"]:VEC["lru_lambda"] + KD], -1.0, None,
                                  ALU.mult).then_inc(sp_dve, 1)
                dve.wait_ge(dt_done, 3)
                dve.tensor_tensor(sp_in[:, KD:].rearrange("p (t h) -> p t h", h=SH),
                                  ps_dt[:, 0:TB * SH].rearrange("p (t h) -> p t h", h=SH),
                                  dt_bias[:].unsqueeze(1).to_broadcast([P, TB, SH]), ALU.add).then_inc(sp_dve, 1)
                dve.wait_ge(sp_act, 2)
                dve.tensor_scalar(s_u[:], s_e[:], 1.0, None, ALU.add).then_inc(sp_dve, 1)
                dve.wait_ge(sp_dve, 3)
                dve.scalar_tensor_tensor(s_c[:], s_u[:], -1.0, s_e[:], ALU.add, ALU.subtract).then_inc(sp_dve, 1)
                dve.reciprocal(s_abs[:], s_u[:]).then_inc(sp_dve, 1)
                dve.wait_ge(sp_dve, 5)
                dve.tensor_tensor(s_c[:], s_c[:], s_abs[:], ALU.mult).then_inc(sp_dve, 1)
                dve.wait_ge(sp_dve, 6)
                dve.wait_ge(sp_act, 3)
                dve.tensor_tensor(sp_out[:], sp_out[:], s_c[:], ALU.subtract).then_inc(sp_dve, 1)
                dve.wait_ge(sp_dve, 7)
                dve.scalar_tensor_tensor(sp_out[:], sp_in[:], 0.0, sp_out[:], ALU.max, ALU.add).then_inc(sp_dve, 1)
                dve.wait_ge(sp_dve, 8)
                dve.tensor_scalar(sp_in[:, 0:KD], sp_out[:, 0:KD], LRU_C, None, ALU.mult).then_inc(sp_dve, 1)
                dve.wait_ge(sp_dve, 9)
                dve.tensor_scalar(sp_out[:, 0:KD], sp_in[:, 0:KD], -1.0, None, ALU.mult).then_inc(sp_dve, 1)

                dve.wait_ge(zeroed, 2)

                def conv(i, u, seg):
                    w, b, first, n = (("lru_conv_w", "lru_conv_b", 0, KD) if seg == 0 else
                                      ("ssd_conv_w", "ssd_conv_b", B_XBC, XBC // P))
                    j = i - first
                    if seg == 0:
                        dst = xl[:, j, :] if isinstance(j, int) else xl[:, bass.ds(j, 1), :].rearrange("p o n -> p (o n)")
                    else:
                        dst = acc[:, u, :]
                        wait_from(dve, silu_done, j - 1)
                    dve.wait_ge(evac_done, i + 1)
                    col = lambda c: cols[:, bass.ds(j + c, 1)]
                    dve.tensor_scalar(dst, pre[:, u, CW - 1:], col(VEC[w] + (CW - 1) * n), col(VEC[b]),
                                      ALU.mult, ALU.add).then_inc(conv_step, 1)
                    for s in range(1, CW):
                        tap = CW - 1 - s
                        dve.wait_ge(conv_step, i * 4 + s)
                        dve.scalar_tensor_tensor(dst, pre[:, u, tap:tap + T], col(VEC[w] + tap * n), dst,
                                                 ALU.mult, ALU.add).then_inc(conv_step, 1)

                pairs(dve, 0, B_XBC, lambda i, u: conv(i, u, 0))
                conv(B_XBC, 0, 1)
                conv(B_XBC + 1, 1, 1)
                pairs(dve, B_XBC + 2, B_Z, lambda i, u: conv(i, u, 1))
                with dve.Fori(0, KD) as j:
                    dve.wait_ge(exp_done, j * 2 + 3)
                    dve.tensor_tensor(v_[:], a_[:], a_[:], ALU.mult).then_inc(v_done, 1)
                    dve.wait_ge(v_done, j * 2 + 1)
                    dve.scalar_tensor_tensor(v_[:], v_[:], 1.0, th[:], ALU.add, ALU.mult).then_inc(v_done, 1)
                    dve.wait_ge(sqrt_done, j + 1)
                    dve.wait_ge(ix_done, j + 2)
                    dve.tensor_tensor(v_[:], sq[:], ix[:], ALU.mult).then_inc(u_done, 1)
                    dve.wait_ge(u_done, j + 2)
                    dve.wait_ge(h_stored, j * 16 + 16)
                    dve.tensor_tensor_scan(hl[:], a_[:], v_[:], 0.0, ALU.mult, ALU.add).then_inc(scan_done, 1)


def ssd(m, inp, keep, scratch):
    nc = m.nc
    CH = T // P
    W = SHG * SP_
    WT = W // P
    ident, tri, mask, ones = keep["ident"], keep["tri"], keep["mask"], keep["ones"]
    dt_all = keep["sp_out"][:, KD:].rearrange("p (c h) -> p c h", h=SH)
    act_passed, pool_passed = keep["act_passed"], keep["pool_passed"]
    with ExitStack() as st:
        xbc = m.sb(st, "xbc_chunk", [P, 2, XBC // P, P])
        zc = m.sb(st, "z_chunk", [P, 2, SI // P, P])
        a_row = m.sb(st, "a_row", [P, SH])
        d_row = m.sb(st, "d_row", [P, SH])
        da = m.sb(st, "da", [P, CH, SH])
        da_cur = [m.sb(st, f"da_cur{i}", [P, 2, SH], F32R) for i in range(2)]
        tri_r = m.sb(st, "tri_r", [P, P], F32R)
        ident_b = m.sb(st, "ident_b", [P, P], BF16)
        neg_acs = m.sb(st, "neg_acs", [P, CH, SH])
        dec_out = m.sb(st, "decay_out", [P, CH, SH])
        dec_state = m.sb(st, "decay_state", [P, CH, SH])
        dec_chunk = m.sb(st, "decay_chunk", [P, CH, SH])
        state = m.sb(st, "state", [P, SG, W])
        state_dec = m.sb(st, "state_dec", [P, W])
        xt = m.sb(st, "x_tok", [P, 2, W])
        xdt = m.sb(st, "x_dt", [P, 2, W])
        xdd = m.sb(st, "x_dt_decay", [P, 2, W])
        x_d = m.sb(st, "x_skip", [P, 2, W])
        bt = m.sb(st, "b_tok", [P, 2, P])
        ell = m.sb(st, "decay_ls", [P, SHG, P])
        mm_ = m.sb(st, "cb_decay", [P, 2, SHG, P])
        yo = m.sb(st, "y_tok", [P, 2, W])
        sq = m.sb(st, "y_sq", [P, 2, W])
        y_ch = m.sb(st, "y_chunk", [P, 2, SI // P, P])
        ss_all = keep["y_squares"]
        ps_x = m.ps(st, "p2_x", [P, 512])
        ps_cb = m.ps(st, "p2_cb", [P, 512])
        ps_l = m.ps(st, "p2_l", [P, 2, 512])
        ps_o = m.ps(st, "p2_o", [P, 512])
        ps_s = m.ps(st, "p2_s", [P, 512])
        ps_y = m.ps(st, "p2_y", [P, 512])
        ps_q = m.ps(st, "p2_q", [P, 512])

        loaded = [m.sem(f"chunk_loaded{i}") for i in range(2)]
        rows_loaded, pre_dve, pre_act = m.sem("ssd_rows_loaded"), m.sem("ssd_pre_dve"), m.sem("ssd_pre_act")
        pre_pe, pre_pool = m.sem("ssd_pre_pe"), m.sem("ssd_pre_pool")
        cur_ready = m.sem("da_cur_ready")
        turned, spread = m.sem("ssd_turned"), m.sem("acs_spread")
        off_done, state_mm, y_done, ss_done = m.sem("y_off_done"), m.sem("state_mm"), m.sem("y_done"), m.sem("ss_done")
        xt_done, ell_done, sq_done, ss_kept = m.sem("x_tok_done"), m.sem("decay_ls_done"), m.sem("sq_done"), m.sem("ss_kept")
        bt_done, yo_done, state_done = m.sem("b_tok_done"), m.sem("y_tok_done"), m.sem("state_done")
        m_done, yg_done = m.sem("cb_decay_done"), m.sem("y_gated")
        pool_step = m.sem("ssd_pool_step")
        y_stored = [m.sem(f"y_stored{i}") for i in range(2)]

        LAST = CH * SG - 1

        def heads(ap):
            return ap.rearrange("p (h q) -> p h q", q=SP_)

        def per_head(ap, c, g):
            part = ap[:, bass.ds(c, 1), g * SHG:(g + 1) * SHG].rearrange("p o h -> p (o h)")
            return part.unsqueeze(2).to_broadcast([P, SHG, SP_])

        def token_slice(ap, lo, n, c):
            return ap[:, lo:lo + n, bass.ds(c * P, P)]

        with nc.Block() as block:
            @block.sync
            def _(sp):
                sp.dma_start(a_row[:], inp["ssd_a_log"][0].partition_broadcast(P)).then_inc(rows_loaded, 16)
                sp.dma_start(d_row[:], inp["ssd_d"][0].partition_broadcast(P)).then_inc(rows_loaded, 16)

                def load(c, u):
                    wait_from(sp, yg_done, c * 4 - 4)
                    sp.dma_start(xbc[:, u], scratch["xbc"].rearrange("(k p) t -> p k t", p=P)[:, :, bass.ds(c * P, P)]
                                 ).then_inc(loaded[u], 16)
                    sp.dma_start(zc[:, u], scratch["z"].rearrange("(k p) t -> p k t", p=P)[:, :, bass.ds(c * P, P)]
                                 ).then_inc(loaded[u], 16)

                def store(c, u):
                    sp.dma_start(scratch["y_ssd"].rearrange("(k p) t -> p k t", p=P)[:, :, bass.ds(c * P, P)], y_ch[:, u]
                                 ).then_inc(y_stored[u], 16)

                def chunk(c, u):
                    load(c, u)
                    if not isinstance(c, int) or c > 1:
                        store(c - 2, u)

                pairs(sp, 0, CH, chunk)
                for c in (CH - 2, CH - 1):
                    sp.wait_ge(yg_done, c * 4 + 4)
                    store(c, c % 2)
                for u in range(2):
                    sp.wait_ge(y_stored[u], 8 * CH)

            @block.gpsimd
            def _(pool):
                pool.memset(state[:], 0.0).then_inc(pre_pool, 1)
                pool.wait_ge(rows_loaded, 32)
                pool.wait_ge(pre_act, 4)
                pool.wait_ge(pre_pool, 1)

                def step(c, u, g):
                    n, v = c * 4 + g, g % 2
                    pool.wait_ge(xt_done, n + 1)
                    wait_from(pool, y_done, n - 1)
                    alone(pool, pool_passed)
                    pool.tensor_tensor(heads(xdt[:, v]), heads(xt[:, v]), per_head(dt_all, c, g), ALU.mult
                                       ).then_inc(pool_step, 1)
                    pool.wait_ge(pool_step, n * 4 + 1)
                    wait_from(pool, state_mm, n - 1)
                    alone(pool, pool_passed)
                    pool.tensor_tensor(heads(xdd[:, v]), heads(xdt[:, v]), per_head(dec_state, c, g), ALU.mult
                                       ).then_inc(pool_step, 1)
                    wait_from(pool, yo_done, n * 2 - 2)
                    pool.tensor_tensor(heads(x_d[:, v]), heads(xt[:, v]),
                                       d_row[:, g * SHG:(g + 1) * SHG].unsqueeze(2).to_broadcast([P, SHG, SP_]),
                                       ALU.mult).then_inc(pool_step, 1)
                    wait_from(pool, state_done, n)
                    alone(pool, pool_passed)
                    pool.tensor_tensor(heads(state_dec[:]), heads(state[:, g]), per_head(dec_chunk, c, g), ALU.mult
                                       ).then_inc(pool_step, 1)

                pairs(pool, 0, CH, lambda c, u: [step(c, u, g) for g in range(SG)])

            @block.tensor
            def _(pe):
                pe.wait_ge(pre_dve, 3)
                pe.matmul(ps_x[:, 0:CH * SH], tri[:], da[:].rearrange("p c h -> p (c h)"), start=True, stop=True
                          ).then_inc(pre_pe, 1)
                pe.matmul(ps_cb[:, 0:CH * SH], ones[:], da[:].rearrange("p c h -> p (c h)"), start=True, stop=True
                          ).then_inc(pre_pe, 1)
                pe.wait_ge(pre_act, 4)
                pe.wait_ge(pre_dve, 6)
                pe.wait_ge(pre_pool, 1)

                def turn(c, u, g):
                    n = c * 4 + g
                    if g == 0:
                        pe.wait_ge(loaded[u], of_buffer(c, u) * 2 + 32)
                        pe.wait_ge(cur_ready, c * 2 + 2)
                    wait_from(pe, xt_done, n)
                    for j in range(WT):
                        pe.transpose(ps_x[:, j * P:(j + 1) * P], xbc[:, u, g * WT + j, :], ident[:])
                    wait_from(pe, m_done, n)
                    b_tile, c_tile = xbc[:, u, SI // P + g, :], xbc[:, u, SI // P + SG + g, :]
                    pe.matmul(ps_cb[:, 0:P], b_tile, c_tile, start=True, stop=True, skip_group_check=True)
                    pe.transpose(ps_cb[:, P:2 * P], b_tile, ident[:]).then_inc(turned, 1)
                    wait_from(pe, ell_done, n * 8)
                    for q in range(2):
                        pe.matmul(ps_l[:, q, :], ident_b[:], mask[:].rearrange("p a b -> p (a b)"), start=True,
                                  stop=False, skip_group_check=True)
                        for h in range(SHG // 2):
                            head = g * SHG + q * (SHG // 2) + h
                            for part in range(2):
                                mm = pe.matmul(ps_l[:, q, h * P:(h + 1) * P],
                                               da_cur[u][:, part, head:head + 1].to_broadcast([P, P]), tri_r[:],
                                               start=False, stop=(part == 1), skip_group_check=True)
                    mm.then_inc(spread, 1)

                def offset(c, u, g):
                    n = c * 4 + g
                    wait_from(pe, state_done, n - 3)
                    wait_from(pe, yo_done, n * 2)
                    pe.matmul(ps_o[:], xbc[:, u, SI // P + SG + g, :], state[:, g], start=True, stop=True
                              ).then_inc(off_done, 1)

                def multiply(c, u, g):
                    n, v = c * 4 + g, g % 2
                    pe.wait_ge(bt_done, n + 1)
                    pe.wait_ge(pool_step, n * 4 + 2)
                    wait_from(pe, state_done, n)
                    pe.matmul(ps_s[:], bt[:, v], xdd[:, v], start=True, stop=True).then_inc(state_mm, 1)
                    pe.wait_ge(yo_done, n * 2 + 2)
                    wait_from(pe, yg_done, n)
                    for j in range(WT):
                        pe.matmul(ps_y[:, j * P:(j + 1) * P], yo[:, v, j * P:(j + 1) * P], ident[:],
                                  start=(j == 0), stop=False, skip_group_check=True)
                    pe.wait_ge(m_done, n + 1)
                    for h in range(SHG):
                        at = slice(SP_ * (h % 2), SP_ * (h % 2) + SP_)
                        mm = pe.matmul(ps_y[at, (h // 2) * P:(h // 2 + 1) * P], xdt[:, v, h * SP_:(h + 1) * SP_],
                                       mm_[:, v, h, :], start=False, stop=True, skip_group_check=True)
                    mm.then_inc(y_done, 1)

                def squares(n, g):
                    pe.wait_ge(sq_done, n + 1)
                    wait_from(pe, ss_kept, n)
                    for j in range(WT):
                        mm = pe.matmul(ps_q[:, 0:P], ones[:], sq[:, g % 2, j * P:(j + 1) * P],
                                       start=(j == 0), stop=(j == WT - 1))
                    mm.then_inc(ss_done, 1)

                def step(c, u, g):
                    before = None
                    if g > 0:
                        before = (c, u, g - 1)
                    elif not isinstance(c, int) or c > 0:
                        before = (c - 1, 1 - u, SG - 1)
                    if before:
                        offset(*before)
                    turn(c, u, g)
                    if before:
                        multiply(*before)
                    if g > 1 or not isinstance(c, int) or c > 0:
                        squares(c * 4 + g - 2, (g - 2) % SG)

                pairs(pe, 0, CH, lambda c, u: [step(c, u, g) for g in range(SG)])
                offset(CH - 1, (CH - 1) % 2, SG - 1)
                multiply(CH - 1, (CH - 1) % 2, SG - 1)
                squares(LAST - 1, SG - 2)
                squares(LAST, SG - 1)

            @block.scalar
            def _(act):
                act.wait_ge(rows_loaded, 32)
                act.activation(a_row[:], a_row[:], ACT.Exp).then_inc(pre_act, 1)
                act.wait_ge(pre_dve, 5)
                act.activation(dec_out[:], neg_acs[:], ACT.Exp, scale=-1.0).then_inc(pre_act, 1)
                act.activation(dec_state[:], dec_state[:], ACT.Exp).then_inc(pre_act, 1)
                act.activation(dec_chunk[:], ps_cb[:, 0:CH * SH].rearrange("p (c h) -> p c h", h=SH), ACT.Exp
                               ).then_inc(pre_act, 1)

                def step(c, u, g):
                    n, v = c * 4 + g, g % 2
                    first = isinstance(c, int) and c == 0
                    act.wait_ge(turned, n + 1)
                    wait_from(act, pool_step, n * 4 - 4)
                    act.copy(xt[:, v], ps_x[:]).then_inc(xt_done, 1)
                    act.wait_ge(spread, n + 1)
                    wait_from(act, m_done, n)
                    alone(act, act_passed)
                    for h in range(SHG):
                        bias = neg_acs[:, bass.ds(c, 1), g * SHG + h:g * SHG + h + 1].rearrange("p a b -> p (a b)")
                        act.activation(ell[:, h, :], ps_l[:, h // 4, (h % 4) * P:(h % 4 + 1) * P], ACT.Exp, bias=bias
                                       ).then_inc(ell_done, 1)
                    if not first or g > 0:
                        square_of(c, u, g - 1) if g > 0 else square_of(c - 1, 1 - u, SG - 1)
                    if not first or g > 1:
                        keep_sum(c, g - 2) if g > 1 else keep_sum(c - 1, g + 2)

                def square_of(c, u, g):
                    n = c * 4 + g
                    act.wait_ge(yg_done, n + 1)
                    wait_from(act, ss_done, n - 1)
                    alone(act, act_passed)
                    act.activation(sq[:, g % 2].rearrange("p (k t) -> p k t", t=P), y_ch[:, u, g * WT:(g + 1) * WT, :],
                                   ACT.Square).then_inc(sq_done, 1)

                def keep_sum(c, g):
                    act.wait_ge(ss_done, c * 4 + g + 1)
                    alone(act, act_passed)
                    act.copy(token_slice(ss_all, g, 1, c).rearrange("p o t -> p (o t)"), ps_q[:, 0:P]).then_inc(ss_kept, 1)

                pairs(act, 0, CH, lambda c, u: [step(c, u, g) for g in range(SG)])
                square_of(CH - 1, (CH - 1) % 2, SG - 1)
                keep_sum(CH - 1, SG - 2)
                keep_sum(CH - 1, SG - 1)

            @block.vector
            def _(dve):
                dve.tensor_copy(tri_r[:], tri[:]).then_inc(pre_dve, 1)
                dve.tensor_copy(ident_b[:], ident[:]).then_inc(pre_dve, 1)
                dve.wait_ge(pre_act, 1)
                dve.scalar_tensor_tensor(da[:], dt_all, -1.0, a_row[:].unsqueeze(1).to_broadcast([P, CH, SH]),
                                         ALU.mult, ALU.mult).then_inc(pre_dve, 1)
                dve.wait_ge(pre_pe, 2)
                dve.tensor_scalar(neg_acs[:].rearrange("p c h -> p (c h)"), ps_x[:, 0:CH * SH], -1.0, None, ALU.mult
                                  ).then_inc(pre_dve, 1)
                dve.wait_ge(pre_dve, 4)
                dve.tensor_tensor(dec_state[:].rearrange("p c h -> p (c h)"), ps_cb[:, 0:CH * SH],
                                  neg_acs[:].rearrange("p c h -> p (c h)"), ALU.add).then_inc(pre_dve, 1)
                dve.wait_ge(pre_dve, 5)
                dve.engine_nop().then_inc(pre_dve, 1)
                dve.wait_ge(pre_act, 4)

                def da_hi_lo(c, u):
                    wait_from(dve, spread, c * 4 - 4)
                    src = da[:, bass.ds(c, 1), :].rearrange("p o h -> p (o h)")
                    dve.tensor_copy(da_cur[u][:, 0, :], src).then_inc(cur_ready, 1)
                    dve.wait_ge(cur_ready, c * 2 + 1)
                    dve.tensor_tensor(da_cur[u][:, 1, :], src, da_cur[u][:, 0, :].bitcast(F32), ALU.subtract
                                      ).then_inc(cur_ready, 1)

                def gate(c, u, g):
                    n = c * 4 + g
                    wait_from(dve, y_stored[u], of_buffer(c, u))
                    wait_from(dve, sq_done, n - 7)
                    dve.wait_ge(y_done, n + 1)
                    dve.tensor_tensor(y_ch[:, u, g * WT:(g + 1) * WT, :], ps_y[:].rearrange("p (k t) -> p k t", t=P),
                                      zc[:, u, g * WT:(g + 1) * WT, :], ALU.mult).then_inc(yg_done, 1)

                def add_up(c, u, g):
                    n, v = c * 4 + g, g % 2
                    dve.wait_ge(off_done, n + 1)
                    wait_from(dve, y_done, n - 1)
                    dve.tensor_tensor(heads(yo[:, v]), heads(ps_o[:]), per_head(dec_out, c, g), ALU.mult
                                      ).then_inc(yo_done, 1)
                    dve.wait_ge(yo_done, n * 2 + 1)
                    dve.wait_ge(pool_step, n * 4 + 4)
                    dve.tensor_tensor(yo[:, v], yo[:, v], x_d[:, v], ALU.add).then_inc(yo_done, 1)

                def add_state(c, u, g):
                    n = c * 4 + g
                    dve.wait_ge(state_mm, n + 1)
                    dve.tensor_tensor(state[:, g], state_dec[:], ps_s[:], ALU.add).then_inc(state_done, 1)

                def step(c, u, g):
                    n, v = c * 4 + g, g % 2
                    first = isinstance(c, int) and c == 0
                    if g == 0 and not (isinstance(c, int) and c < 2):
                        da_hi_lo(c, u)
                    before = None
                    if not first or g > 0:
                        before = (c, u, g - 1) if g > 0 else (c - 1, 1 - u, SG - 1)
                        add_up(*before)
                    dve.wait_ge(turned, n + 1)
                    wait_from(dve, state_mm, n - 1)
                    dve.tensor_copy(bt[:, v], ps_cb[:, P:2 * P]).then_inc(bt_done, 1)
                    if before:
                        add_state(*before)
                    dve.wait_ge(ell_done, n * 8 + 8)
                    wait_from(dve, y_done, n - 1)
                    dve.tensor_tensor(mm_[:, v], ell[:], ps_cb[:, 0:P].unsqueeze(1).to_broadcast([P, SHG, P]),
                                      ALU.mult).then_inc(m_done, 1)
                    if before:
                        gate(*before)

                da_hi_lo(0, 0)
                da_hi_lo(1, 1)
                pairs(dve, 0, CH, lambda c, u: [step(c, u, g) for g in range(SG)])
                add_up(CH - 1, (CH - 1) % 2, SG - 1)
                add_state(CH - 1, (CH - 1) % 2, SG - 1)
                gate(CH - 1, (CH - 1) % 2, SG - 1)


def merge(m, inp, keep, scratch):
    nc = m.nc
    KINDS = 1 + SI // D
    STAGES = 2 * KINDS
    GW = SI // SG
    cols, rstd = keep["cols"], keep["y_squares"]
    acc, w_o = keep["merged"], keep["w_o"]
    act_passed = keep["act_passed"]
    with ExitStack() as st:
        y_raw = m.sb(st, "y_raw", [P, 4, TH])
        y_hi = [m.sb(st, f"y_hi{i}", [P, KD, TH], F32R) for i in range(2)]
        y_lo = [m.sb(st, f"y_lo{i}", [P, KD, TH], F32R) for i in range(2)]
        w_raw = m.sb(st, "wo_raw", [P, 2, KD, P])
        w_hi = m.sb(st, "wo_hi", [P, 4, KD, P], F32R)
        w_lo = m.sb(st, "wo_lo", [P, 2, KD, P], F32R)
        gates = m.sb(st, "gates_sb", [P, 4, TH])
        part = m.sb(st, "merge_part", [P, TH])
        eps = m.sb(st, "eps2", [P, 1])
        ps = [m.ps(st, f"p3_{j}", [P, TH]) for j in range(4)]
        first_raw = w_o[:].bitcast(F32).rearrange("p k (b t) -> p (k b) t", t=TH)

        first_loaded = [m.sem(f"y_first_loaded{i}") for i in range(KD)]
        y_loaded = [m.sem(f"y_loaded{i}") for i in range(4)]
        w_loaded = [m.sem(f"wo_loaded{i}") for i in range(2)]
        g_loaded = [m.sem(f"gates_loaded{i}") for i in range(4)]
        eps_set, root_done, rstd_done = m.sem("eps2_set"), m.sem("y_root_done"), m.sem("y_rstd_done")
        y_normed, y_hi_done, y_lo_done = m.sem("y_normed"), m.sem("y_hi_done"), m.sem("y_lo_done")
        hi_done, lo_done, mm_done = m.sem("wo_hi_done"), m.sem("wo_lo_done"), m.sem("merge_mm")
        part_done, add_done = m.sem("merge_parts"), m.sem("merge_sums")
        w_o_loaded, sp_passed = m.sem("w_o_loaded"), m.sem("sp_passed")

        def stages(eng, start, step, early=None):
            for q in range(STAGES):
                half, kind = divmod(q, KINDS)
                start(q, half, kind)
                with eng.Fori(0, KD // 4) as gg:
                    if early:
                        early(q, half, kind, gg, 0)
                    for j in range(4):
                        if early and j < 3:
                            early(q, half, kind, gg, j + 1)
                        step(q, half, kind, gg, j)

        def nothing(q, half, kind):
            pass

        with nc.Block() as block:
            @block.sync
            def _(sp):
                def load_y(q, n, j):
                    half, kind = divmod(q, KINDS)
                    src = scratch["y_lru"] if kind == 0 else scratch["y_ssd"]
                    row = n * P + (0 if kind == 0 else (kind - 1) * D)
                    sp.wait_ge(y_lo_done, q * KD + n + 1)
                    alone(sp, sp_passed)
                    sp.dma_start(y_raw[:, j], src[bass.ds(row, P), half * TH:(half + 1) * TH]).then_inc(y_loaded[j], 16)

                def step(q, half, kind, gg, j):
                    n, u = gg * 4 + j, j % 2
                    b = n + q * KD
                    if q + 1 < STAGES:
                        load_y(q + 1, n, j)
                    w = inp["w_lru_out"][0] if kind == 0 else inp["w_ssd_out"][0, (kind - 1) * D:kind * D, :]
                    sp.wait_ge(lo_done, b + 1)
                    alone(sp, sp_passed)
                    sp.dma_start(w_raw[:, u], w[:, bass.ds(n * P, P)].rearrange("(k p) n -> p k n", p=P)
                                 ).then_inc(w_loaded[u], 16)
                    sp.wait_ge(part_done, b + 1)
                    alone(sp, sp_passed)
                    sp.dma_start(gates[:, j], scratch["gates"][bass.ds(n * P + min(kind, 1) * D, P),
                                                               half * TH:(half + 1) * TH]).then_inc(g_loaded[j], 16)
                    if q == STAGES - 2:
                        sp.dma_start(w_o[:, bass.ds(n, 1), :].rearrange("p o d -> p (o d)").bitcast(F32),
                                     inp["w_o"][0, bass.ds(n * P, P), :]).then_inc(w_o_loaded, 16)

                for n in range(KD):
                    sp.dma_start(first_raw[:, n], scratch["y_lru"][n * P:(n + 1) * P, 0:TH]).then_inc(first_loaded[n], 16)
                stages(sp, nothing, step)
                sp.wait_ge(w_o_loaded, 16 * KD)

            @block.gpsimd
            def _(pool):
                pool.memset(eps[:], EPS).then_inc(eps_set, 1)
                ahead(pool, lo_done, by=2)

                def step(q, half, kind, gg, j):
                    u, b = j % 2, gg * 4 + (q * KD + j)
                    pool.wait_ge(hi_done, b + 1)
                    pool.wait_ge(mm_done, b + 3)
                    pool.tensor_tensor(w_lo[:, u], w_raw[:, u], w_hi[:, j].bitcast(F32), ALU.subtract).then_inc(lo_done, 1)

                stages(pool, nothing, step)

            @block.scalar
            def _(act):
                def high(q, n, j):
                    s = n + q * KD
                    half, kind = divmod(q, KINDS)
                    if isinstance(s, int):
                        act.wait_ge(first_loaded[n], 16)
                    elif kind == 0:
                        act.wait_ge(y_loaded[j], (s - j) * 4 - 16)
                    else:
                        act.wait_ge(y_normed, n + (q - 1 - half) * KD + 1)
                    alone(act, act_passed)
                    src = first_raw[:, n] if isinstance(s, int) else y_raw[:, j]
                    act.copy(y_hi[q % 2][:, bass.ds(n, 1), :].rearrange("p o t -> p (o t)"), src).then_inc(y_hi_done, 1)

                def cut(q, half, kind, gg, j):
                    u, b = j % 2, gg * 4 + (q * KD + j)
                    act.wait_ge(w_loaded[u], (b - u) * 8 + 16)
                    act.wait_ge(mm_done, b + 1)
                    act.copy(w_hi[:, j], w_raw[:, u]).then_inc(hi_done, 1)

                def step(q, half, kind, gg, j):
                    if q + 1 < STAGES:
                        high(q + 1, gg * 4 + j, j)

                def start(q, half, kind):
                    if q == 1:
                        roots(1)
                    if q:
                        act.wait_ge(mm_done, q * KD + 4)
                        alone(act, act_passed)

                def roots(half):
                    p = rstd[:, :, half * TH:(half + 1) * TH]
                    act.activation(p, p, ACT.Sqrt, bias=eps[:], scale=1.0 / GW).then_inc(root_done, 1)

                act.wait_ge(eps_set, 1)
                roots(0)
                for n in range(KD):
                    high(0, n, n % 4)
                stages(act, start, step, early=cut)

            @block.vector
            def _(dve):
                ahead(dve, y_lo_done, part_done, by=4)
                ahead(dve, add_done)

                def low(q, n, j):
                    s = n + q * KD
                    at = lambda ap: ap[q % 2][:, bass.ds(n, 1), :].rearrange("p o t -> p (o t)")
                    src = first_raw[:, n] if isinstance(s, int) else y_raw[:, j]
                    dve.wait_ge(y_hi_done, s + 1)
                    dve.tensor_tensor(at(y_lo), src, at(y_hi).bitcast(F32), ALU.subtract).then_inc(y_lo_done, 1)

                LATER = ((0, 2), (1, 0), (1, 2))
                PIECE = TH // 4

                def invert(q, gg, j):
                    of, group = LATER[q]
                    at = slice(of * TH + j * PIECE, of * TH + (j + 1) * PIECE)
                    p = rstd[:, bass.ds(gg + group, 1), at].rearrange("p o t -> p (o t)")
                    dve.reciprocal(p, p).then_inc(rstd_done, 1)

                def start(q, half, kind):
                    if q in (1, 2, 3):
                        if q == 1:
                            dve.wait_ge(root_done, 2)
                        dve.wait_ge(rstd_done, 1 + KD * q)
                        alone(dve, keep["dve_passed"])

                def norm(q, half, kind, gg, j):
                    if q + 1 < STAGES and (kind + 1) % KINDS:
                        n = gg * 4 + j
                        s = n + (q + 1) * KD
                        w = n + (VEC["ssd_norm_w"] + kind * KD)
                        dve.wait_ge(y_loaded[j], (s - j) * 4 - 16)
                        dve.scalar_tensor_tensor(y_raw[:, j], y_raw[:, j], cols[:, bass.ds(w, 1)],
                                                 rstd[:, bass.ds(gg + 2 * kind, 1), half * TH:(half + 1) * TH].rearrange(
                                                     "p o t -> p (o t)"), ALU.mult, ALU.mult).then_inc(y_normed, 1)

                def step(q, half, kind, gg, j):
                    n, u = gg * 4 + j, j % 2
                    b = n + q * KD
                    into = acc[:, bass.ds(n, 1), half * TH:(half + 1) * TH].rearrange("p o t -> p (o t)")
                    dve.wait_ge(g_loaded[j], (b - j) * 4 + 16)
                    dve.wait_ge(mm_done, b + 5)
                    if kind == 0:
                        dve.tensor_tensor(into, ps[j][:], gates[:, j], ALU.mult).then_inc(part_done, 1)
                    else:
                        adds = n + (q - 1 - half) * KD
                        dve.wait_ge(add_done, adds + 1)
                        dve.tensor_tensor(part[:], ps[j][:], gates[:, j], ALU.mult).then_inc(part_done, 1)
                        dve.wait_ge(part_done, b + 5)
                        dve.tensor_tensor(into, part[:], into, ALU.add).then_inc(add_done, 1)
                    if q + 1 < STAGES:
                        low(q + 1, n, j)
                    if q < len(LATER):
                        invert(q, gg, j)

                for n in range(KD):
                    low(0, n, n % 4)
                dve.wait_ge(root_done, 1)
                dve.reciprocal(rstd[:, 0:2, 0:TH], rstd[:, 0:2, 0:TH]).then_inc(rstd_done, 1)
                dve.wait_ge(rstd_done, 1)
                alone(dve, keep["dve_passed"])
                stages(dve, start, step, early=norm)

            @block.tensor
            def _(pe):
                ahead(pe, mm_done, by=4)

                def start(q, half, kind):
                    pe.wait_ge(y_lo_done, (q + 1) * KD + 4)

                def step(q, half, kind, gg, j):
                    u, b = j % 2, gg * 4 + (q * KD + j)
                    pe.wait_ge(lo_done, b + 3)
                    pe.wait_ge(part_done, b + 1)
                    n = 0
                    for k in range(KD):
                        for w, y in ((w_hi[:, j], y_hi), (w_hi[:, j], y_lo), (w_lo[:, u], y_hi)):
                            mm = pe.matmul(ps[j][:], w[:, k, :], y[q % 2][:, k, :],
                                           start=(n == 0), stop=(n == 3 * KD - 1))
                            n += 1
                    mm.then_inc(mm_done, 1)

                stages(pe, start, step)


def post_mix(m, inp, keep, scratch):
    nc = m.nc
    ident, mod, gate_rows = keep["ident"], keep["mod"], keep["gate_rows"]
    DH = D // 2
    with ExitStack() as st:
        mg = [m.sb(st, "merged_hi", [P, KD, T], F32R), keep["merged_lo"]]
        wo = [m.sb(st, "w_o_hi", [P, KD, D], F32R), keep["w_o"]]
        x_in = m.sb(st, "x_res", [P, 2, D])
        junk = m.sb(st, "pm_square", [P, D])
        x1 = m.sb(st, "x1_sb", [P, 2, D])
        xn = m.sb(st, "x1_normed", [P, D])
        h2 = m.sb(st, "h2_sb", [P, 2, KD, P])
        stat = m.sb(st, "pm_stat", [P, TB, 2, 3])
        eps = m.sb(st, "eps3", [P, 1])
        ps_o = [m.ps(st, f"p3b_o{i}", [P, 2, DH]) for i in range(2)]
        ps_t = m.ps(st, "p3b_t", [P, 2, 4, P])

        hi_done, lo_done = m.sem("pm_hi_done"), [m.sem("merged_lo_done"), m.sem("w_o_lo_done")]
        x_loaded = [m.sem(f"x_res_loaded{i}") for i in range(2)]
        eps_set, mm_done, ssq_done, std_done = m.sem("eps3_set"), m.sem("w_o_done"), m.sem("pm_ssq"), m.sem("pm_std")
        rec_done, part_done, x1_done, xn_done = m.sem("pm_rstd"), m.sem("pm_part"), m.sem("x1_done"), m.sem("x1_normed_s")
        turned, h2_done = m.sem("x1_turned"), m.sem("h2_done")
        stored = [m.sem(f"pm_stored{i}") for i in range(2)]
        h_stored = [m.sem(f"h2_stored{i}") for i in range(2)]

        def slices():
            for n in range(2 * KD):
                which, k = n % 2, n // 2
                yield n, which, k

        def low(eng, which, k):
            hi, lo = (mg, wo)[which]
            eng.wait_ge(hi_done, 2 * k + which + 1)
            eng.tensor_tensor(lo[:, k, :], lo[:, k, :].bitcast(F32), hi[:, k, :].bitcast(F32), ALU.subtract
                              ).then_inc(lo_done[which], 1)

        with nc.Block() as block:
            @block.sync
            def _(sp):
                def load_x(t):
                    sp.dma_start(x_in[:, t % 2], inp["x"][0, t * P:(t + 1) * P, :]).then_inc(x_loaded[t % 2], 16)

                load_x(0)
                load_x(1)
                for t in range(TB):
                    sp.wait_ge(x1_done, t + 1)
                    sp.dma_start(scratch["x1"][t * P:(t + 1) * P, :], x1[:, t % 2]).then_inc(stored[t % 2], 16)
                    if t + 2 < TB:
                        load_x(t + 2)
                    sp.wait_ge(h2_done, KD * (t + 1))
                    sp.dma_start(scratch["h2"].rearrange("(k p) t -> p k t", p=P)[:, :, t * P:(t + 1) * P],
                                 h2[:, t % 2]).then_inc(h_stored[t % 2], 16)
                for u in range(2):
                    sp.wait_ge(stored[u], 8 * TB)
                    sp.wait_ge(h_stored[u], 8 * TB)

            @block.gpsimd
            def _(pool):
                pool.memset(eps[:], EPS).then_inc(eps_set, 1)
                for k in range(KD):
                    low(pool, 1, k)

            @block.scalar
            def _(act):
                act.wait_ge(eps_set, 1)
                for n, which, k in slices():
                    hi, lo = (mg, wo)[which]
                    act.copy(hi[:, k, :], lo[:, k, :].bitcast(F32)).then_inc(hi_done, 1)
                for t in range(TB):
                    for which in range(2):
                        s = 2 * t + which
                        if which == 0:
                            act.wait_ge(mm_done, t + 1)
                            src = ps_o[t % 2][:].rearrange("p a b -> p (a b)")
                        else:
                            act.wait_ge(x1_done, t + 1)
                            src = x1[:, t % 2]
                        act.activation(junk[:], src, ACT.Square, accum_out=stat[:, t, which, 0:1]).then_inc(ssq_done, 1)
                        act.wait_ge(ssq_done, s + 1)
                        act.activation(stat[:, t, which, 1:2], stat[:, t, which, 0:1], ACT.Sqrt, bias=eps[:],
                                       scale=1.0 / D).then_inc(std_done, 1)
                    act.wait_ge(turned, t + 1)
                    if t >= 2:
                        act.wait_ge(h_stored[t % 2], 16 * (t // 2))
                    for k in range(KD):
                        act.activation(h2[:, t % 2, k, :], ps_t[:, k // 4, k % 4, :], ACT.Identity,
                                       bias=mod[:, 2, k:k + 1], scale=mod[:, 3, k:k + 1]).then_inc(h2_done, 1)

            @block.vector
            def _(dve):
                for k in range(KD):
                    low(dve, 0, k)
                for t in range(TB):
                    for which in range(2):
                        dve.wait_ge(std_done, 2 * t + which + 1)
                        dve.reciprocal(stat[:, t, which, 2:3], stat[:, t, which, 1:2]).then_inc(rec_done, 1)
                        dve.wait_ge(rec_done, 2 * t + which + 1)
                        if which == 0:
                            if t >= 2:
                                dve.wait_ge(stored[t % 2], 16 * (t // 2))
                            dve.scalar_tensor_tensor(x1[:, t % 2], ps_o[t % 2][:].rearrange("p a b -> p (a b)"),
                                                     stat[:, t, 0, 2:3], gate_rows[:, 0, :], ALU.mult, ALU.mult
                                                     ).then_inc(part_done, 1)
                            dve.wait_ge(x_loaded[t % 2], 16 * (t // 2 + 1))
                            dve.wait_ge(part_done, t + 1)
                            dve.tensor_tensor(x1[:, t % 2], x1[:, t % 2], x_in[:, t % 2], ALU.add).then_inc(x1_done, 1)
                        else:
                            if t >= 1:
                                dve.wait_ge(turned, t)
                            dve.tensor_scalar(xn[:], x1[:, t % 2], stat[:, t, 1, 2:3], None, ALU.mult).then_inc(xn_done, 1)

            @block.tensor
            def _(pe):
                def turn(t):
                    pe.wait_ge(xn_done, t + 1)
                    if t >= 1:
                        pe.wait_ge(h2_done, KD * t)
                    for k in range(KD):
                        mm = pe.transpose(ps_t[:, k // 4, k % 4, :], xn[:, k * P:(k + 1) * P], ident[:])
                    mm.then_inc(turned, 1)

                for t in range(TB):
                    if t >= 2:
                        pe.wait_ge(part_done, t - 1)
                    for half in range(2):
                        n = 0
                        for k in range(KD):
                            if t == 0 and half == 0:
                                for which in range(2):
                                    pe.wait_ge(lo_done[which], k + 1)
                            for a, b in ((0, 0), (0, 1), (1, 0)):
                                mm = pe.matmul(ps_o[t % 2][:, half, :], mg[a][:, k, t * P:(t + 1) * P],
                                               wo[b][:, k, half * DH:(half + 1) * DH],
                                               start=(n == 0), stop=(n == 3 * KD - 1))
                                n += 1
                    mm.then_inc(mm_done, 1)
                    if t >= 1:
                        turn(t - 1)
                turn(TB - 1)


PH, PK, TOPK = 8, 128, 16
HP = 2 * PH
SEL_STEPS = 28


SCORES_READ = 6


def selection(m, st, tag):
    b = {}
    for name, shape, dt in (("scores", [P, 2, PK], F32), ("scores_rest", [P, 2, PK], F32), ("top", [P, 2, TOPK], F32),
                            ("idx", [P, 2, TOPK], U32), ("idx_f", [P, 2, TOPK], F32),
                            ("cand", [P, TOPK, TOPK], F32), ("cand_rest", [P, TOPK, TOPK], F32),
                            ("cv", [P, TOPK], F32), ("ci", [P, TOPK], U32), ("ij", [P, 2, TOPK], U32),
                            ("ij_f", [P, 2, TOPK], F32), ("neg_max", [P, 1], F32),
                            ("exp", [P, TOPK], F32), ("exp_sum", [P, 1], F32), ("inv", [P, 1], F32)):
        b[name] = m.sb(st, f"{tag}_{name}", shape, dt)
    b["hit"] = b["cand"]
    return b


def select_keys(dve, b, step, keep, n):
    sc, rest, top, idx = b["scores"], b["scores_rest"], b["top"], b["idx"]

    def after(k):
        dve.wait_ge(step, (n + 1) * SEL_STEPS + k)

    after(0)
    alone(dve, keep["dve_passed"])
    for p in range(2):
        dve.max(top[:, p, 0:8], sc[:, p]).then_inc(step, 1)
    after(2)
    alone(dve, keep["dve_passed"])
    for p in range(2):
        dve.max_index(idx[:, p, 0:8], top[:, p, 0:8], sc[:, p]).then_inc(step, 1)
        dve.match_replace(rest[:, p], top[:, p, 0:8], sc[:, p], -3.0e38).then_inc(step, 1)
    after(6)
    alone(dve, keep["dve_passed"])
    for p in range(2):
        dve.max(top[:, p, 8:16], rest[:, p]).then_inc(step, 1)
    after(8)
    alone(dve, keep["dve_passed"])
    for p in range(2):
        dve.max_index(idx[:, p, 8:16], top[:, p, 8:16], rest[:, p]).then_inc(step, 1)
    dve.tensor_tensor(b["cand"][:], top[:, 0].unsqueeze(2).to_broadcast([P, TOPK, TOPK]),
                      top[:, 1].unsqueeze(1).to_broadcast([P, TOPK, TOPK]), ALU.add).then_inc(step, 1)


def select_picks(dve, b, step, exp_done, keep, n, out):
    iota, idx = keep["iota_row"], b["idx"]

    def after(k):
        dve.wait_ge(step, (n + 1) * SEL_STEPS + k)

    flat = lambda ap: ap[:].rearrange("p a b -> p (a b)")
    after(11)
    alone(dve, keep["dve_passed"])
    dve.max(b["cv"][:, 0:8], flat(b["cand"])).then_inc(step, 1)
    dve.tensor_copy(b["idx_f"][:], idx[:]).then_inc(step, 1)
    after(12)
    alone(dve, keep["dve_passed"])
    dve.max_index(b["ci"][:, 0:8], b["cv"][:, 0:8], flat(b["cand"])).then_inc(step, 1)
    dve.match_replace(flat(b["cand_rest"]), b["cv"][:, 0:8], flat(b["cand"]), -3.0e38).then_inc(step, 1)
    dve.tensor_scalar(b["neg_max"][:], b["cv"][:, 0:1], -1.0, None, ALU.mult).then_inc(step, 1)
    after(15)
    alone(dve, keep["dve_passed"])
    dve.max(b["cv"][:, 8:16], flat(b["cand_rest"])).then_inc(step, 1)
    after(17)
    alone(dve, keep["dve_passed"])
    dve.max_index(b["ci"][:, 8:16], b["cv"][:, 8:16], flat(b["cand_rest"])).then_inc(step, 1)
    after(18)
    dve.tensor_scalar(b["ij"][:, 0], b["ci"][:], 4, None, ALU.logical_shift_right).then_inc(step, 1)
    dve.tensor_scalar(b["ij"][:, 1], b["ci"][:], TOPK - 1, None, ALU.bitwise_and).then_inc(step, 1)
    after(20)
    dve.tensor_copy(b["ij_f"][:], b["ij"][:]).then_inc(step, 1)
    for p in range(2):
        after(21 + 3 * p)
        dve.tensor_tensor(b["hit"][:], b["ij_f"][:, p].unsqueeze(2).to_broadcast([P, TOPK, TOPK]),
                          iota[:, 0:TOPK].unsqueeze(1).to_broadcast([P, TOPK, TOPK]), ALU.is_equal).then_inc(step, 1)
        after(22 + 3 * p)
        dve.tensor_tensor(b["hit"][:], b["hit"][:], b["idx_f"][:, p].unsqueeze(1).to_broadcast([P, TOPK, TOPK]),
                          ALU.mult).then_inc(step, 1)
        after(23 + 3 * p)
        dve.reduce_sum(out(1 + p), b["hit"][:], axis=AX.X).then_inc(step, 1)
    dve.wait_ge(exp_done, n + 1)
    dve.reciprocal(b["inv"][:], b["exp_sum"][:]).then_inc(step, 1)
    after(28)
    dve.tensor_scalar(out(0), b["exp"][:], b["inv"][:], None, ALU.mult).then_inc(keep["sel_done"], 1)


def select_act(act, b, step, exp_done, n):
    act.wait_ge(step, n * SEL_STEPS + (SEL_STEPS + 17))
    act.activation(b["exp"][:], b["cv"][:], ACT.Exp, bias=b["neg_max"][:], accum_out=b["exp_sum"][:]
                   ).then_inc(exp_done, 1)


def expert_keep(m, stack, keep):
    keep["iota_row"] = m.sb(stack, "iota_row", [P, P])
    keep["chosen"] = m.sb(stack, "chosen", [P, 3, P])
    keep["h2T"] = [m.sb(stack, "h2T_hi", [P, KD, T], F32R), m.sb(stack, "h2T_lo", [P, KD, T], F32R)]
    keep["sel_done"] = m.kept_sem("sel_done")


def queries(m, inp, keep, scratch):
    nc = m.nc
    ident, h2 = keep["ident"], keep["h2T"]
    pool_passed = keep["pool_passed"]
    with ExitStack() as st:
        h_raw = keep["y_acc"]
        iota_i = m.sb(st, "iota_i", [P, P], mybir.dt.int32)
        iota_set = m.sem("iota_set")
        keys = m.sb(st, "sub_keys", [P, HP, P])
        key_hi = m.sb(st, "keys_hi", [P, HP, P], F32R)
        key_lo = m.sb(st, "keys_lo", [P, HP, P], F32R)
        w_raw = m.sb(st, "wq_raw", [P, 2, KD, P])
        w_hi = m.sb(st, "wq_hi", [P, 2, KD, P], F32R)
        w_lo = m.sb(st, "wq_lo", [P, 2, KD, P], F32R)
        q_hi = m.sb(st, "q_hi", [P, T], F32R)
        q_lo = m.sb(st, "q_lo", [P, T], F32R)
        score = m.sb(st, "scores", [P, 2, TB, PK])
        ps_q = m.ps(st, "p4_q", [P, 2, TH])
        ps_q2 = m.ps(st, "p4_q2", [P, 2, TH])
        ps_s = m.ps(st, "p4_s", [P, TB, PK])
        ps_k = m.ps(st, "p4_k", [P, 2, 4, P])
        ps_qs = (ps_q, ps_q2)
        sel = selection(m, st, "query_sel")

        h_loaded = [m.sem(f"h2_loaded{i}") for i in range(KD)]
        h_hi, h_lo = m.sem("h2_hi_done"), m.sem("h2_lo_done")
        keys_loaded, keys_turned, keys_cut = m.sem("keys_loaded"), m.sem("keys_turned"), m.sem("keys_cut")
        w_loaded = [m.sem(f"wq_loaded{i}") for i in range(2)]
        hi_done, lo_done = m.sem("wq_hi_done"), m.sem("wq_lo_done")
        q_mm, q_hi_done, q_lo_done = m.sem("q_mm"), m.sem("q_hi_done"), m.sem("q_lo_done")
        s_mm, s_kept, s_block0 = m.sem("score_mm"), m.sem("scores_kept"), m.sem("scores_block0")
        s_stored = [m.sem(f"scores_stored{i}") for i in range(2)]
        step, exp_done = m.sem("q_sel_step"), m.sem("q_sel_exp")

        with nc.Block() as block:
            @block.sync
            def _(sp):
                def load(n, u):
                    wait_from(sp, lo_done, n - 1)
                    sp.dma_start(w_raw[:, u], inp["peer_wq"][0, :, bass.ds(n * P, P)].rearrange("(k p) n -> p k n", p=P)
                                 ).then_inc(w_loaded[u], 16)
                    if isinstance(n, int) and n == 0:
                        for k in range(KD):
                            sp.dma_start(h_raw[:, k], scratch["h2"][k * P:(k + 1) * P, :]).then_inc(h_loaded[k], 16)
                        sp.dma_start(keys[:], inp["peer_sub_keys"][0].rearrange("h p k d -> k (h p) d")
                                     ).then_inc(keys_loaded, 16)

                pairs(sp, 0, HP, load)

            @block.gpsimd
            def _(pool):
                pool.iota(iota_i[:], pattern=[[1, P]], base=0, channel_multiplier=0).then_inc(iota_set, 1)
                pool.wait_ge(iota_set, 1)
                pool.tensor_copy(keep["iota_row"][:], iota_i[:]).then_inc(iota_set, 1)

                def cut(n, u):
                    pool.wait_ge(w_loaded[u], of_buffer(n, u) + 16)
                    wait_from(pool, q_mm, n - 1)
                    alone(pool, pool_passed)
                    pool.tensor_copy(w_hi[:, u], w_raw[:, u]).then_inc(hi_done, 1)
                    pool.wait_ge(hi_done, n + 1)
                    pool.tensor_tensor(w_lo[:, u], w_raw[:, u], w_hi[:, u].bitcast(F32), ALU.subtract).then_inc(lo_done, 1)

                pairs(pool, 0, HP, cut)

            @block.tensor
            def _(pe):
                def turn_keys():
                    pe.wait_ge(keys_loaded, 16)
                    for r in range(2):
                        if r:
                            pe.wait_ge(keys_cut, 2)
                        for j in range(HP // 2):
                            mm = pe.transpose(ps_k[:, j // 4, j % 4, :], keys[:, r * (HP // 2) + j, :], ident[:])
                        mm.then_inc(keys_turned, 1)
                    pe.wait_ge(keys_cut, 4)

                def query(n, u):
                    pe.wait_ge(lo_done, n + 1)
                    wait_from(pe, q_lo_done, n - 1)
                    for half in range(2):
                        j = 0
                        for k in range(KD):
                            if isinstance(n, int) and n == 0 and half == 0:
                                pe.wait_ge(h_lo, k + 1)
                            for w, h in ((w_hi, 0), (w_hi, 1), (w_lo, 0)):
                                mm = pe.matmul(ps_qs[u][:, half, :], w[:, u, k, :], h2[h][:, k, half * TH:(half + 1) * TH],
                                               start=(j == 0), stop=(j == 3 * KD - 1))
                                j += 1
                    mm.then_inc(q_mm, 1)

                def scores(n):
                    pe.wait_ge(q_lo_done, n + 1)
                    wait_from(pe, s_kept, n)
                    wait_from(pe, s_block0, n)
                    for t in range(TB):
                        for j, (q, k) in enumerate(((q_hi, key_hi), (q_hi, key_lo), (q_lo, key_hi))):
                            mm = pe.matmul(ps_s[:, t, :], q[:, t * P:(t + 1) * P],
                                           k[:, bass.ds(n, 1), :].rearrange("p o k -> p (o k)"),
                                           start=(j == 0 and t % 4 == 0), stop=(j == 2), skip_group_check=True)
                    mm.then_inc(s_mm, 1)

                def tile(n, u):
                    query(n, u)
                    if isinstance(n, int) and n == 0:
                        turn_keys()
                    else:
                        scores(n - 1)

                pairs(pe, 0, HP, tile)
                scores(HP - 1)

            @block.scalar
            def _(act):
                ahead(act, *s_stored, by=16)
                for k in range(KD):
                    act.wait_ge(h_loaded[k], 16)
                    act.copy(h2[0][:, k, :], h_raw[:, k]).then_inc(h_hi, 1)
                for r in range(2):
                    act.wait_ge(keys_turned, r + 1)
                    act.copy(key_hi[:, r * 8:r * 8 + 8, :], ps_k[:].rearrange("p a b c -> p (a b) c")).then_inc(keys_cut, 1)
                    act.wait_ge(keys_cut, 2 * r + 2)

                def keep_scores(n, u, h):
                    act.wait_ge(s_mm, n + 1)
                    act.wait_ge(s_stored[u], of_buffer(n, u) + 16)
                    act.copy(score[:, u], ps_s[:]).then_inc(s_kept, 1)
                    act.wait_ge(step, h * SEL_STEPS + SCORES_READ)
                    alone(act, keep["act_passed"])
                    act.copy(sel["scores"][:, u], ps_s[:, 0, :]).then_inc(s_block0, 1)
                    act.wait_ge(s_kept, n + 1)
                    act.dma_start(scratch["scores"].rearrange("(b h) t p k -> t b h p k", h=PH)[:, :, bass.ds(h, 1), u, :]
                                  .rearrange("t b o k -> t (b o) k"), score[:, u]).then_inc(s_stored[u], 16)

                def cut(n, u):
                    act.wait_ge(q_mm, n + 1)
                    wait_from(act, s_mm, n)
                    act.copy(q_hi[:], ps_qs[u][:].rearrange("p a b -> p (a b)")).then_inc(q_hi_done, 1)

                cut(0, 0)
                cut(1, 1)
                keep_scores(0, 0, 0)
                with act.Fori(1, PH) as h:
                    cut(h * 2, 0)
                    keep_scores(h * 2 - 1, 1, h - 1)
                    cut(h * 2 + 1, 1)
                    select_act(act, sel, step, exp_done, h - 1)
                    keep_scores(h * 2, 0, h)
                keep_scores(HP - 1, 1, PH - 1)
                select_act(act, sel, step, exp_done, PH - 1)
                for u in range(2):
                    act.wait_ge(s_stored[u], 8 * HP + 16)

            @block.vector
            def _(dve):
                ahead(dve, step, by=SEL_STEPS)
                for k in range(KD):
                    dve.wait_ge(h_hi, k + 1)
                    dve.tensor_tensor(h2[1][:, k, :], h_raw[:, k], h2[0][:, k, :].bitcast(F32), ALU.subtract
                                      ).then_inc(h_lo, 1)
                for r in range(2):
                    dve.wait_ge(keys_cut, 2 * r + 1)
                    part = slice(r * 8, r * 8 + 8)
                    dve.tensor_tensor(key_lo[:, part, :], ps_k[:].rearrange("p a b c -> p (a b) c"),
                                      key_hi[:, part, :].bitcast(F32), ALU.subtract).then_inc(keys_cut, 1)
                dve.wait_ge(iota_set, 2)

                def q_low(n, u):
                    dve.wait_ge(q_hi_done, n + 1)
                    dve.tensor_tensor(q_lo[:], ps_qs[u][:].rearrange("p a b -> p (a b)"), q_hi[:].bitcast(F32),
                                      ALU.subtract).then_inc(q_lo_done, 1)

                def choose(h):
                    dve.wait_ge(s_block0, (h + 1) * 2)
                    select_keys(dve, sel, step, keep, h)
                    select_picks(dve, sel, step, exp_done, keep, h,
                                 lambda which: keep["chosen"][:, which, bass.ds(h * TOPK, TOPK)])

                q_low(0, 0)
                q_low(1, 1)
                with dve.Fori(1, PH) as h:
                    q_low(h * 2, 0)
                    choose(h - 1)
                    q_low(h * 2 + 1, 1)
                choose(PH - 1)


QB = 4
STEP_TOKENS = 16
STEPS = P // STEP_TOKENS
WT = 64
PIECES = 8
E1 = 128


def experts_down(m, inp, keep, scratch):
    nc = m.nc
    ident, h2, chosen, iota = keep["ident"], keep["h2T"], keep["chosen"], keep["iota_row"]
    sel_done = keep["sel_done"]
    with ExitStack() as st:
        raw = m.sb(st, "down_raw", [P, 2, D])
        d_hi = m.sb(st, "downT_hi", [P, 2, KD, P], F32R)
        d_lo = m.sb(st, "downT_lo", [P, 2, KD, P], F32R)
        gu = m.sb(st, "gelu_out", [P, 2, T])
        hit1 = m.sb(st, "hit_first", [P, 2, QB, P])
        a_ = m.sb(st, "first_weighted", [P, 2, QB, 2, P], F32R)
        b_ = m.sb(st, "hit_second", [P, 2, QB, P], F32R)
        wt = [m.sb(st, "weights_out", [P, E1, WT]),
              keep["y_acc"][:].rearrange("p a (e t) -> p (a e) t", t=WT)]
        pick_g_hi = m.sb(st, "pick_weight_hi", [P, P], F32R)
        pick_g_lo = m.sb(st, "pick_weight_lo", [P, P], F32R)
        pick_1, pick_2 = m.sb(st, "pick_first", [P, P]), m.sb(st, "pick_second", [P, P])
        sel = selection(m, st, "down_sel")
        ps_d = m.ps(st, "p5_down", [P, KD, P])
        ps_u = [m.ps(st, f"p5_u{i}", [P, TH]) for i in range(2)]
        ps_w = [m.ps(st, f"p5_w{i}", [P, QB, 2, P]) for i in range(2)]

        loaded = [m.sem(f"down_loaded{i}") for i in range(2)]
        s_loaded = m.sem("scores_loaded")
        turned = [m.sem(f"down_turned{i}") for i in range(2)]
        hi_done, lo_done = m.sem("down_hi_done"), m.sem("down_lo_done")
        u_done = [m.sem(f"u_done{i}") for i in range(2)]
        gelu_done = [m.sem(f"gelu_done{i}") for i in range(2)]
        gu_stored = [m.sem(f"gelu_stored{i}") for i in range(2)]
        picks_turned, picks_ready = m.sem("picks_turned"), m.sem("picks_ready")
        hit1_ready, b_ready, a_ready = m.sem("hit_first_ready"), m.sem("hit_second_ready"), m.sem("first_ready")
        w_mm = [m.sem(f"weights_mm{i}") for i in range(2)]
        w_hi_kept, w_kept = m.sem("weights_hi_kept"), m.sem("weights_kept")
        w_stored = [m.sem(f"weights_stored{i}") for i in range(2)]
        step, exp_done = m.sem("d_sel_step"), m.sem("d_sel_exp")
        pe_passed, sp_passed = m.sem("pe_passed"), m.sem("down_sp_passed")
        down = inp["peer_down"][0].rearrange("(e p) d -> e p d", p=P)
        PE1 = E1 // PIECES

        def blocks(eng, block):
            with eng.Fori(0, TB - 1) as o:
                block(o, False)
            block(TB - 1, True)

        def steps(eng, o, last, step_of):
            half = STEPS // 2
            for hh in range(2):
                end = last and hh == 1
                with eng.Fori(0, half - end) as r:
                    step_of(hh, r, o * STEPS + hh * half + r, True)
            if last:
                step_of(1, half - 1, TB * STEPS - 1, False)

        with nc.Block() as block:
            @block.sync
            def _(sp):
                def load(s, u):
                    sp.wait_ge(turned[u], s + 1)
                    sp.dma_start(raw[:, u], down[bass.ds(s * 2 + u, 1)].rearrange("o p d -> (o p) d")
                                 ).then_inc(loaded[u], 16)

                def store_piece(tile, hh, piece, stored=None):
                    sp.dma_start(scratch["w"][bass.ds(tile, 1), :, bass.ds(piece * PE1, PE1), :].rearrange("o p e t -> (o p) e t"),
                                 wt[hh][:, bass.ds(piece * PE1, PE1), :]).then_inc(stored or w_stored[hh], 16)

                def load_scores(s):
                    sp.wait_ge(step, s * SEL_STEPS + SCORES_READ)
                    alone(sp, sp_passed)
                    sp.dma_start(sel["scores"][:], scratch["scores"][bass.ds(s + PH, 1)].rearrange("o t p k -> (o t) p k")
                                 ).then_inc(s_loaded, 16)

                def halves(o, first, last):
                    for hh in range(2):
                        with sp.Fori(0, STEPS // 2) as r:
                            s = o * STEPS + hh * (STEPS // 2) + r
                            for u in range(2):
                                load(s, u)
                            if not last:
                                load_scores(s)
                            if not (first and hh == 0):
                                sp.wait_ge(w_kept, (o * 2 + hh) * (STEPS * 2) + 4)
                                for u in range(2):
                                    store_piece(o * 2 + hh - 1, 1 - hh, r * 2 + u)

                halves(0, True, False)
                with sp.Fori(1, TB - 1) as o:
                    halves(o, False, False)
                halves(TB - 1, False, True)
                sp.wait_ge(w_kept, TB * STEPS * 4 + 4)
                for piece in range(PIECES):
                    store_piece(2 * TB - 1, 1, piece, keep["last_stored"][min(piece, 1)])
                for hh in range(2):
                    sp.wait_ge(w_stored[hh], 16 * (PIECES * (TB - hh) + 1))
                    sp.wait_ge(gu_stored[hh], 16 * (E1 // 2 + 1))

            @block.gpsimd
            def _(pool):
                ahead(pool, a_ready)

                def weighted(hh, r, s, more):
                    for b in range(4):
                        pool.wait_ge(w_mm[b % 2], s * 2 + (b // 2 + 1))
                        pool.wait_ge(hit1_ready, s * 4 + (b + 1))
                        alone(pool, keep["pool_passed"])
                        at = bass.ds(r * STEP_TOKENS + (hh * WT + b * QB), QB)
                        for part, pick in enumerate((pick_g_hi, pick_g_lo)):
                            pool.tensor_tensor(a_[:, b % 2, :, part, :], hit1[:, b % 2],
                                               pick[:, at].unsqueeze(2).to_broadcast([P, QB, P]).bitcast(F32), ALU.mult
                                               ).then_inc(a_ready, 1)

                def of_block(o, last):
                    pool.wait_ge(picks_ready, o * 4 + 4)
                    alone(pool, keep["pool_passed"])
                    steps(pool, o, last, weighted)

                blocks(pool, of_block)

            @block.tensor
            def _(pe):
                ahead(pe, *turned, *w_mm)

                def turn(s, u):
                    pe.wait_ge(loaded[u], s * 16 + 16)
                    for k in range(KD):
                        mm = pe.transpose(ps_d[:, k, :], raw[:, u, k * P:(k + 1) * P], ident[:])
                    mm.then_inc(turned[u], 1)

                def products(s, u, half):
                    if half == 0:
                        pe.wait_ge(lo_done, s * 2 + (u + 2))
                    pe.wait_ge(gelu_done[half], s * 2 + (u + 1))
                    n = 0
                    for k in range(KD):
                        for d, h in ((d_hi, 0), (d_hi, 1), (d_lo, 0)):
                            mm = pe.matmul(ps_u[half][:], d[:, u, k, :], h2[h][:, k, half * TH:(half + 1) * TH],
                                           start=(n == 0), stop=(n == 3 * KD - 1))
                            n += 1
                    mm.then_inc(u_done[half], 1)

                def weights(s, pair):
                    b1 = 2 * pair + 1
                    pe.wait_ge(b_ready, s * 4 + (b1 + 2))
                    pe.wait_ge(a_ready, s * 8 + (2 * b1 + 3))
                    pe.wait_ge(w_kept, s * 4 + (b1 + 3))
                    for b in (b1 - 1, b1):
                        for t in range(QB):
                            mm = pe.matmul(ps_w[b % 2][:, t].rearrange("p a e -> p (a e)"), b_[:, b % 2, t, :],
                                           a_[:, b % 2, t].rearrange("p a e -> p (a e)"),
                                           start=(t % 2 == 0), stop=(t % 2 == 1), skip_group_check=True)
                        mm.then_inc(w_mm[b % 2], 1)

                def of_step(hh, r, s, more):
                    products(s, 0, 0)
                    turn(s, 1)
                    products(s, 0, 1)
                    weights(s, 0)
                    products(s, 1, 0)
                    if more:
                        turn(s + 1, 0)
                    products(s, 1, 1)
                    weights(s, 1)

                def of_block(o, last):
                    pe.wait_ge(sel_done, o * PH + PH)
                    pe.wait_ge(w_kept, o * (STEPS * 4) + 4)
                    for j in range(3):
                        mm = pe.transpose(ps_w[0][:, j, 0, :], chosen[:, j, :], ident[:])
                    mm.then_inc(picks_turned, 1)
                    pe.wait_ge(picks_ready, o * 4 + 4)
                    alone(pe, pe_passed)
                    steps(pe, o, last, of_step)

                turn(0, 0)
                blocks(pe, of_block)

            @block.scalar
            def _(act):
                ahead(act, *gelu_done)
                ahead(act, *gu_stored, *w_stored, by=16)

                def cut(s, u):
                    act.wait_ge(turned[u], s + 2)
                    act.copy(d_hi[:, u], ps_d[:]).then_inc(hi_done, 1)

                def gelu(s, u, half):
                    act.wait_ge(u_done[half], s * 2 + (u + 1))
                    act.wait_ge(gu_stored[u], s * 16 + 16)
                    act.activation(gu[:, u, half * TH:(half + 1) * TH], ps_u[half][:], ACT.Gelu).then_inc(gelu_done[half], 1)

                def store(s, u):
                    for half in range(2):
                        act.wait_ge(gelu_done[half], s * 2 + (u + 2))
                    act.dma_start(scratch["gu"][bass.ds(s * 2 + u, 1)].rearrange("o p t -> (o p) t"), gu[:, u]
                                  ).then_inc(gu_stored[u], 16)

                def keep_high(hh, r, s, b):
                    act.wait_ge(w_mm[b % 2], s * 2 + (b // 2 + 2))
                    alone(act, keep["act_passed"])
                    act.copy(wt[hh][:, :, bass.ds(r * STEP_TOKENS + b * QB, QB)],
                             ps_w[b % 2][:, :, 0, :].rearrange("p t e -> p e t")).then_inc(w_hi_kept, 1)

                def of_block(o, last):
                    def of_step(hh, r, s, more):
                        gelu(s, 0, 0)
                        cut(s, 1)
                        gelu(s, 0, 1)
                        act.wait_ge(w_stored[hh], o * (16 * PIECES) + 16)
                        keep_high(hh, r, s, 0)
                        keep_high(hh, r, s, 1)
                        store(s, 0)
                        if not last:
                            select_act(act, sel, step, exp_done, s)
                        gelu(s, 1, 0)
                        if more:
                            cut(s + 1, 0)
                        gelu(s, 1, 1)
                        keep_high(hh, r, s, 2)
                        keep_high(hh, r, s, 3)
                        store(s, 1)

                    steps(act, o, last, of_step)

                cut(0, 0)
                blocks(act, of_block)

            @block.vector
            def _(dve):
                ahead(dve, lo_done, b_ready)
                ahead(dve, w_kept, by=4)
                ahead(dve, step, by=SEL_STEPS)

                def low(s, u):
                    dve.wait_ge(hi_done, s * 2 + (u + 1))
                    dve.tensor_tensor(d_lo[:, u], ps_d[:], d_hi[:, u].bitcast(F32), ALU.subtract).then_inc(lo_done, 1)

                def first(hh, r, s, b):
                    at = bass.ds(r * STEP_TOKENS + (hh * WT + b * QB), QB)
                    wide = lambda ap: ap[:, at].unsqueeze(2).to_broadcast([P, QB, P])
                    keys = iota[:].unsqueeze(1).to_broadcast([P, QB, P])
                    dve.wait_ge(w_mm[b % 2], s * 2 + (b // 2 + 1))
                    dve.tensor_tensor(hit1[:, b % 2], wide(pick_1), keys, ALU.is_equal).then_inc(hit1_ready, 1)
                    dve.tensor_tensor(b_[:, b % 2], wide(pick_2), keys, ALU.is_equal).then_inc(b_ready, 1)

                def keep_weights(hh, r, s, b):
                    at = wt[hh][:, :, bass.ds(r * STEP_TOKENS + b * QB, QB)]
                    dve.wait_ge(w_hi_kept, s * 4 + (b + 1))
                    dve.tensor_tensor(at, ps_w[b % 2][:, :, 1, :].rearrange("p t e -> p e t"), at, ALU.add
                                      ).then_inc(w_kept, 1)

                def of_block(o, last):
                    dve.wait_ge(picks_turned, o + 1)
                    dve.wait_ge(a_ready, o * (8 * STEPS) + 1)
                    dve.wait_ge(b_ready, o * (4 * STEPS) + 1)
                    dve.tensor_copy(pick_g_hi[:], ps_w[0][:, 0, 0, :]).then_inc(picks_ready, 1)
                    dve.tensor_copy(pick_1[:], ps_w[0][:, 1, 0, :]).then_inc(picks_ready, 1)
                    dve.tensor_copy(pick_2[:], ps_w[0][:, 2, 0, :]).then_inc(picks_ready, 1)
                    dve.wait_ge(picks_ready, o * 4 + 3)
                    dve.tensor_tensor(pick_g_lo[:], ps_w[0][:, 0, 0, :], pick_g_hi[:].bitcast(F32), ALU.subtract
                                      ).then_inc(picks_ready, 1)
                    dve.wait_ge(picks_ready, o * 4 + 4)
                    alone(dve, keep["dve_passed"])

                    def of_step(hh, r, s, more):
                        first(hh, r, s, 0)
                        first(hh, r, s, 1)
                        low(s, 1)
                        h = r + hh * (STEPS // 2)
                        if not last:
                            dve.wait_ge(s_loaded, s * 16 + 16)
                            select_keys(dve, sel, step, keep, s)
                        keep_weights(hh, r, s, 0)
                        keep_weights(hh, r, s, 1)
                        first(hh, r, s, 2)
                        first(hh, r, s, 3)
                        if not last:
                            select_picks(dve, sel, step, exp_done, keep, s,
                                         lambda which: chosen[:, which, bass.ds(h * TOPK, TOPK)])
                        if more:
                            low(s + 1, 0)
                        keep_weights(hh, r, s, 2)
                        keep_weights(hh, r, s, 3)

                    steps(dve, o, last, of_step)

                low(0, 0)
                blocks(dve, of_block)


GT = 4


def experts_up(m, inp, keep, scratch, out):
    nc = m.nc
    gate_rows, last_stored = keep["gate_rows"], keep["last_stored"]
    GROUPS = E1 // GT
    SLOTS = 2 * TB
    with ExitStack() as st:
        up_raw = m.sb(st, "up_raw", [P, 2, D])
        gu = m.sb(st, "gelu_in", [P, 2, T])
        w = m.sb(st, "weights_in", [P, 2, T])
        g_hi = m.sb(st, "coef_hi", [P, 2, GT, T], F32R)
        g_lo = m.sb(st, "coef_lo", [P, 2, GT, T], F32R)
        up_hi = m.sb(st, "up_hi", [P, 2, GT, D], F32R)
        up_lo = m.sb(st, "up_lo", [P, 2, GT, D], F32R)
        acc = keep["y_acc"]
        x1 = m.sb(st, "x1_in", [P, 2, D])
        stat = m.sb(st, "y_stat", [P, TB, 3])
        eps = m.sb(st, "eps6", [P, 1])
        ps_y = [m.ps(st, f"p6_y{i}", [P, TH]) for i in range(8)]

        gu_loaded = [m.sem(f"gelu_loaded{i}") for i in range(2)]
        w_loaded = [m.sem(f"weights_loaded{i}") for i in range(2)]
        up_loaded = [m.sem(f"up_loaded{i}") for i in range(2)]
        coef_ready, g_hi_done, g_lo_done = m.sem("coef_ready"), m.sem("coef_hi_done"), m.sem("coef_lo_done")
        up_hi_done, up_lo_done = m.sem("up_hi_done"), m.sem("up_lo_done")
        eps_set, y_mm, added = m.sem("eps6_set"), m.sem("y_mm"), m.sem("y_added")
        x1_loaded = [m.sem(f"x1_in_loaded{i}") for i in range(2)]
        ssq, std, rstd, scaled, summed = (m.sem(f"y_{n}") for n in ("ssq", "std", "rstd", "scaled", "summed"))
        out_stored = m.sem("out_stored")
        up = inp["peer_up"][0].rearrange("(e p) d -> e p d", p=P)

        with nc.Block() as block:
            @block.sync
            def _(sp):
                def load(g, v):
                    for j in range(GT):
                        n, u = g * GT + j, j % 2
                        wait_from(sp, up_lo_done, n - 1)
                        sp.dma_start(up_raw[:, u], up[bass.ds(n, 1)].rearrange("o p d -> (o p) d")
                                     ).then_inc(up_loaded[u], 16)
                        wait_from(sp, g_lo_done, n - 1)
                        sp.dma_start(gu[:, u], scratch["gu"][bass.ds(n, 1)].rearrange("o p t -> (o p) t")
                                     ).then_inc(gu_loaded[u], 16)
                        if isinstance(g, int) and g == 0 and j == 0:
                            sp.wait_ge(last_stored[0], 16)
                        sp.dma_start(w[:, u].rearrange("p (h t) -> p h t", t=WT),
                                     scratch["w"][:, :, bass.ds(n, 1), :].rearrange("h p o t -> p (h o) t")
                                     ).then_inc(w_loaded[u], 16)

                load(0, 0)
                load(1, 1)
                sp.wait_ge(last_stored[1], 16 * (PIECES - 1))
                pairs(sp, 2, GROUPS, load)
                for t in range(TB):
                    if t >= 2:
                        sp.wait_ge(summed, t - 1)
                    sp.dma_start(x1[:, t % 2], scratch["x1"][t * P:(t + 1) * P, :]).then_inc(x1_loaded[t % 2], 16)
                    if t >= 1:
                        sp.wait_ge(summed, t)
                        sp.dma_start(out[0, (t - 1) * P:t * P, :], acc[:, t - 1, :]).then_inc(out_stored, 16)
                sp.wait_ge(summed, TB)
                sp.dma_start(out[0, (TB - 1) * P:TB * P, :], acc[:, TB - 1, :]).then_inc(out_stored, 16)
                sp.wait_ge(out_stored, 16 * TB)

            @block.gpsimd
            def _(pool):
                pool.memset(eps[:], EPS).then_inc(eps_set, 1)

                def cut(g, v):
                    for j in range(GT):
                        n, u = g * GT + j, j % 2
                        pool.wait_ge(up_hi_done, n + 1)
                        pool.tensor_tensor(up_lo[:, v, j, :], up_raw[:, u], up_hi[:, v, j, :].bitcast(F32),
                                           ALU.subtract).then_inc(up_lo_done, 1)

                pairs(pool, 0, GROUPS, cut)

            @block.scalar
            def _(act):
                def cut(g, v):
                    wait_from(act, y_mm, (g - 1) * SLOTS)
                    for j in range(GT):
                        n, u = g * GT + j, j % 2
                        loads = g * (8 * GT) + 16 * (j // 2 + 1)
                        act.wait_ge(up_loaded[u], loads)
                        act.copy(up_hi[:, v, j, :], up_raw[:, u]).then_inc(up_hi_done, 1)
                        act.wait_ge(coef_ready, n + 1)
                        act.copy(g_hi[:, v, j, :], gu[:, u]).then_inc(g_hi_done, 1)

                pairs(act, 0, GROUPS, cut)
                act.wait_ge(eps_set, 1)
                for t in range(TB):
                    act.wait_ge(added, SLOTS * (GROUPS - 1) + 2 * t + 2)
                    if t >= 1:
                        act.wait_ge(ssq, t)
                    act.activation(gu[:, 0], acc[:, t, :], ACT.Square, accum_out=stat[:, t, 0:1]).then_inc(ssq, 1)
                    act.wait_ge(ssq, t + 1)
                    act.activation(stat[:, t, 1:2], stat[:, t, 0:1], ACT.Sqrt, bias=eps[:], scale=1.0 / D).then_inc(std, 1)

            @block.vector
            def _(dve):
                def coef(g, v, j):
                    n, u = g * GT + j, j % 2
                    loads = g * (8 * GT) + 16 * (j // 2 + 1)
                    dve.wait_ge(gu_loaded[u], loads)
                    dve.wait_ge(w_loaded[u], loads)
                    dve.tensor_tensor(gu[:, u], gu[:, u], w[:, u], ALU.mult).then_inc(coef_ready, 1)
                    dve.wait_ge(g_hi_done, n + 1)
                    dve.tensor_tensor(g_lo[:, v, j, :], gu[:, u], g_hi[:, v, j, :].bitcast(F32), ALU.subtract
                                      ).then_inc(g_lo_done, 1)

                def add(g, s):
                    dve.wait_ge(y_mm, g * SLOTS + (s + 1))
                    wait_from(dve, added, g * SLOTS + (s + 1 - SLOTS))
                    part = acc[:, s // 2, (s % 2) * TH:(s % 2 + 1) * TH]
                    if isinstance(g, int) and g == 0:
                        if s == 0:
                            dve.wait_ge(last_stored[0], 16)
                            dve.wait_ge(last_stored[1], 16 * (PIECES - 1))
                        dve.tensor_copy(part, ps_y[s % 8][:]).then_inc(added, 1)
                    else:
                        dve.tensor_tensor(part, ps_y[s % 8][:], part, ALU.add).then_inc(added, 1)

                def group(g, v):
                    for j in range(GT):
                        coef(g, v, j)
                        if not isinstance(g, int) or g > 0:
                            for s in range(4 * j, 4 * j + 4):
                                add(g - 1, s)

                pairs(dve, 0, GROUPS, group)

                def finish(t):
                    dve.wait_ge(std, t + 1)
                    dve.reciprocal(stat[:, t, 2:3], stat[:, t, 1:2]).then_inc(rstd, 1)
                    dve.wait_ge(rstd, t + 1)
                    dve.scalar_tensor_tensor(acc[:, t, :], acc[:, t, :], stat[:, t, 2:3], gate_rows[:, 1, :],
                                             ALU.mult, ALU.mult).then_inc(scaled, 1)
                    dve.wait_ge(scaled, t + 1)
                    dve.wait_ge(x1_loaded[t % 2], 16 * (t // 2 + 1))
                    dve.tensor_tensor(acc[:, t, :], acc[:, t, :], x1[:, t % 2], ALU.add).then_inc(summed, 1)

                for s in range(SLOTS):
                    add(GROUPS - 1, s)
                    if s % 2 and s > 1:
                        finish(s // 2 - 1)
                finish(TB - 1)

            @block.tensor
            def _(pe):
                def first_group():
                    for base in (0, 8):
                        for j in range(GT):
                            if base == 0:
                                pe.wait_ge(g_lo_done, j + 1)
                                pe.wait_ge(up_lo_done, j + 1)
                            for s in range(base, base + 8):
                                t, half = divmod(s, 2)
                                if base and j == 0:
                                    pe.wait_ge(added, s - 7)
                                for n, (a, b) in enumerate(((g_hi, up_hi), (g_hi, up_lo), (g_lo, up_hi))):
                                    mm = pe.matmul(ps_y[s % 8][:], a[:, 0, j, t * P:(t + 1) * P],
                                                   b[:, 0, j, half * TH:(half + 1) * TH],
                                                   start=(j == 0 and n == 0), stop=(j == GT - 1 and n == 2))
                                if j == GT - 1:
                                    mm.then_inc(y_mm, 1)

                def group(g, v):
                    if isinstance(g, int) and g == 0:
                        first_group()
                        return
                    pe.wait_ge(g_lo_done, g * GT + GT)
                    pe.wait_ge(up_lo_done, g * GT + GT)
                    for s in range(SLOTS):
                        t, half = divmod(s, 2)
                        wait_from(pe, added, g * SLOTS + (s - 7))
                        n = 0
                        for j in range(GT):
                            for a, b in ((g_hi, up_hi), (g_hi, up_lo), (g_lo, up_hi)):
                                mm = pe.matmul(ps_y[s % 8][:], a[:, v, j, t * P:(t + 1) * P],
                                               b[:, v, j, half * TH:(half + 1) * TH],
                                               start=(n == 0), stop=(n == 3 * GT - 1))
                                n += 1
                        mm.then_inc(y_mm, 1)

                pairs(pe, 0, GROUPS, group)


def build(nc, inp, out):
    scratch = {}
    for name, shape in (("xbc", [XBC, T]), ("z", [SI, T]), ("gates", [2 * D, T]), ("y_lru", [D, T]), ("y_ssd", [SI, T]),
                        ("x1", [T, D]), ("h2", [D, T]), ("scores", [TB * PH, P, 2, PK]), ("gu", [E1, P, T]),
                        ("w", [T // WT, P, E1, WT])):
        scratch[name] = nc.dram_tensor(f"scratch_{name}", shape, F32, kind="Internal").ap()
    with ExitStack() as stack:
        m = Machine(nc, stack)
        keep = {
            "ident": m.sb(stack, "ident", [P, P]),
            "mod": m.sb(stack, "mod", [P, 4, KD]),
            "gate_rows": m.sb(stack, "gate_rows", [P, 2, D]),
            "pool_passed": m.kept_sem("pool_passed"),
            "act_passed": m.kept_sem("act_passed"),
            "dve_passed": m.kept_sem("dve_passed"),
            "consts_ready": m.kept_sem("consts_ready"),
        }
        with ExitStack() as mix:
            keep["cols"] = m.sb(mix, "cols", [P, 272])
            keep["tri"] = m.sb(mix, "tri", [P, P])
            keep["mask"] = m.sb(mix, "mask", [P, 4, P], BF16)
            keep["ones"] = m.sb(mix, "ones", [P, P])
            keep["sp_in"] = m.sb(mix, "softplus_in", [P, KD + TB * SH])
            keep["sp_out"] = m.sb(mix, "softplus_out", [P, KD + TB * SH])
            with ExitStack() as project:
                keep["hT"] = [m.sb(project, "hT_hi", [P, KD, T], F32R), m.sb(project, "hT_lo", [P, KD, T], F32R)]
                vectors_and_norm(m, inp, keep)
                m.end_phase()
                project_in(m, inp, keep, scratch)
                m.end_phase()
            keep["y_squares"] = m.sb(mix, "y_squares", [P, SG, T])
            ssd(m, inp, keep, scratch)
            m.end_phase()
            with ExitStack() as merged:
                keep["merged_lo"] = m.sb(merged, "merged_lo", [P, KD, T], F32R)
                keep["merged"] = keep["merged_lo"][:].bitcast(F32)
                keep["w_o"] = m.sb(merged, "w_o_lo", [P, KD, D], F32R)
                merge(m, inp, keep, scratch)
                m.end_phase()
                post_mix(m, inp, keep, scratch)
                m.end_phase()
        keep["y_acc"] = m.sb(stack, "y_acc", [P, TB, D])
        keep["last_stored"] = [m.kept_sem("last_weights_first_piece"), m.kept_sem("last_weights_other_pieces")]
        with ExitStack() as picks:
            expert_keep(m, picks, keep)
            queries(m, inp, keep, scratch)
            m.end_phase()
            experts_down(m, inp, keep, scratch)
            m.end_phase()
        experts_up(m, inp, keep, scratch, out)


_INS = ["x", "c", "w_ada", "b_ada", "norm_pre_mix", "norm_post_mix", "norm_pre_ffn", "norm_post_ffn", "w_in",
        "lru_conv_w", "lru_conv_b", "lru_wa", "lru_ba", "lru_wx", "lru_bx", "lru_lambda", "ssd_conv_w", "ssd_conv_b",
        "ssd_dt_bias", "ssd_a_log", "ssd_d", "ssd_norm_w", "w_lru_out", "w_ssd_out", "w_o", "peer_wq",
        "peer_sub_keys", "peer_down", "peer_up"]
_OUTS = [((1, T, D), "float32")]


def kernel(**inputs):
    import numpy as _np
    import concourse.bacc as _bacc
    from concourse import mybir as _mybir
    from concourse.bass_utils import run_bass_kernel_spmd as _run

    nc = _bacc.Bacc("TRN2", target_bir_lowering=False, num_devices=1)
    arrays, inp = {}, {}
    for name in _INS:
        a = _np.ascontiguousarray(inputs[name])
        arrays[f"in_{name}_dram"] = a
        inp[name] = nc.dram_tensor(f"in_{name}_dram", a.shape, _mybir.dt.from_np(a.dtype), kind="ExternalInput").ap()
    shape, dtype = _OUTS[0]
    out = nc.dram_tensor("out_0_dram", shape, _mybir.dt.from_np(_np.dtype(dtype)), kind="ExternalOutput").ap()
    build(nc, inp, out)
    r = _run(nc, [arrays], core_ids=[0])
    return r.results[0]["out_0_dram"]
```
